# Optimizing a Trainium2 kernel written in Bass

```python
import math
import jax, jax.numpy as jnp
from jax import lax
import numpy as np

D_MODEL = 1024
BATCH = 1
SEQ = 256
DEPTH = 1
DEC_BATCH = 8
DEC_SEQ = 4
PAST_LEN = 2048
PAGE_SIZE = 128

D_PLE = 256
EPS = 1e-6
CONV_W = 4
W_LRU = D_MODEL
LRU_BLOCKS = 8
LRU_BW = W_LRU // LRU_BLOCKS
LRU_C = 8.0
D_INNER = 2 * D_MODEL
SSD_HEADDIM = 64
SSD_HEADS = D_INNER // SSD_HEADDIM
SSD_GROUPS = 8
SSD_HPG = SSD_HEADS // SSD_GROUPS
SSD_STATE = 128
SSD_GN = SSD_GROUPS * SSD_STATE
SSD_CONV_DIM = D_INNER + 2 * SSD_GN
SSD_CHUNK = 128
IN_COLS = 2 * W_LRU + D_INNER + SSD_CONV_DIM + SSD_HEADS + 2 * D_MODEL
N_EGROUPS = 4
EXP_PER_GROUP = 4
N_EXPERTS = N_EGROUPS * EXP_PER_GROUP
TOP_K = 2
D_FF_E = 512

kernel_name = 'hybrid_rglru_ssd_hmoe_step'

def grouped_rmsnorm(y, g, groups):
    sh = y.shape
    yf = y.astype(jnp.float32).reshape(sh[:-1] + (groups, sh[-1] // groups))
    yf = yf * lax.rsqrt(jnp.mean(yf * yf, axis=-1, keepdims=True) + EPS)
    return (yf.reshape(sh) * g.astype(jnp.float32)).astype(y.dtype)

def rmsnorm(y, g):
    return grouped_rmsnorm(y, g, 1)

def causal_dwconv(x, buf, w, b):
    L = x.shape[1]
    xx = jnp.concatenate([buf.astype(x.dtype), x], axis=1)
    y = b + sum(xx[:, k:k + L] * w[k] for k in range(CONV_W))
    return y, xx[:, -(CONV_W - 1):]

def rg_lru(x, h0, w_a, b_a, w_x, b_x, lam, reset_first):
    bsz, L, W = x.shape
    xf = x.astype(jnp.float32)
    xb = xf.reshape(bsz, L, LRU_BLOCKS, LRU_BW)
    r = jax.nn.sigmoid(jnp.einsum('blnc,ncd->blnd', xb, w_a.astype(jnp.float32)).reshape(bsz, L, W) + b_a)
    i = jax.nn.sigmoid(jnp.einsum('blnc,ncd->blnd', xb, w_x.astype(jnp.float32)).reshape(bsz, L, W) + b_x)
    log_a = LRU_C * r * jax.nn.log_sigmoid(lam.astype(jnp.float32))
    a = jnp.exp(log_a)
    mult = jnp.sqrt(-jnp.expm1(2.0 * log_a))
    if reset_first:
        reset = (jnp.arange(L) == 0)[None, :, None]
        mult = jnp.where(reset, 1.0, mult)
        a = jnp.where(reset, 0.0, a)
    u = xf * i * mult

    def comb(e1, e2):
        return (e1[0] * e2[0], e2[0] * e1[1] + e2[1])

    a_cum, h_part = lax.associative_scan(comb, (a, u), axis=1)
    h = a_cum * h0.astype(jnp.float32)[:, None, :] + h_part
    return h, h[:, -1]

def ssd_chunked(xs, dt, A, Bm, Cm, s0):
    bsz, L = xs.shape[:2]
    Q = SSD_CHUNK if L % SSD_CHUNK == 0 else L
    nc = L // Q
    x = (xs * dt[..., None]).reshape(bsz, nc, Q, SSD_GROUPS, SSD_HPG, SSD_HEADDIM)
    a = (dt * A).reshape(bsz, nc, Q, SSD_GROUPS, SSD_HPG)
    Bc = Bm.reshape(bsz, nc, Q, SSD_GROUPS, SSD_STATE)
    Cc = Cm.reshape(bsz, nc, Q, SSD_GROUPS, SSD_STATE)
    cum = jnp.cumsum(a, axis=2)
    cum_t = jnp.moveaxis(cum, 2, -1)
    diff = cum_t[..., :, None] - cum_t[..., None, :]
    causal = jnp.tril(jnp.ones((Q, Q), dtype=bool))
    decay = jnp.exp(jnp.where(causal, diff, -jnp.inf))
    cb = jnp.einsum('bcqgn,bcsgn->bcgqs', Cc, Bc)
    y_diag = jnp.einsum('bcgqs,bcghqs,bcsghp->bcqghp', cb, decay, x)
    decay_to_end = jnp.exp(cum[:, :, -1:] - cum)
    chunk_states = jnp.einsum('bcsgn,bcsgh,bcsghp->bcghpn', Bc, decay_to_end, x)
    chunk_decay = jnp.exp(cum[:, :, -1])
    s0g = s0.reshape(bsz, SSD_GROUPS, SSD_HPG, SSD_HEADDIM, SSD_STATE)

    def step(s, inp):
        dec, st = inp
        return dec[..., None, None] * s + st, s

    s_final, s_prev = lax.scan(step, s0g, (jnp.moveaxis(chunk_decay, 1, 0), jnp.moveaxis(chunk_states, 1, 0)))
    s_prev = jnp.moveaxis(s_prev, 0, 1)
    y_off = jnp.einsum('bcqgn,bcghpn,bcqgh->bcqghp', Cc, s_prev, jnp.exp(cum))
    y = (y_diag + y_off).reshape(bsz, L, SSD_HEADS, SSD_HEADDIM)
    return y, s_final.reshape(bsz, SSD_HEADS, SSD_HEADDIM, SSD_STATE)

def hier_moe(h, w_rg, b_rg, w_re, b_re, w1, w3, w2):
    bsz, L, D = h.shape
    t = h.reshape(bsz * L, D)
    g_logits = (t @ w_rg).astype(jnp.float32) + b_rg
    g_idx = jnp.argmax(g_logits, axis=-1)
    g_w = jnp.take_along_axis(jax.nn.softmax(g_logits, axis=-1), g_idx[:, None], axis=-1)[:, 0]
    e_logits = ((t @ w_re).astype(jnp.float32) + b_re).reshape(-1, N_EGROUPS, EXP_PER_GROUP)
    e_sel = jnp.take_along_axis(e_logits, g_idx[:, None, None], axis=1)[:, 0]
    top_v, top_i = lax.top_k(jax.nn.softmax(e_sel, axis=-1), TOP_K)
    w = g_w[:, None] * top_v / jnp.sum(top_v, axis=-1, keepdims=True)
    e_id = g_idx[:, None] * EXP_PER_GROUP + top_i
    combine = jnp.sum(jax.nn.one_hot(e_id, N_EXPERTS, dtype=jnp.float32) * w[..., None], axis=1).astype(h.dtype)
    out = jnp.zeros_like(t)
    for e in range(N_EXPERTS):
        act = jax.nn.silu(t @ w1[e]) * (t @ w3[e])
        out = out + (combine[:, e:e + 1] * act) @ w2[e]
    return out.reshape(bsz, L, D)

def decoder_layer(x, p, lru_h0, lru_buf0, ssd_s0, ssd_buf0, reset_first, lw):
    bsz, L, _ = x.shape
    h = rmsnorm(x, lw['g_mix'])
    proj = h @ lw['w_in']
    o1 = W_LRU
    o2 = o1 + W_LRU
    o3 = o2 + D_INNER
    o4 = o3 + SSD_CONV_DIM
    o5 = o4 + SSD_HEADS
    o6 = o5 + D_MODEL
    lru_in, lru_gate, z = proj[..., :o1], proj[..., o1:o2], proj[..., o2:o3]
    xbc, dt_raw = proj[..., o3:o4], proj[..., o4:o5]
    gate_a, gate_b = proj[..., o5:o6], proj[..., o6:]
    u, lru_buf = causal_dwconv(lru_in, lru_buf0, lw['lru_conv_w'], lw['lru_conv_b'])
    hs, lru_h = rg_lru(u, lru_h0, lw['lru_wa'], lw['lru_ba'], lw['lru_wx'], lw['lru_bx'], lw['lru_lambda'], reset_first)
    y_a = hs.astype(x.dtype) * jax.nn.gelu(lru_gate)
    xbc_c, ssd_buf = causal_dwconv(xbc, ssd_buf0, lw['ssd_conv_w'], lw['ssd_conv_b'])
    xbc_c = jax.nn.silu(xbc_c).astype(jnp.float32)
    xs = xbc_c[..., :D_INNER].reshape(bsz, L, SSD_HEADS, SSD_HEADDIM)
    Bm = xbc_c[..., D_INNER:D_INNER + SSD_GN].reshape(bsz, L, SSD_GROUPS, SSD_STATE)
    Cm = xbc_c[..., D_INNER + SSD_GN:].reshape(bsz, L, SSD_GROUPS, SSD_STATE)
    dt = jax.nn.softplus(dt_raw.astype(jnp.float32) + lw['ssd_dt_bias'])
    A = -jnp.exp(lw['ssd_A_log'].astype(jnp.float32))
    y_ssd, ssd_s = ssd_chunked(xs, dt, A, Bm, Cm, ssd_s0.astype(jnp.float32))
    y_ssd = y_ssd + lw['ssd_D'].astype(jnp.float32)[:, None] * xs
    y_b = y_ssd.reshape(bsz, L, D_INNER) * jax.nn.silu(z.astype(jnp.float32))
    y_b = grouped_rmsnorm(y_b, lw['ssd_norm_g'], SSD_GROUPS).astype(x.dtype)
    merged = jax.nn.sigmoid(gate_a) * (y_a @ lw['w_br_lru']) + jax.nn.sigmoid(gate_b) * (y_b @ lw['w_br_ssd'])
    x = x + merged @ lw['w_out']
    x = x + hier_moe(rmsnorm(x, lw['g_ffn']), lw['w_router_g'], lw['b_router_g'], lw['w_router_e'], lw['b_router_e'], lw['w1'], lw['w3'], lw['w2'])
    e = rmsnorm(p.astype(x.dtype) @ lw['w_ple_proj'], lw['g_ple'])
    x = x + jax.nn.sigmoid(rmsnorm(x, lw['g_ple_gate']) @ lw['w_ple_gate']) * e
    return x, (lru_h, lru_buf, ssd_s, ssd_buf)

def setup_inputs(seed: int = 0) -> dict:
    key = jax.random.key(seed)
    ks = iter(jax.random.split(key, 64))
    f32 = jnp.float32

    def nrm(shape, scale):
        return jax.random.normal(next(ks), shape, f32) * scale

    def gain(shape):
        return 1.0 + 0.02 * jax.random.normal(next(ks), shape, f32)

    def unif(shape, lo, hi):
        return jax.random.uniform(next(ks), shape, f32, lo, hi)

    a0 = unif((DEPTH, W_LRU), 0.9, 0.999)
    s = a0 ** (1.0 / LRU_C)
    lam = jnp.log(s) - jnp.log1p(-s)
    dt0 = jnp.exp(unif((DEPTH, SSD_HEADS), math.log(1e-3), math.log(1e-1)))
    dt_bias = dt0 + jnp.log(-jnp.expm1(-dt0))
    return {
        'x_prompt': nrm((BATCH, SEQ, D_MODEL), 1.0),
        'x_sample': nrm((DEC_BATCH, DEC_SEQ, D_MODEL), 1.0),
        'state_lru_h': nrm((DEPTH, DEC_BATCH, W_LRU), 0.5),
        'state_lru_conv': nrm((DEPTH, DEC_BATCH, CONV_W - 1, W_LRU), 1.0),
        'state_ssd': nrm((DEPTH, DEC_BATCH, SSD_HEADS, SSD_HEADDIM, SSD_STATE), 0.1),
        'state_ssd_conv': nrm((DEPTH, DEC_BATCH, CONV_W - 1, SSD_CONV_DIM), 1.0),
        'p_prompt': nrm((DEPTH, BATCH, SEQ, D_PLE), 1.0),
        'p_sample': nrm((DEPTH, DEC_BATCH, DEC_SEQ, D_PLE), 1.0),
        'g_mix': gain((DEPTH, D_MODEL)),
        'w_in': nrm((DEPTH, D_MODEL, IN_COLS), D_MODEL ** -0.5),
        'lru_conv_w': nrm((DEPTH, CONV_W, W_LRU), 0.5),
        'lru_conv_b': nrm((DEPTH, W_LRU), 0.02),
        'lru_wa': nrm((DEPTH, LRU_BLOCKS, LRU_BW, LRU_BW), LRU_BW ** -0.5),
        'lru_ba': nrm((DEPTH, W_LRU), 0.02),
        'lru_wx': nrm((DEPTH, LRU_BLOCKS, LRU_BW, LRU_BW), LRU_BW ** -0.5),
        'lru_bx': nrm((DEPTH, W_LRU), 0.02),
        'lru_lambda': lam,
        'ssd_conv_w': nrm((DEPTH, CONV_W, SSD_CONV_DIM), 0.5),
        'ssd_conv_b': nrm((DEPTH, SSD_CONV_DIM), 0.02),
        'ssd_dt_bias': dt_bias,
        'ssd_A_log': jnp.log(unif((DEPTH, SSD_HEADS), 1.0, 16.0)),
        'ssd_D': gain((DEPTH, SSD_HEADS)),
        'ssd_norm_g': gain((DEPTH, D_INNER)),
        'w_br_lru': nrm((DEPTH, W_LRU, D_MODEL), W_LRU ** -0.5),
        'w_br_ssd': nrm((DEPTH, D_INNER, D_MODEL), D_INNER ** -0.5),
        'w_out': nrm((DEPTH, D_MODEL, D_MODEL), D_MODEL ** -0.5),
        'g_ffn': gain((DEPTH, D_MODEL)),
        'w_router_g': nrm((DEPTH, D_MODEL, N_EGROUPS), D_MODEL ** -0.5),
        'b_router_g': nrm((DEPTH, N_EGROUPS), 0.01),
        'w_router_e': nrm((DEPTH, D_MODEL, N_EXPERTS), D_MODEL ** -0.5),
        'b_router_e': nrm((DEPTH, N_EXPERTS), 0.01),
        'w1': nrm((DEPTH, N_EXPERTS, D_MODEL, D_FF_E), D_MODEL ** -0.5),
        'w3': nrm((DEPTH, N_EXPERTS, D_MODEL, D_FF_E), D_MODEL ** -0.5),
        'w2': nrm((DEPTH, N_EXPERTS, D_FF_E, D_MODEL), D_FF_E ** -0.5),
        'w_ple_proj': nrm((DEPTH, D_PLE, D_MODEL), D_PLE ** -0.5),
        'g_ple': gain((DEPTH, D_MODEL)),
        'g_ple_gate': gain((DEPTH, D_MODEL)),
        'w_ple_gate': nrm((DEPTH, D_MODEL, D_MODEL), D_MODEL ** -0.5),
        'g_final': gain((D_MODEL,)),
    }

def reference(x_prompt, x_sample, state_lru_h, state_lru_conv, state_ssd, state_ssd_conv, p_prompt, p_sample,
              g_mix, w_in, lru_conv_w, lru_conv_b, lru_wa, lru_ba, lru_wx, lru_bx, lru_lambda,
              ssd_conv_w, ssd_conv_b, ssd_dt_bias, ssd_A_log, ssd_D, ssd_norm_g,
              w_br_lru, w_br_ssd, w_out, g_ffn, w_router_g, b_router_g, w_router_e, b_router_e,
              w1, w3, w2, w_ple_proj, g_ple, g_ple_gate, w_ple_gate, g_final):
    xp, xs = x_prompt, x_sample
    bp = x_prompt.shape[0]
    st_p = ([], [], [], [])
    st_s = ([], [], [], [])
    for i in range(DEPTH):
        lw = {
            'g_mix': g_mix[i], 'w_in': w_in[i], 'lru_conv_w': lru_conv_w[i], 'lru_conv_b': lru_conv_b[i],
            'lru_wa': lru_wa[i], 'lru_ba': lru_ba[i], 'lru_wx': lru_wx[i], 'lru_bx': lru_bx[i],
            'lru_lambda': lru_lambda[i], 'ssd_conv_w': ssd_conv_w[i], 'ssd_conv_b': ssd_conv_b[i],
            'ssd_dt_bias': ssd_dt_bias[i], 'ssd_A_log': ssd_A_log[i], 'ssd_D': ssd_D[i],
            'ssd_norm_g': ssd_norm_g[i], 'w_br_lru': w_br_lru[i], 'w_br_ssd': w_br_ssd[i], 'w_out': w_out[i],
            'g_ffn': g_ffn[i], 'w_router_g': w_router_g[i], 'b_router_g': b_router_g[i],
            'w_router_e': w_router_e[i], 'b_router_e': b_router_e[i], 'w1': w1[i], 'w3': w3[i], 'w2': w2[i],
            'w_ple_proj': w_ple_proj[i], 'g_ple': g_ple[i], 'g_ple_gate': g_ple_gate[i], 'w_ple_gate': w_ple_gate[i],
        }
        z_h = jnp.zeros((bp, W_LRU), jnp.float32)
        z_lb = jnp.zeros((bp, CONV_W - 1, W_LRU), xp.dtype)
        z_s = jnp.zeros((bp, SSD_HEADS, SSD_HEADDIM, SSD_STATE), jnp.float32)
        z_sb = jnp.zeros((bp, CONV_W - 1, SSD_CONV_DIM), xp.dtype)
        xp, sp = decoder_layer(xp, p_prompt[i], z_h, z_lb, z_s, z_sb, True, lw)
        xs, ss = decoder_layer(xs, p_sample[i], state_lru_h[i], state_lru_conv[i], state_ssd[i], state_ssd_conv[i], False, lw)
        for j in range(4):
            st_p[j].append(sp[j])
            st_s[j].append(ss[j])
    y_prompt = rmsnorm(xp, g_final)
    y_sample = rmsnorm(xs, g_final)
    new_lru_h_p = jnp.stack(st_p[0]).astype(state_lru_h.dtype)
    new_lru_conv_p = jnp.stack(st_p[1]).astype(state_lru_conv.dtype)
    new_ssd_p = jnp.stack(st_p[2]).astype(state_ssd.dtype)
    new_ssd_conv_p = jnp.stack(st_p[3]).astype(state_ssd_conv.dtype)
    new_lru_h_s = jnp.stack(st_s[0]).astype(state_lru_h.dtype)
    new_lru_conv_s = jnp.stack(st_s[1]).astype(state_lru_conv.dtype)
    new_ssd_s = jnp.stack(st_s[2]).astype(state_ssd.dtype)
    new_ssd_conv_s = jnp.stack(st_s[3]).astype(state_ssd_conv.dtype)
    return (y_prompt, y_sample, new_lru_h_p, new_lru_conv_p, new_ssd_p, new_ssd_conv_p, new_lru_h_s, new_lru_conv_s, new_ssd_s, new_ssd_conv_s)


_drawn_inputs = setup_inputs


def setup_inputs(seed=0):
    import zlib

    import numpy as np

    out = dict(_drawn_inputs(seed))
    spreads = {}
    factors = {'lru_ba': 8.0,
     'lru_bx': 7.037,
     'ssd_D': 69.692,
     'b_router_g': 95.356,
     'b_router_e': 13.573,
     'g_ple': 63.356,
     'g_ple_gate': 8.0,
     'g_final': 23.297,
     'ssd_norm_g': 2.681,
     'g_ffn': 3.403}
    for name, (base, spread) in spreads.items():
        noise = np.random.default_rng([zlib.crc32(name.encode()), seed]).standard_normal(out[name].shape)
        drawn = base * np.exp(spread * noise) if base else spread * noise
        out[name] = __import__('jax').numpy.asarray(drawn.astype(out[name].dtype))
    for name, factor in factors.items():
        out[name] = (out[name] * factor).astype(out[name].dtype)
    return out
```

```python
from contextlib import ExitStack

import numpy as np

import concourse.bass as bass
from concourse import mybir

F32 = mybir.dt.float32
ALU = mybir.AluOpType
ACT = mybir.ActivationFunctionType
AX = mybir.AxisListType
ds = bass.ds

P = 128
D = 1024
KC = D // P
NP = 256
NB, NT = 8, 4
NS = NB * NT
T = NP + NS
QC = 2
TOK = [(0, P), (P, P), (NP, NS)]
G = 8
H = 32
PAD = 3 + NP + NB * (3 + NT)
SMP = 3 + NP
CVW = PAD - 3
EPS = 1e-6
NE, NEG, EPG, FF = 16, 4, 4, 512
FC = FF // P

O_LRU, O_LGATE, O_Z, O_XS = 0, 1024, 2048, 4096
O_B, O_C, O_DT, O_GA, O_GB = 6144, 7168, 8192, 8224, 9248
IN_COLS = 10272

C_SW, C_SB, C_LW, C_NG, C_GMIX, C_GFFN, C_GPLE, C_GPG, C_GFIN, C_LB, C_BA, C_BX, C_LAM, C_END = (
    0, 128, 160, 192, 208, 216, 224, 232, 240, 248, 256, 264, 272, 280)

K_ID, K_TRI, K_NEG, K_TRIS, K_NEGS, K_BM, K_TIE, K_ONE, K_SEL = 0, 128, 256, 384, 416, 448, 456, 460, 588
K_END = K_SEL + 16 * P


def constants():
    c = np.zeros((P, K_END), np.float32)
    s, q = np.arange(P)[:, None], np.arange(P)[None, :]
    c[:, K_ID:K_ID + P] = s == q
    c[:, K_TRI:K_TRI + P] = s <= q
    c[:, K_NEG:K_NEG + P] = np.where(s <= q, 0.0, -1e30)
    same = (s[:NS] // NT == q[:, :NS] // NT) & (s[:NS] <= q[:, :NS])
    c[:NS, K_TRIS:K_TRIS + NS] = same
    c[:NS, K_NEGS:K_NEGS + NS] = np.where(same, 0.0, -1e30)
    c[:NS, K_BM:K_BM + NB] = s[:NS] // NT == np.arange(NB)[None, :]
    c[:, K_TIE:K_TIE + 4] = 4.0 - np.arange(4)[None, :]
    c[:, K_ONE:K_ONE + P] = 1.0
    for j in range(16):
        c[:H, K_SEL + j * P:K_SEL + (j + 1) * P] = s[:H] == 2 * j + q // 64
    return c


class Signal:

    def __init__(self, sem, per=0, credit=0):
        self.sem, self.per, self.credit = sem, per, credit

    def at(self, g, k):
        return g * self.per + (k + self.credit)


class Chain:

    def __init__(self, eng, sem):
        self.eng, self.sem, self.base, self.k, self.g, self.per = eng, sem, 0, 0, 0, 0

    def enter(self, g, per):
        self.base += self.k
        self.g, self.per, self.k = g, per, 0

    def leave(self, steps):
        assert self.k == self.per, (self.k, self.per)
        self.base += steps * self.per
        self.g, self.per, self.k = 0, 0, 0

    def __call__(self, ins):
        self.k += 1
        ins.then_inc(self.sem, 1)
        self.eng.wait_ge(self.sem, self.g * self.per + (self.base + self.k))

    def tell(self, ins, sig, k):
        ins.then_inc(sig.sem, 1)
        self.eng.wait_ge(sig.sem, sig.at(self.g, k))

    def step(self, ins, steps, name):
        ins.then_inc(steps.sem, 1)
        self.eng.wait_ge(steps.sem, steps.at(name))


class Steps:

    def __init__(self, sem, names):
        self.sem, self.names = sem, list(names)

    def at(self, name):
        return self.names.index(name) + 1


def build(nc, a):
    with ExitStack() as ctx:
        def sb(name, shape):
            return ctx.enter_context(nc.sbuf_tensor(name, shape, F32))

        def sem(name):
            return ctx.enter_context(nc.semaphore(name))

        def sig(name, per=0, credit=0):
            return Signal(sem(name), per, credit)

        bank = [ctx.enter_context(nc.psum_tensor(f"bank{i}", [P, 512], F32)) for i in range(8)]
        bP, bT, bCB, bCU, bY, bYO = bank[0:2], bank[2], bank[3], bank[4], bank[5:7], bank[7]

        NSLOT = 12
        wb = sb("wb", [P, NSLOT, KC, P])
        wdt = sb("wdt", [P, KC, H])
        wr = sb("wr", [P, KC, 20])
        wg = sb("wg", [P, 2, P])
        cst = sb("cst", [P, K_SEL])
        par = sb("par", [P, C_END])
        xT = sb("xT", [P, KC, T])
        hT = sb("hT", [P, KC, T])
        ya = sb("ya", [P, KC, T])
        ga = sb("ga", [P, KC, T])
        gb = sb("gb", [P, KC, T])
        yb = sb("yb", [P, 16, T])
        EX = sb("EX", [P, 16, 161])
        cstS = sb("cstS", [P, 24, 32])
        cstL = sb("cstL", [P, 24, 8])
        h0T = sb("h0T", [P, NB, KC])
        stS = sb("stS", [P, 27, 32])
        stL = sb("stL", [P, 27, 8])
        hfin = sb("hfin", [P, 9, 8])
        TM = sb("TM", [P, 3, 3, H])
        cumT = sb("cumT", [H, T])
        rb = sb("rb", [1, 20])
        arena = sb("arena", [P, 7616])
        pads = [sb(f"pad{i}", [P, PAD]) for i in range(5)]
        cv = [sb(f"cv{i}", [P, PAD]) for i in range(2)]
        xbc = [sb(f"xbc{i}", [P, T]) for i in range(4)]
        zs = sb("zs", [P, 2, T])
        xdt = sb("xdt", [P, 3, 256])
        xdte = sb("xdte", [P, 3, 256])
        btok = sb("btok", [P, 3, P])
        tw = sb("tw", [P, 2, 512])
        tws = sb("tws", [NS, 4 * NS])
        sprev = sb("sprev", [P, 256])
        fin = sb("fin", [P, 2, P])
        u = sb("u", [P, T])
        rr = sb("rr", [P, T])
        ii = sb("ii", [P, T])
        TT = sb("TT", [P, T])
        aS = sb("aS", [P, T])
        gl = sb("gl", [P, T])
        kc2 = sb("kc2", [P, 2, 8])

        ident = cst[:, K_ID:K_ID + P]
        tri = cst[:, K_TRI:K_TRI + P]
        ones = cst[:, K_ONE:K_ONE + P]
        sel = wb[:, 10:12].rearrange("p a b c -> p (a b c)")
        sq = yb[:, 0:KC, :]

        Sin = arena[:, 0:2048].rearrange("p (j b n) -> p j b n", j=2, b=NB)
        Snew = arena[:, 2048:4096].rearrange("p (j b n) -> p j b n", j=2, b=NB)
        sT = arena[:, 4096:5120].rearrange("p (b n) -> p b n", b=NB)
        Bm = arena[0:NS, 5120:6144].rearrange("p (b n) -> p b n", b=NB)
        Dg = arena[0:H, 6144:7296].rearrange("p (h t) -> p h t", h=4)
        yot = arena[:, 7296:7616].rearrange("p (j t) -> p j t", j=2)
        xrow = arena[:, 0:3072].rearrange("p (c n) -> p c n", c=3)
        prow = arena[:, 3072:3456].rearrange("p (c n) -> p c n", c=3)
        srow = arena[:, 3456:4224].rearrange("p (c n) -> p c n", c=6)
        lrow = arena[:, 4224:4480].rearrange("p (c n) -> p c n", c=2)
        hrow = arena[:, 4480:4608]
        sp = [arena[:, 4608 + 296 * i:4904 + 296 * i] for i in range(5)]
        exr = arena[0:H, 6088:6249]
        aT = arena[0:H, 6249:6537]
        dteT = arena[0:H, 6537:6825]
        atok = arena[:, 6825:6921].rearrange("p (c h) -> p c h", c=3)
        hc = arena[0:H, 6921:6924]
        Acol = arena[0:H, 6924:6925]
        orow = arena[:, 0:1280].rearrange("p (c n) -> p c n", c=10)
        lrowo = arena[:, 1280:1408]
        plr = arena[:, 1408:2176].rearrange("p (c n) -> p c n", c=3)
        pT = arena[:, 2176:2752].rearrange("p (k t) -> p k t", k=2)
        rt = arena[:, 2752:3252]
        combT = arena[0:NE, 3252:3540]
        actT = arena[:, 3540:4692].rearrange("p (f t) -> p f t", f=FC)
        sg = [arena[:, 4692 + T * i:4980 + T * i] for i in range(2)]
        sgu = arena[:, 5268:5556]
        rs = arena[:, 5556:5844]
        rs2 = arena[:, 5844:6132]
        yrow = yb[:, :, :].rearrange("p a b -> p (a b)")[:, 0:3072].rearrange("p (c n) -> p c n", c=3)
        cbc = yb
        acc = ya
        eT = gb
        mg = hT

        rsP = rr
        XB = [0, 1, 2, 4, 5, 6, 7, 0]
        EB = [0, 1, 2, 4, 5, 6]
        R4 = [bT, bCB, bCU, bYO]
        BR = UP = [(bP[0], bP[1]), (bY[0], bY[1])]
        base_use = [G + 4] * 6 + [G + 2] * 4 + [0] * 2
        base_land = [G + 4] * 6 + [G + 2] * 4 + [1] * 2
        end_use = [b + NE + 1 for b in base_use]

        def rv(o, n, pat=None, **kw):
            w = rt[:, o:o + n]
            return w.rearrange(pat, **kw) if pat else w
        r_lg = rv(0, 60, "p (c n) -> p c n", c=3)
        r_goh, r_gs, r_es, r_o1, r_o2, r_e2 = (rv(64 + 12 * i, 12, "p (c n) -> p c n", c=3) for i in range(6))
        r_m, r_m2, r_gw = (rv(140 + 3 * i, 3) for i in range(3))
        r_pr = rv(152, 48, "p (c g j) -> p c g j", c=3, g=4)

        landed = [sem(f"landed{s}") for s in range(NSLOT)]
        used = [sem(f"used{s}") for s in range(NSLOT)]
        nload = [0] * NSLOT
        ncons = [0] * NSLOT

        d_cst, d_x, d_par, d_row, d_small, d_wdt, d_wr = (
            sem("d_cst"), sem("d_x"), sem("d_par"), sem("d_row"), sem("d_small"), sem("d_wdt"), sem("d_wr"))
        d_plr = sem("d_plr")
        d_out = sem("d_out")
        gate_landed = sem("gate_landed")
        sin_landed, state_out = sem("sin_landed"), sem("state_out")
        pe_pro = Steps(sem("pe_pro"), ["par"] + [f"x{k}" for k in range(KC)]
                       + ["hist", "rms", "dt", "atok", "cum", "tm"] + [f"ex{b}" for b in range(6)])
        act_pro = Steps(sem("act_pro"), [f"sq{k}" for k in range(KC)] + ["rs", "A", "z", "ln", "ecum", "dte"])
        dve_pro = Steps(sem("dve_pro"), ["par", "hist", "hT", "ax", "u", "soft", "aT", "atok", "cum", "dteT", "tm"]
                        + [f"ex{b}" for b in range(6)])
        dve_ch, act_ch, pool_ch = sem("dve_ch"), sem("act_ch"), sem("pool_ch")

        proj_free = sig("proj_free", 10, 2)
        pad_hist = sig("pad_hist", 5)
        conv_done = sig("conv_done", 5, 5)
        stashed = sig("stashed", 5, 5)
        silu_done = sig("silu_done", 4, 4)
        y_done = sig("y_done", 1, 1)
        T_ready, T_free = sig("T_ready", 8), sig("T_free", 8, 1)
        CU_ready, CU_free = sig("CU_ready", 8), sig("CU_free", 8, 1)
        CB_ready, CB_free = sig("CB_ready", 2), sig("CB_free", 1, 1)
        Y_ready, Y_free = sig("Y_ready", 2), sig("Y_free", 2, 1)
        YO_ready, YO_free = sig("YO_ready", 1, 1), sig("YO_free", 1, 1)
        dg_ready = sig("dg_ready", 1)
        masked = sig("masked", 3)
        decay_ready = sig("decay_ready", 3)
        W_ready = sig("W_ready", 3)
        xdte_ready = sig("xdte_ready", 3)
        bm_ready = sig("bm_ready", 1)
        sdec_ready = sig("sdec_ready", 2)
        lru_act = sig("lru_act", 1)
        m2_ready = sig("m2_ready", 1)
        m_ready = sig("m_ready", 1)
        gelu_ready = sig("gelu_ready", 1)
        lru_tail = sig("lru_tail", 1, 1)
        sq_ready = sig("sq_ready", 1)
        br_done = sig("br_done", 2, 2)
        gates_ready = sem("gates_ready")
        pe_mid = Steps(sem("pe_mid"), ["st", "pT", "frms"] + [f"e{j}" for j in range(8)]
                       + ["erms", "route", "combT"] + [f"cbc{e}" for e in range(NE)])
        act_mid = Steps(sem("act_mid"), [f"sqf{j}" for j in range(8)] + ["st", "pT", "frs"]
                        + [f"e{j}" for j in range(8)] + ["ers", "gexp", "eexp"] + [f"cbc{e}" for e in range(0, NE, 2)])
        dve_mid = Steps(sem("dve_mid"), [f"x2_{j}" for j in range(8)] + ["hf", "eN", "gsub", "esub", "comb", "combT"]
                        + [f"cbc{e}" for e in range(1, NE, 2)])
        silu_e = sig("silu_e", 4)
        act_ready = sig("act_ready", 4, 2)
        dn_ready, dn_done = sig("dn_ready", 4), sig("dn_done", 8, 4)
        pe_end = Steps(sem("pe_end"), ["grms", "yrms"] + [f"out{i}" for i in range(6)])
        act_end = Steps(sem("act_end"), [f"sg{j}" for j in range(8)] + ["grs"]
                        + [n for j in range(8) for n in (f"sig{j}", f"sy{j}")] + ["yrs"])
        dve_end = Steps(sem("dve_end"), [f"x3_{j}" for j in range(8)] + ["hg"] + [f"x4_{j}" for j in range(8)]
                        + ["hy"] + [f"out{i}" for i in range(6)])

        w_in = a["w_in"][0].rearrange("(k p) c -> p k c", p=P)
        w1 = a["w1"].rearrange("l e (k p) f -> (l e) p k f", p=P)
        w3 = a["w3"].rearrange("l e (k p) f -> (l e) p k f", p=P)
        w2 = a["w2"].rearrange("l e (k p) n -> (l e) p k n", p=P)
        w_lru = a["w_br_lru"][0].rearrange("(k p) c -> p k c", p=P)
        w_ssd = a["w_br_ssd"][0].rearrange("(k p) c -> p k c", p=P)
        w_out = a["w_out"][0].rearrange("(k p) c -> p k c", p=P)
        w_pp = a["w_ple_proj"][0].rearrange("(k p) c -> p k c", p=P)
        w_pg = a["w_ple_gate"][0].rearrange("(k p) c -> p k c", p=P)
        wa = a["lru_wa"][0].rearrange("n c d -> c n d")
        wx = a["lru_wx"][0].rearrange("n c d -> c n d")
        st_in = a["state_ssd"].rearrange("l b h p n -> (l h p) b n")
        st_out = a["new_ssd_s"].rearrange("l b h p n -> (l h p) b n")
        stp_out = a["new_ssd_p"].rearrange("l b h p n -> (l b h p) n")

        BLOCKS = [(O_XS, 256), (O_XS + 128, 256), (O_B, 128), (O_C, 128), (O_LRU, 128),
                  (O_Z, 256), (O_Z + 128, 256), (O_LGATE, 128), (O_GA, 128), (O_GB, 128)]

        block = ctx.enter_context(nc.Block())

        @block.sync
        def _(sp_):
            eng = nc.sync
            eng.dma_start(xrow[:, 0:2, :], a["x_prompt"][0].rearrange("(c p) d -> p c d", p=P)).then_inc(d_x, 16)
            eng.dma_start(xrow[0:NS, 2, :], a["x_sample"].rearrange("b t d -> (b t) d")).then_inc(d_x, 16)
            eng.dma_start(wdt[:], w_in[:, :, O_DT:O_DT + H]).then_inc(d_wdt, 16)

            def load(s, dst, src):
                if nload[s] > 0:
                    sp_.wait_ge(used[s], nload[s])
                eng.dma_start(dst, src).then_inc(landed[s], 16)
                nload[s] += 1

            for s in range(10):
                o, w = BLOCKS[s]
                load(s, wb[:, s], w_in[:, :, o:o + P])
            eng.dma_start(wg[:, 0, :], wa[:, 0, :]).then_inc(gate_landed, 16)
            eng.dma_start(wg[:, 1, :], wx[:, 0, :]).then_inc(gate_landed, 16)
            sp_.sem_inc(state_out, 1)
            sp_.wait_ge(act_pro.sem, act_pro.at("dte"))
            sp_.wait_ge(dve_pro.sem, dve_pro.at("ex5"))
            sp_.wait_ge(pe_pro.sem, pe_pro.at("ex5"))
            for j in range(2):
                eng.dma_start(Sin[:, j], st_in[j * P:(j + 1) * P]).then_inc(sin_landed, 16)
            with sp_.Fori(1, G) as g:
                col1, col2 = sp_.snap(g * 128), sp_.snap(g * 256)
                for s in range(10):
                    o, w = BLOCKS[s]
                    col = {128: col1, 256: col2}[w]
                    sp_.wait_ge(used[s], g)
                    if s == 4:
                        sp_.wait_ge(Y_ready.sem, Y_ready.at(g - 1, 1))
                        eng.dma_start(wg[:, 0, :], wa[:, ds(g, 1), :]).then_inc(gate_landed, 16)
                        eng.dma_start(wg[:, 1, :], wx[:, ds(g, 1), :]).then_inc(gate_landed, 16)
                    eng.dma_start(wb[:, s], w_in[:, :, ds(col + o, P)]).then_inc(landed[s], 16)
                sp_.wait_ge(CU_free.sem, CU_free.at(g - 1, 4))
                eng.dma_start(stp_out[ds((g - 1) * 256, 256)].rearrange("(j q) n -> q j n", j=2), fin[:]).then_inc(state_out, 16)
                sp_.wait_ge(CU_free.sem, CU_free.at(g - 1, 8))
                for j in range(2):
                    eng.dma_start(st_out[ds((g - 1) * 256 + j * P, P)], Snew[:, j]).then_inc(state_out, 16)
                for j in range(2):
                    eng.dma_start(Sin[:, j], st_in[ds(g * 256 + j * P, P)]).then_inc(sin_landed, 16)
            for s in range(10):
                nload[s] = G
            sp_.wait_ge(CU_free.sem, CU_free.at(G - 1, 4))
            eng.dma_start(stp_out[7 * 256:8 * 256].rearrange("(j q) n -> q j n", j=2), fin[:]).then_inc(state_out, 16)
            sp_.wait_ge(CU_free.sem, CU_free.at(G - 1, 8))
            for j in range(2):
                eng.dma_start(st_out[7 * 256 + j * P:7 * 256 + (j + 1) * P], Snew[:, j]).then_inc(state_out, 16)

            def branch(j, o, wait):
                for s, src in ((o, w_lru[:, :, ds(j * P, P)]), (o + 1, w_ssd[:, 0:8, ds(j * P, P)]),
                               (o + 2, w_ssd[:, 8:16, ds(j * P, P)])):
                    sp_.wait_ge(used[s], wait)
                    eng.dma_start(wb[:, s], src).then_inc(landed[s], 16)
            branch(0, 0, G)
            branch(1, 3, G)
            for i in range(4):
                load(6 + i, wb[:, 6 + i], w_out[:, :, i * P:(i + 1) * P])
            with sp_.Fori(1, 4) as i:
                branch(2 * i, 0, G + i)
                branch(2 * i + 1, 3, G + i)
            for s in range(6):
                nload[s] = G + 4
            for i in range(4):
                load(6 + i, wb[:, 6 + i], w_out[:, :, (4 + i) * P:(5 + i) * P])
            sp_.wait_ge(state_out, 16 * 3 * G + 1)
            for c in range(2):
                eng.dma_start(plr[:, c, :], a["p_prompt"][0, 0, c * P:(c + 1) * P, :]).then_inc(d_plr, 16)
            eng.dma_start(plr[0:NS, 2, :], a["p_sample"][0].rearrange("b t d -> (b t) d")).then_inc(d_plr, 16)
            for i in range(2):
                load(10 + i, wb[:, 10 + i].rearrange("p a b -> p (a b)").rearrange("p (k c) -> p k c", k=2),
                     w_pp[:, :, i * 512:(i + 1) * 512])
            def w2_slot(s):
                return wb[:, s].rearrange("p a b -> p (a b)").rearrange("p (k c) -> p k c", k=FC)
            for f in range(FC):
                load(f, wb[:, f], w1[0, :, :, f * P:(f + 1) * P])
                load(FC + f, wb[:, FC + f], w3[0, :, :, f * P:(f + 1) * P])
            for i in range(2):
                load(8 + i, w2_slot(8 + i), w2[0, :, :, i * 256:(i + 1) * 256])
            for i in range(2, 4):
                sp_.wait_ge(pe_mid.sem, pe_mid.at(f"e{4 * i - 5}"))
                eng.dma_start(w2_slot(8 + i), w2[0, :, :, i * 256:(i + 1) * 256]).then_inc(landed[8 + i], 16)
            first = [b + 1 for b in base_use]
            assert nload[0:10] == first[0:10]
            with sp_.Fori(1, NE) as e:
                for f in range(FC):
                    for s, w in ((f, w1), (FC + f, w3)):
                        sp_.wait_ge(used[s], e + (first[s] - 1))
                        eng.dma_start(wb[:, s], w[ds(e, 1), :, :, f * P:(f + 1) * P]).then_inc(landed[s], 16)
                for i in range(4):
                    sp_.wait_ge(used[8 + i], e + (first[8 + i] - 1))
                    eng.dma_start(w2_slot(8 + i), w2[ds(e, 1), :, :, i * 256:(i + 1) * 256]).then_inc(landed[8 + i], 16)
            for s in range(NSLOT):
                nload[s] += NE - 1
            for i in range(8):
                load(i, wb[:, i], w_pg[:, :, i * P:(i + 1) * P])
            sp_.wait_ge(act_mid.sem, act_mid.at("st"))
            eng.dma_start(a["new_ssd_conv_p"].rearrange("l b r (c x) -> (l b r c) x", x=P), orow[0:96, 0, :]).then_inc(d_out, 16)
            eng.dma_start(a["new_ssd_conv_s"].rearrange("l b r (c x) -> (l b r c) x", x=P).rearrange("(t q) x -> q t x", q=P),
                          orow[:, 1:7, :]).then_inc(d_out, 16)
            eng.dma_start(a["new_lru_conv_p"].rearrange("l b r (c x) -> (l b r c) x", x=P), orow[0:24, 7, :]).then_inc(d_out, 16)
            eng.dma_start(a["new_lru_conv_s"].rearrange("l b r (c x) -> (l b r c) x", x=P).rearrange("(t q) x -> q t x", q=96),
                          orow[0:96, 8:10, :]).then_inc(d_out, 16)
            eng.dma_start(a["new_lru_h_p"].rearrange("l b (c x) -> (l b c) x", x=P), lrowo[0:8, :]).then_inc(d_out, 16)
            eng.dma_start(a["new_lru_h_s"].rearrange("l b (c x) -> (l b c) x", x=P), lrowo[8:72, :]).then_inc(d_out, 16)
            sp_.wait_ge(dve_end.sem, dve_end.at("out5"))
            eng.dma_start(a["y_prompt"][0].rearrange("(c p) d -> p c d", p=P), yrow[:, 0:2, :]).then_inc(d_out, 16)
            eng.dma_start(a["y_sample"].rearrange("b t d -> (b t) d"), yrow[0:NS, 2, :]).then_inc(d_out, 16)
            sp_.wait_ge(d_out, 16 * 8)
            sp_.wait_ge(state_out, 16 * 3 * G + 1)

        @block.gpsimd
        def _(pool):
            eng = nc.gpsimd
            ch = Chain(pool, pool_ch)
            pool.sem_inc(stashed.sem, 5)
            pool.wait_ge(dve_pro.sem, dve_pro.at("ex5"))
            pool.wait_ge(pe_pro.sem, pe_pro.at("ex5"))
            with pool.Fori(0, G) as g:
                ch.enter(g, 5)
                for i, (src, at) in enumerate(((cstS, 2 * g), (cstS, 2 * g + 1), (cstS, g + 16), (cstS, g + 24), (cstL, g))):
                    pool.wait_ge(conv_done.sem, g * 5 + (i + 1))
                    pool.wait_ge(stashed.sem, g * 5 + (i + 1))
                    v = pads[i][:, SMP:PAD].rearrange("p (b r) -> p b r", r=7)[:, :, 0:3]
                    ch.tell(eng.tensor_copy(v, src[:, :, ds(at, 1)].rearrange("p (b r) o -> p b (r o)", r=3)), pad_hist, i + 1)
                pool.wait_ge(YO_ready.sem, YO_ready.at(g, 0))
                ch.tell(eng.tensor_tensor(Dg, cumT[:].unsqueeze(1).to_broadcast([H, 4, T]),
                                          cst[0:H, ds(g * 4, 4)].unsqueeze(2).to_broadcast([H, 4, T]), ALU.mult), dg_ready, 1)
                for i, (dst, at) in enumerate(((stS, 2 * g), (stS, 2 * g + 1), (stS, g + 16), (stS, g + 24), (stL, g))):
                    pool.wait_ge(proj_free.sem, proj_free.at(g, i + 1))
                    ch(eng.tensor_copy(dst[:, 0:3, ds(at, 1)].rearrange("p r o -> p (r o)"), pads[i][:, NP:NP + 3]))
                    v = pads[i][:, SMP:PAD].rearrange("p (b r) -> p b r", r=7)[:, :, 4:7]
                    ch.tell(eng.tensor_copy(dst[:, 3:27, ds(at, 1)].rearrange("p (b r) o -> p b (r o)", r=3), v), stashed, i + 1)
                for c, (t0, n) in enumerate(TOK):
                    pool.wait_ge(CU_free.sem, CU_free.at(g, c + 1))
                    t = tw[:, c, :] if c < 2 else tws[:]
                    m = cst[0:n, K_NEG:K_NEG + P] if c < 2 else cst[0:n, K_NEGS:K_NEGS + NS]
                    t4 = t.rearrange("p (h q) -> p h q", h=4)
                    ch.tell(eng.tensor_tensor(t4, t4, m.unsqueeze(1).to_broadcast([n, 4, n]), ALU.add), masked, c + 1)
                    pool.wait_ge(T_free.sem, T_free.at(g, c + 1))
                    ch.tell(eng.tensor_tensor(xdte[0:n, c, :].rearrange("p (h e) -> p h e", h=4),
                                              xdt[0:n, c, :].rearrange("p (h e) -> p h e", h=4),
                                              TM[0:n, 2, c, ds(g * 4, 4)].unsqueeze(2).to_broadcast([n, 4, 64]), ALU.mult),
                            xdte_ready, c + 1)
                ch.tell(eng.tensor_tensor(Bm, btok[0:NS, 2, :].unsqueeze(1).to_broadcast([NS, NB, P]),
                                          cst[0:NS, K_BM:K_BM + NB].unsqueeze(2).to_broadcast([NS, NB, P]), ALU.mult), bm_ready, 1)
                for j in range(2):
                    pool.wait_ge(sin_landed, g * 32 + 32)
                    if j == 0:
                        pool.wait_ge(state_out, g * 48 + 1)
                    dec = EX[:, ds(2 * g + j, 1), 128 + 3:160:4].rearrange("p o b -> p (o b)")
                    ch.tell(eng.tensor_tensor(Snew[:, j], Sin[:, j], dec.unsqueeze(2).to_broadcast([P, NB, P]), ALU.mult), sdec_ready, j + 1)
            ch.leave(G)

        @block.scalar
        def _(act):
            eng = nc.scalar
            ch = Chain(act, act_ch)
            act_f = eng.activation
            q = nc.scalar
            q.dma_start(cst[:], a["constants"][:, 0:K_SEL]).then_inc(d_cst, 16)
            rows = {
                0: [("ssd_conv_w", "l k (c x) -> (l k c) x")],
                1: [("ssd_conv_b", "l (c x) -> (l c) x"), ("lru_conv_w", "l k (c x) -> (l k c) x"),
                    ("ssd_norm_g", "l (c x) -> (l c) x"), ("g_mix", "l (c x) -> (l c) x"), ("g_ffn", "l (c x) -> (l c) x"),
                    ("g_ple", "l (c x) -> (l c) x"), ("g_ple_gate", "l (c x) -> (l c) x"), ("g_final", "(c x) -> c x"),
                    ("lru_conv_b", "l (c x) -> (l c) x")],
                2: [("lru_ba", "l (c x) -> (l c) x"), ("lru_bx", "l (c x) -> (l c) x"), ("lru_lambda", "l (c x) -> (l c) x")],
            }
            for t, ps in rows.items():
                r = 0
                for name, pat in ps:
                    src = a[name].rearrange(pat, x=P)
                    n = src.shape[0]
                    q.dma_start(prow[r:r + n, t, :], src).then_inc(d_par, 16)
                    r += n
            q.dma_start(srow, a["state_ssd_conv"].rearrange("l b r (c x) -> (l b r c) x", x=P).rearrange("(t q) x -> q t x", q=P)).then_inc(d_row, 16)
            q.dma_start(lrow[0:96], a["state_lru_conv"].rearrange("l b r (c x) -> (l b r c) x", x=P).rearrange("(t q) x -> q t x", q=96)).then_inc(d_row, 16)
            q.dma_start(hrow[0:64], a["state_lru_h"].rearrange("l b (c x) -> (l b c) x", x=P)).then_inc(d_row, 16)
            for i, name in enumerate(("ssd_dt_bias", "ssd_A_log", "ssd_D")):
                q.dma_start(hc[:, i:i + 1], a[name].rearrange("l h -> h l")).then_inc(d_small, 16)
            q.dma_start(sel[0:H], a["constants"][0:H, K_SEL:K_END]).then_inc(d_cst, 16)
            q.dma_start(rb[:, 0:4], a["b_router_g"]).then_inc(d_wr, 16)
            q.dma_start(rb[:, 4:20], a["b_router_e"]).then_inc(d_wr, 16)
            q.dma_start(wr[:, :, 0:4], a["w_router_g"][0].rearrange("(k p) c -> p k c", p=P)).then_inc(d_wr, 16)
            q.dma_start(wr[:, :, 4:20], a["w_router_e"][0].rearrange("(k p) c -> p k c", p=P)).then_inc(d_wr, 16)
            for k in range(KC):
                b = bank[XB[k]]
                act.wait_ge(pe_pro.sem, pe_pro.at(f"x{k}"))
                ch(act_f(xT[:, k, :], b[:, 0:T], ACT.Copy))
                ch.step(act_f(sq[:, k, :], b[:, 0:T], ACT.Square), act_pro, f"sq{k}")
            act.wait_ge(pe_pro.sem, pe_pro.at("rms"))
            ch(act_f(rsP[:], bCB[:, 0:T], ACT.Ln, bias=EPS, scale=1.0 / D))
            ch.step(act_f(rsP[:], rsP[:], ACT.Exp, scale=-0.5), act_pro, "rs")
            act.wait_ge(d_small, 48)
            ch.step(act_f(Acol, hc[:, 1:2], ACT.Exp), act_pro, "A")
            act.wait_ge(dve_pro.sem, dve_pro.at("ax"))
            ch.step(act_f(sp[2], sp[1], ACT.Exp, scale=-1.0), act_pro, "z")
            act.wait_ge(dve_pro.sem, dve_pro.at("u"))
            ch.step(act_f(sp[4], sp[3], ACT.Ln), act_pro, "ln")
            act.wait_ge(dve_pro.sem, dve_pro.at("cum"))
            ch.step(act_f(exr[:, 0:160], cumT[:, P:T], ACT.Exp), act_pro, "ecum")
            act.wait_ge(dve_pro.sem, dve_pro.at("dteT"))
            ch.step(act_f(dteT, dteT, ACT.Exp), act_pro, "dte")

            act.sem_inc(proj_free.sem, 2)
            act.sem_inc(silu_done.sem, 4)
            act.sem_inc(T_free.sem, 1)
            act.sem_inc(CB_free.sem, 1)

            def samples(v):
                return v.rearrange("p (b t) -> p b t", t=NT)

            def new_tokens(v, r0):
                return v[:, SMP:PAD].rearrange("p (b r) -> p b r", r=7)[:, :, r0:r0 + NT]

            with act.Fori(0, G) as g:
                ch.enter(g, 11)

                def evac(i):
                    act.wait_ge(used[i], g + 1)
                    act.wait_ge(conv_done.sem, conv_done.at(g, i + 1 - 5))
                    act.wait_ge(stashed.sem, stashed.at(g, i + 1 - 5))
                    ch(act_f(pads[i][:, 3:SMP], bP[i % 2][:, 0:NP], ACT.Copy))
                    ch.tell(act_f(new_tokens(pads[i], 3), samples(bP[i % 2][:, NP:T]), ACT.Copy), proj_free, i + 1)

                def silu(i):
                    act.wait_ge(conv_done.sem, conv_done.at(g, i + 1))
                    ch(act_f(xbc[i][:, 0:NP], cv[i % 2][:, 0:NP], ACT.Silu))
                    ch.tell(act_f(samples(xbc[i][:, NP:T]), new_tokens(cv[i % 2], 0), ACT.Silu), silu_done, i + 1)

                def decay(c):
                    act.wait_ge(masked.sem, masked.at(g, c + 1))
                    t = tw[:, c, :] if c < 2 else tws[:]
                    ch.tell(act_f(t, t, ACT.Exp), decay_ready, c + 1)

                def raw(i, dst):
                    act.wait_ge(used[i], g + 1)
                    ch.tell(act_f(dst, bP[i % 2][:, 0:T], ACT.Copy), proj_free, i + 1)

                def from_T(k, dst, n):
                    act.wait_ge(T_ready.sem, T_ready.at(g, k))
                    ch.tell(act_f(dst, bT[:, 0:n], ACT.Copy), T_free, k)

                evac(0)
                evac(1)
                act.wait_ge(YO_ready.sem, YO_ready.at(g, 0))
                act.wait_ge(y_done.sem, y_done.at(g, 0))
                silu(0)
                evac(2)
                silu(1)
                evac(3)
                silu(2)
                evac(4)
                silu(3)
                act.wait_ge(lru_tail.sem, lru_tail.at(g, 0))
                for j in range(2):
                    act.wait_ge(used[5 + j], g + 1)
                    ch.tell(act_f(zs[:, j, :], bP[(5 + j) % 2][:, 0:T], ACT.Silu), proj_free, 6 + j)
                act.wait_ge(Y_ready.sem, Y_ready.at(g, 1))
                ch(act_f(rr[:], bY[0][:, 0:T], ACT.Sigmoid, bias=par[:, ds(g + C_BA, 1)]))
                ch.tell(act_f(ii[:], bY[1][:, 0:T], ACT.Sigmoid, bias=par[:, ds(g + C_BX, 1)]), Y_free, 1)
                ch(act_f(TT[:], rr[:], ACT.Tanh, scale=kc2[:, 1, ds(g, 1)]))
                ch.tell(act_f(aS[:], rr[:], ACT.Exp, scale=kc2[:, 0, ds(g, 1)]), lru_act, 1)
                decay(0)
                raw(7, gl[:])
                decay(1)
                decay(2)
                raw(8, ga[:, ds(g, 1), :].rearrange("p o t -> p (o t)"))
                from_T(4, sprev[:], 256)
                from_T(5, sT[:, 0:4, :].rearrange("p b n -> p (b n)"), 512)
                from_T(6, sT[:, 4:8, :].rearrange("p b n -> p (b n)"), 512)
                raw(9, gb[:, ds(g, 1), :].rearrange("p o t -> p (o t)"))
                from_T(7, sT[:, 0:4, :].rearrange("p b n -> p (b n)"), 512)
                from_T(8, sT[:, 4:8, :].rearrange("p b n -> p (b n)"), 512)
                act.wait_ge(m2_ready.sem, m2_ready.at(g, 1))
                ch.tell(act_f(TT[:], TT[:], ACT.Sqrt), m_ready, 1)
                act.wait_ge(y_done.sem, y_done.at(g, 1))
                ch.tell(act_f(tw[:, :, 0:T], yb[:, ds(2 * g, 2), :], ACT.Square), sq_ready, 1)
                act.wait_ge(CB_ready.sem, CB_ready.at(g, 2))
                ch.tell(act_f(zs[:, 0, :], bCB[:, 0:T], ACT.Sqrt, bias=EPS, scale=1.0 / 256), CB_free, 1)
                ch.tell(act_f(gl[:], gl[:], ACT.Gelu_apprx_tanh), gelu_ready, 1)
            ch.leave(G)

            ch(act_f(ga[:], ga[:], ACT.Sigmoid))
            act_f(gb[:], gb[:], ACT.Sigmoid).then_inc(gates_ready, 1)
            act.wait_ge(gates_ready, 1)
            for j in range(8):
                act.wait_ge(dve_mid.sem, dve_mid.at(f"x2_{j}"))
                ch.step(act_f(sq[:, j, :], xT[:, j, :], ACT.Square), act_mid, f"sqf{j}")
            act.wait_ge(pe_mid.sem, pe_mid.at("st"))
            ch(act_f(orow[0:96, 0, :], bT[0:96, 0:P], ACT.Copy))
            ch(act_f(orow[:, 1:4, :].rearrange("p c n -> p (c n)"), bT[:, P:512], ACT.Copy))
            ch(act_f(orow[:, 4:7, :].rearrange("p c n -> p (c n)"), bCB[:, 0:384], ACT.Copy))
            ch(act_f(orow[0:24, 7, :], bCB[0:24, 384:512], ACT.Copy))
            ch(act_f(orow[0:96, 8:10, :].rearrange("p c n -> p (c n)"), bCU[0:96, 0:256], ACT.Copy))
            ch.step(act_f(lrowo[0:72], bCU[0:72, 256:384], ACT.Copy), act_mid, "st")
            act.wait_ge(pe_mid.sem, pe_mid.at("pT"))
            ch(act_f(pT[:, 0, :], bY[0][:, 0:T], ACT.Copy))
            ch.step(act_f(pT[:, 1, :], bY[1][:, 0:T], ACT.Copy), act_mid, "pT")
            act.wait_ge(pe_mid.sem, pe_mid.at("frms"))
            ch(act_f(rs, bP[0][:, 0:T], ACT.Ln, bias=EPS, scale=1.0 / D))
            ch.step(act_f(rs, rs, ACT.Exp, scale=-0.5), act_mid, "frs")
            for j in range(8):
                act.wait_ge(pe_mid.sem, pe_mid.at(f"e{j}"))
                ch(act_f(eT[:, j, :], R4[j % 4][:, 0:T], ACT.Copy))
                ch.step(act_f(ga[:, j, :], R4[j % 4][:, 0:T], ACT.Square), act_mid, f"e{j}")
            act.wait_ge(pe_mid.sem, pe_mid.at("erms"))
            ch(act_f(rs2, bP[1][:, 0:T], ACT.Ln, bias=EPS, scale=1.0 / D))
            ch.step(act_f(rs2, rs2, ACT.Exp, scale=-0.5), act_mid, "ers")
            act.wait_ge(dve_mid.sem, dve_mid.at("gsub"))
            ch.step(act_f(r_gs, r_gs, ACT.Exp), act_mid, "gexp")
            act.wait_ge(dve_mid.sem, dve_mid.at("esub"))
            ch.step(act_f(r_es, r_es, ACT.Exp), act_mid, "eexp")
            for e in range(0, NE, 2):
                act.wait_ge(pe_mid.sem, pe_mid.at(f"cbc{e}"))
                ch.step(act_f(cbc[:, e, :], R4[e % 4][:, 0:T], ACT.Copy), act_mid, f"cbc{e}")
            with act.Fori(0, NE) as e:
                ch.enter(e, 0)
                for f in range(FC):
                    act.wait_ge(used[f], e + (base_use[f] + 1))
                    act.wait_ge(act_ready.sem, act_ready.at(e, f - 1))
                    ch.tell(act_f(sg[f % 2], UP[f % 2][0][:, 0:T], ACT.Silu), silu_e, f + 1)
            ch.leave(NE)
            for j in range(8):
                act.wait_ge(dve_end.sem, dve_end.at(f"x3_{j}"))
                ch.step(act_f(sq[:, j, :], xT[:, j, :], ACT.Square), act_end, f"sg{j}")
            act.wait_ge(pe_end.sem, pe_end.at("grms"))
            ch(act_f(rs, bP[0][:, 0:T], ACT.Ln, bias=EPS, scale=1.0 / D))
            ch.step(act_f(rs, rs, ACT.Exp, scale=-0.5), act_end, "grs")
            for j in range(8):
                act.wait_ge(used[j], end_use[j])
                if j >= 2:
                    act.wait_ge(dve_end.sem, dve_end.at(f"x4_{j - 2}"))
                ch.step(act_f(sg[j % 2], R4[j % 4][:, 0:T], ACT.Sigmoid), act_end, f"sig{j}")
                act.wait_ge(dve_end.sem, dve_end.at(f"x4_{j}"))
                ch.step(act_f(sq[:, j, :], xT[:, j, :], ACT.Square), act_end, f"sy{j}")
            act.wait_ge(pe_end.sem, pe_end.at("yrms"))
            ch(act_f(rs, bP[1][:, 0:T], ACT.Ln, bias=EPS, scale=1.0 / D))
            ch.step(act_f(rs, rs, ACT.Exp, scale=-0.5), act_end, "yrs")

        @block.vector
        def _(dve):
            v = nc.vector
            ch = Chain(dve, dve_ch)
            dve.wait_ge(pe_pro.sem, pe_pro.at("par"))
            ch.step(v.tensor_copy(par[:], bCB[:, 0:C_END]), dve_pro, "par")
            for i in range(5):
                ch(v.memset(pads[i][:, 0:3], 0.0))
            ch(v.memset(sp[0], 0.0))
            dve.wait_ge(pe_pro.sem, pe_pro.at("hist"))
            cs = cstS[:].rearrange("p a b -> p (a b)")
            ch(v.tensor_copy(cs[:, 0:512], bank[1][:, :]))
            ch(v.tensor_copy(cs[:, 512:768], bank[2][:, 0:256]))
            ch(v.tensor_copy(cstL[:].rearrange("p a b -> p (a b)"), bank[2][:, 256:448]))
            ch.step(v.tensor_copy(h0T[:].rearrange("p a b -> p (a b)"), bank[2][:, 448:512]), dve_pro, "hist")

            def norm(dst, src, col, r, steps, name):
                for k in range(KC):
                    ins = v.scalar_tensor_tensor(out=dst[:, k, :], in0=src[:, k, :], scalar=par[:, col + k:col + k + 1],
                                                 in1=r, op0=ALU.mult, op1=ALU.mult)
                    if k < KC - 1:
                        ch(ins)
                    else:
                        ch.step(ins, steps, name)

            dve.wait_ge(act_pro.sem, act_pro.at("rs"))
            norm(hT, xT, C_GMIX, rsP[:], dve_pro, "hT")
            dve.wait_ge(pe_pro.sem, pe_pro.at("dt"))
            dve.wait_ge(d_small, 48)
            ch(v.tensor_scalar(sp[0][0:H, 0:T], bank[4][0:H, 0:T], hc[:, 0:1], None, ALU.add))
            ch(v.tensor_scalar(sp[0][:, T:T + 8], par[:, C_LAM:C_LAM + 8], -1.0, None, ALU.mult))
            ch.step(v.scalar_tensor_tensor(out=sp[1], in0=sp[0], scalar=-1.0, in1=sp[0], op0=ALU.mult, op1=ALU.max), dve_pro, "ax")
            dve.wait_ge(act_pro.sem, act_pro.at("z"))
            ch.step(v.tensor_scalar(sp[3], sp[2], 1.0, None, ALU.add), dve_pro, "u")
            dve.wait_ge(act_pro.sem, act_pro.at("ln"))
            ch(v.tensor_scalar(sp[3], sp[3], -1.0, 1e-30, ALU.add, ALU.add))
            ch(v.reciprocal(sp[3], sp[3]))
            ch(v.scalar_tensor_tensor(out=sp[4], in0=sp[4], scalar=1e-30, in1=sp[3], op0=ALU.add, op1=ALU.mult))
            ch(v.tensor_tensor(sp[4], sp[4], sp[2], ALU.mult))
            ch.step(v.scalar_tensor_tensor(out=sp[0], in0=sp[0], scalar=0.0, in1=sp[4], op0=ALU.max, op1=ALU.add), dve_pro, "soft")
            ch(v.tensor_scalar(kc2[:, 0, :], sp[0][:, T:T + 8], -8.0, None, ALU.mult))
            ch(v.tensor_scalar(kc2[:, 1, :], sp[0][:, T:T + 8], 8.0, None, ALU.mult))
            dve.wait_ge(act_pro.sem, act_pro.at("A"))
            ch.step(v.tensor_scalar(aT, sp[0][0:H, 0:T], Acol, -1.0, ALU.mult, ALU.mult), dve_pro, "aT")
            dve.wait_ge(pe_pro.sem, pe_pro.at("atok"))
            ch(v.tensor_copy(atok[:, 0:2, :].rearrange("p c h -> p (c h)"), bank[5][:, 0:2 * H]))
            ch.step(v.tensor_copy(atok[0:NS, 2, :], bank[5][0:NS, 2 * H:3 * H]), dve_pro, "atok")
            dve.wait_ge(pe_pro.sem, pe_pro.at("cum"))
            ch.step(v.tensor_copy(cumT[:], bank[6][0:H, 0:T]), dve_pro, "cum")
            for c in range(QC):
                ch(v.tensor_scalar(dteT[:, c * P:(c + 1) * P], cumT[:, c * P:(c + 1) * P], -1.0,
                                   cumT[:, (c + 1) * P - 1:(c + 1) * P], ALU.mult, ALU.add))
            ct = cumT[:, NP:T].rearrange("p (b t) -> p b t", t=NT)
            ch(v.tensor_tensor(dteT[:, NP:T].rearrange("p (b t) -> p b t", t=NT), ct[:, :, NT - 1:NT].to_broadcast([H, NB, NT]),
                               ct, ALU.subtract))
            ch.step(v.tensor_copy(exr[:, 160:161], hc[:, 2:3]), dve_pro, "dteT")
            dve.wait_ge(pe_pro.sem, pe_pro.at("tm"))
            tmb = bank[7][:, 0:9 * H].rearrange("p (k c h) -> p k c h", k=3, c=3)
            ch(v.tensor_copy(TM[:, :, 0:2, :].rearrange("p k c h -> p k (c h)"), tmb[:, :, 0:2, :].rearrange("p k c h -> p k (c h)")))
            ch.step(v.tensor_copy(TM[0:NS, :, 2, :], tmb[0:NS, :, 2, :]), dve_pro, "tm")
            for i in range(6):
                n = min(3, 16 - 3 * i)
                dve.wait_ge(pe_pro.sem, pe_pro.at(f"ex{i}"))
                ch.step(v.tensor_copy(EX[:, 3 * i:3 * i + n, :].rearrange("p j t -> p (j t)"), bank[EB[i]][:, 0:161 * n]), dve_pro, f"ex{i}")

            dve.sem_inc(conv_done.sem, 5)
            dve.sem_inc(y_done.sem, 1)
            dve.sem_inc(CU_free.sem, 1)
            dve.sem_inc(Y_free.sem, 1)
            dve.sem_inc(YO_free.sem, 1)
            dve.sem_inc(lru_tail.sem, 1)

            def new_tokens(w):
                return w[:, SMP:PAD].rearrange("p (b r) -> p b r", r=7)[:, :, 0:NT]

            def samples(w):
                return w.rearrange("p (b t) -> p b t", t=NT)

            with dve.Fori(0, G) as g:
                ch.enter(g, 38)

                def conv(i, wcol, stride, bcol, at):
                    dve.wait_ge(proj_free.sem, proj_free.at(g, i + 1))
                    dve.wait_ge(pad_hist.sem, pad_hist.at(g, i + 1))
                    dve.wait_ge(silu_done.sem, silu_done.at(g, i - 1))
                    x, y = pads[i], cv[i % 2]
                    w = lambda k: par[:, ds(at + (wcol + k * stride), 1)]
                    ch(v.tensor_scalar(y[:, 0:CVW], x[:, 0:CVW], w(0), par[:, ds(at + bcol, 1)], ALU.mult, ALU.add))
                    for k in (1, 2):
                        ch(v.scalar_tensor_tensor(out=y[:, 0:CVW], in0=x[:, k:k + CVW], scalar=w(k), in1=y[:, 0:CVW],
                                                  op0=ALU.mult, op1=ALU.add))
                    if i < 4:
                        ch.tell(v.scalar_tensor_tensor(out=y[:, 0:CVW], in0=x[:, 3:3 + CVW], scalar=w(3), in1=y[:, 0:CVW],
                                                       op0=ALU.mult, op1=ALU.add), conv_done, i + 1)
                    else:
                        ch(v.scalar_tensor_tensor(out=u[:, 0:NP], in0=x[:, 3:3 + NP], scalar=w(3), in1=y[:, 0:NP],
                                                  op0=ALU.mult, op1=ALU.add))
                        xs_ = x[:, SMP:PAD].rearrange("p (b r) -> p b r", r=7)[:, :, 3:7]
                        ch.tell(v.scalar_tensor_tensor(out=samples(u[:, NP:T]), in0=xs_, scalar=w(3), in1=new_tokens(y),
                                                       op0=ALU.mult, op1=ALU.add), conv_done, i + 1)

                def tokens(c):
                    n = TOK[c][1]
                    dve.wait_ge(T_ready.sem, T_ready.at(g, c + 1))
                    ch(v.tensor_tensor(xdt[0:n, c, :].rearrange("p (h e) -> p h e", h=4), bT[0:n, 0:256].rearrange("p (h e) -> p h e", h=4),
                                       TM[0:n, 0, c, ds(g * 4, 4)].unsqueeze(2).to_broadcast([n, 4, 64]), ALU.mult))
                    ch.tell(v.tensor_copy(btok[0:n, c, :], bT[0:n, 256:384]), T_free, c + 1)

                def diff(c):
                    n = TOK[c][1]
                    t = tw[:, c, :] if c < 2 else tws[:]
                    dve.wait_ge(CU_ready.sem, CU_ready.at(g, c + 1))
                    ch.tell(v.tensor_tensor(t.rearrange("p (h q) -> p h q", h=4), bCU[0:n, 0:4 * n].rearrange("p (h q) -> p h q", h=4),
                                            TM[0:n, 1, c, ds(g * 4, 4)].unsqueeze(2).to_broadcast([n, 4, n]), ALU.subtract), CU_free, c + 1)

                def weights(c):
                    t0, n = TOK[c]
                    t = tw[:, c, :] if c < 2 else tws[:]
                    dve.wait_ge(decay_ready.sem, decay_ready.at(g, c + 1))
                    dve.wait_ge(CB_ready.sem, CB_ready.at(g, 1))
                    t4 = t.rearrange("p (h q) -> p h q", h=4)
                    ch.tell(v.tensor_tensor(t4, t4, bCB[0:n, t0:t0 + n].unsqueeze(1).to_broadcast([n, 4, n]), ALU.mult), W_ready, c + 1)

                conv(0, C_SW, 32, C_SB, 2 * g)
                conv(1, C_SW, 32, C_SB, 2 * g + 1)
                conv(2, C_SW, 32, C_SB, g + 16)
                conv(3, C_SW, 32, C_SB, g + 24)
                conv(4, C_LW, 8, C_LB, g)
                tokens(0)
                diff(0)
                dve.wait_ge(lru_act.sem, lru_act.at(g, 1))
                ch(v.tensor_tensor(rr[:], aS[:], aS[:], ALU.mult))
                ch.tell(v.scalar_tensor_tensor(out=TT[:], in0=rr[:], scalar=1.0, in1=TT[:], op0=ALU.add, op1=ALU.mult), m2_ready, 1)
                weights(0)
                tokens(1)
                diff(1)
                tokens(2)
                diff(2)
                weights(1)
                weights(2)
                dve.wait_ge(Y_ready.sem, Y_ready.at(g, 2))
                for j in range(2):
                    ins = v.scalar_tensor_tensor(out=yb[:, ds(2 * g + j, 1), :].rearrange("p o t -> p (o t)"), in0=xbc[j][:],
                                                 scalar=EX[:, ds(2 * g + j, 1), 160:161].rearrange("p o t -> p (o t)"),
                                                 in1=bY[j][:, 0:T], op0=ALU.mult, op1=ALU.add)
                    ch(ins) if j == 0 else ch.tell(ins, Y_free, 2)
                dve.wait_ge(YO_ready.sem, YO_ready.at(g, 1))
                ch.tell(v.tensor_tensor(yot, bYO[:, 0:320].rearrange("p (j t) -> p j t", j=2), EX[:, ds(2 * g, 2), 0:160], ALU.mult), YO_free, 1)
                ch(v.tensor_tensor(yb[:, ds(2 * g, 2), P:T], yb[:, ds(2 * g, 2), P:T], yot, ALU.add))
                dve.wait_ge(proj_free.sem, proj_free.at(g, 7))
                ch.tell(v.tensor_tensor(yb[:, ds(2 * g, 2), :], yb[:, ds(2 * g, 2), :], zs[:], ALU.mult), y_done, 1)
                dve.wait_ge(CU_ready.sem, CU_ready.at(g, 4))
                dve.wait_ge(state_out, g * 48 + 1)
                for j in range(2):
                    ch(v.tensor_scalar(fin[:, j, :], bCU[:, 256 * j:256 * j + P],
                                       EX[:, ds(2 * g + j, 1), 127:128].rearrange("p o t -> p (o t)"), None, ALU.mult))
                    ins = v.tensor_tensor(fin[:, j, :], fin[:, j, :], bCU[:, 256 * j + P:256 * j + 2 * P], ALU.add)
                    ch(ins) if j == 0 else ch.tell(ins, CU_free, 4)
                for k in range(4):
                    j, hf = k // 2, k % 2
                    dve.wait_ge(CU_ready.sem, CU_ready.at(g, 5 + k))
                    dve.wait_ge(sdec_ready.sem, sdec_ready.at(g, j + 1))
                    t = Snew[:, j, 4 * hf:4 * hf + 4, :].rearrange("p b n -> p (b n)")
                    ch.tell(v.tensor_tensor(t, t, bCU[:, :], ALU.add), CU_free, 5 + k)
                dve.wait_ge(CB_free.sem, CB_free.at(g, 1))
                ch(v.reciprocal(zs[:, 0, :], zs[:, 0, :]))
                for j in range(2):
                    t = yb[:, ds(2 * g + j, 1), :].rearrange("p o t -> p (o t)")
                    ch(v.scalar_tensor_tensor(out=t, in0=t, scalar=par[:, ds(2 * g + (C_NG + j), 1)], in1=zs[:, 0, :],
                                              op0=ALU.mult, op1=ALU.mult))
                dve.wait_ge(m_ready.sem, m_ready.at(g, 1))
                ch(v.memset(TT[:, 0:1], 1.0))
                ch(v.tensor_tensor(ii[:], ii[:], u[:], ALU.mult))
                ch(v.tensor_tensor(ii[:], ii[:], TT[:], ALU.mult))
                h0 = h0T[:, :, ds(g, 1)].rearrange("p b o -> p (b o)")
                ch(v.tensor_tensor(rr[:, 0:NB], aS[:, NP:T:NT], h0, ALU.mult))
                ch(v.tensor_tensor(ii[:, NP:T:NT], ii[:, NP:T:NT], rr[:, 0:NB], ALU.add))
                ch(v.memset(aS[:, 0:1], 0.0))
                ch(v.memset(aS[:, NP:T:NT], 0.0))
                ch(v.tensor_tensor_scan(rr[:], aS[:], ii[:], 0.0, ALU.mult, ALU.add))
                ch(v.tensor_copy(hfin[:, 0:1, ds(g, 1)].rearrange("p b o -> p (b o)"), rr[:, NP - 1:NP]))
                ch(v.tensor_copy(hfin[:, 1:9, ds(g, 1)].rearrange("p b o -> p (b o)"), rr[:, NP + NT - 1:T:NT]))
                dve.wait_ge(gelu_ready.sem, gelu_ready.at(g, 1))
                ch.tell(v.tensor_tensor(ya[:, ds(g, 1), :].rearrange("p o t -> p (o t)"), rr[:], gl[:], ALU.mult), lru_tail, 1)
            ch.leave(G)

            dve.wait_ge(gates_ready, 1)
            dve.sem_inc(br_done.sem, 2)
            with dve.Fori(0, 4) as i:
                ch.enter(i, 4)
                for jj in range(2):
                    dve.wait_ge(used[3 * jj + 2], i + (G + 1))
                    ch(v.tensor_tensor(u[:], BR[jj][0][:, 0:T], ga[:, ds(2 * i + jj, 1), :].rearrange("p o t -> p (o t)"), ALU.mult))
                    ch(v.tensor_tensor(ii[:], BR[jj][1][:, 0:T], gb[:, ds(2 * i + jj, 1), :].rearrange("p o t -> p (o t)"), ALU.mult))
                    ch.tell(v.tensor_tensor(mg[:, ds(2 * i + jj, 1), :].rearrange("p o t -> p (o t)"), u[:], ii[:], ALU.add), br_done, jj + 1)
            ch.leave(4)
            for j in range(8):
                dve.wait_ge(used[6 + j % 4], G + 1 + j // 4)
                ch.step(v.tensor_tensor(xT[:, j, :], xT[:, j, :], R4[j % 4][:, 0:T], ALU.add), dve_mid, f"x2_{j}")
            dve.wait_ge(act_mid.sem, act_mid.at("frs"))
            norm(hT, xT, C_GFFN, rs, dve_mid, "hf")
            dve.wait_ge(act_mid.sem, act_mid.at("ers"))
            norm(eT, eT, C_GPLE, rs2, dve_mid, "eN")
            ch(v.memset(r_lg, 0.0))
            dve.wait_ge(pe_mid.sem, pe_mid.at("route"))
            ch(v.tensor_copy(r_lg[:, 0:2, :].rearrange("p c n -> p (c n)"), bY[0][:, 0:40]))
            ch(v.tensor_copy(r_lg[0:NS, 2, :], bY[0][0:NS, 40:60]))
            bc = lambda t, n: t.unsqueeze(2).to_broadcast([P, 3, n])
            tie = cst[:, K_TIE:K_TIE + 4].unsqueeze(1).to_broadcast([P, 3, 4])

            def first_max(oh, x, m):
                ch(v.tensor_reduce(m, x, AX.X, ALU.max))
                ch(v.tensor_tensor(oh, x, bc(m, 4), ALU.is_equal))
                ch(v.tensor_tensor(oh, oh, tie, ALU.mult))
                ch(v.tensor_reduce(r_m2, oh, AX.X, ALU.max))
                ch(v.tensor_tensor(oh, oh, bc(r_m2, 4), ALU.is_equal))

            first_max(r_goh, r_lg[:, :, 0:4], r_m)
            ch.step(v.tensor_tensor(r_gs, r_lg[:, :, 0:4], bc(r_m, 4), ALU.subtract), dve_mid, "gsub")
            e4 = r_lg[:, :, 4:20].rearrange("p c (g j) -> p c g j", g=4)
            ch(v.tensor_tensor(r_pr, e4, r_goh.unsqueeze(3).to_broadcast([P, 3, 4, 4]), ALU.mult))
            ch(v.tensor_reduce(r_es, r_pr.rearrange("p c g j -> p c j g"), AX.X, ALU.add))
            ch(v.tensor_reduce(r_m, r_es, AX.X, ALU.max))
            ch.step(v.tensor_tensor(r_es, r_es, bc(r_m, 4), ALU.subtract), dve_mid, "esub")
            dve.wait_ge(act_mid.sem, act_mid.at("gexp"))
            ch(v.tensor_reduce(r_gw, r_gs, AX.X, ALU.add))
            dve.wait_ge(act_mid.sem, act_mid.at("eexp"))
            first_max(r_o1, r_es, r_m)
            ch(v.scalar_tensor_tensor(out=r_e2, in0=r_o1, scalar=-2.0, in1=r_es, op0=ALU.mult, op1=ALU.add))
            first_max(r_o2, r_e2, r_m)
            ch(v.tensor_tensor(r_o1, r_o1, r_o2, ALU.add))
            ch(v.tensor_tensor(r_o1, r_o1, r_es, ALU.mult))
            ch(v.tensor_reduce(r_m, r_o1, AX.X, ALU.add))
            ch(v.tensor_tensor(r_m, r_m, r_gw, ALU.mult))
            ch(v.reciprocal(r_m, r_m))
            ch(v.tensor_tensor(r_o1, r_o1, bc(r_m, 4), ALU.mult))
            ch.step(v.tensor_tensor(r_pr, r_goh.unsqueeze(3).to_broadcast([P, 3, 4, 4]), r_o1.unsqueeze(2).to_broadcast([P, 3, 4, 4]), ALU.mult),
                    dve_mid, "comb")
            dve.wait_ge(pe_mid.sem, pe_mid.at("combT"))
            ch.step(v.tensor_copy(combT, bY[1][0:NE, 0:T]), dve_mid, "combT")
            ch(v.memset(acc[:], 0.0))
            for e in range(1, NE, 2):
                dve.wait_ge(pe_mid.sem, pe_mid.at(f"cbc{e}"))
                ch.step(v.tensor_copy(cbc[:, e, :], R4[e % 4][:, 0:T]), dve_mid, f"cbc{e}")
            dve.wait_ge(act_mid.sem, act_mid.at("cbc14"))
            dve.sem_inc(act_ready.sem, 2)
            dve.sem_inc(dn_done.sem, 4)
            with dve.Fori(0, NE) as e:
                ch.enter(e, 4)
                for f in range(FC):
                    dve.wait_ge(silu_e.sem, silu_e.at(e, f + 1))
                    dve.wait_ge(used[4 + f], e + (base_use[4 + f] + 1))
                    ch(v.tensor_tensor(sgu, sg[f % 2], UP[f % 2][1][:, 0:T], ALU.mult))
                    ch.tell(v.tensor_tensor(actT[:, f, :], sgu, cbc[:, ds(e, 1), :].rearrange("p o t -> p (o t)"), ALU.mult), act_ready, f + 1)
                for j in range(8):
                    if j % 2 == 0:
                        dve.wait_ge(dn_ready.sem, dn_ready.at(e, j // 2 + 1))
                    else:
                        dve.wait_ge(used[8 + j // 2], e + (base_use[8 + j // 2] + 1))
                    ch.tell(v.tensor_tensor(acc[:, j, :], acc[:, j, :], R4[j % 4][:, 0:T], ALU.add), dn_done, j + 1)
            ch.leave(NE)
            for j in range(8):
                ch.step(v.tensor_tensor(xT[:, j, :], xT[:, j, :], acc[:, j, :], ALU.add), dve_end, f"x3_{j}")
            dve.wait_ge(act_end.sem, act_end.at("grs"))
            norm(hT, xT, C_GPG, rs, dve_end, "hg")
            for j in range(8):
                dve.wait_ge(act_end.sem, act_end.at(f"sig{j}"))
                ch(v.tensor_tensor(sgu, sg[j % 2], eT[:, j, :], ALU.mult))
                ch.step(v.tensor_tensor(xT[:, j, :], xT[:, j, :], sgu, ALU.add), dve_end, f"x4_{j}")
            dve.wait_ge(act_end.sem, act_end.at("yrs"))
            norm(hT, xT, C_GFIN, rs, dve_end, "hy")
            for i in range(6):
                c, hf = i // 2, i % 2
                n = TOK[c][1]
                dve.wait_ge(pe_end.sem, pe_end.at(f"out{i}"))
                ch.step(v.tensor_copy(yrow[0:n, c, 512 * hf:512 * hf + 512], bank[EB[i]][0:n, :]), dve_end, f"out{i}")

        @block.tensor
        def _(pe):
            mm, tr = nc.tensor.matmul, nc.tensor.transpose
            pe.wait_ge(d_cst, 32)
            pe.wait_ge(d_par, 16 * 13)
            for t, n in enumerate((P, P, 24)):
                ins = tr(bCB[:, t * P:t * P + n], prow[0:n, t, :], ident[0:n, 0:n])
            ins.then_inc(pe_pro.sem, 1)
            pe.wait_ge(d_x, 32)
            for k in range(KC):
                if k == 7:
                    pe.wait_ge(act_pro.sem, act_pro.at("sq0"))
                for c, (t0, n) in enumerate(TOK):
                    ins = tr(bank[XB[k]][:, t0:t0 + n], xrow[0:n, c, k * P:(k + 1) * P], ident[0:n, 0:n])
                ins.then_inc(pe_pro.sem, 1)
            pe.wait_ge(d_row, 48)
            pe.wait_ge(act_pro.sem, act_pro.at("sq2"))
            for t in range(4):
                tr(bank[1][:, t * P:(t + 1) * P], srow[:, t, :], ident)
            for t in range(2):
                tr(bank[2][:, t * P:(t + 1) * P], srow[:, 4 + t, :], ident)
            for t in range(2):
                tr(bank[2][:, 256 + 96 * t:352 + 96 * t], lrow[0:96, t, :], ident[0:96, 0:96])
            tr(bank[2][:, 448:512], hrow[0:64], ident[0:64, 0:64]).then_inc(pe_pro.sem, 1)

            def rms(b, src, steps, names):
                for k in range(KC):
                    if names:
                        pe.wait_ge(names[0].sem, names[0].at(f"{names[1]}{k}"))
                    ins = mm(b[:, 0:T], ones, src[:, k, :], start=(k == 0), stop=(k == KC - 1))
                ins.then_inc(steps.sem, 1)

            pe.wait_ge(dve_pro.sem, dve_pro.at("par"))
            rms(bCB, sq, pe_pro, (act_pro, "sq"))
            pe.wait_ge(d_wdt, 16)
            pe.wait_ge(dve_pro.sem, dve_pro.at("hT"))
            for k in range(KC):
                ins = mm(bank[4][0:H, 0:T], wdt[:, k, :], hT[:, k, :], start=(k == 0), stop=(k == KC - 1))
            ins.then_inc(pe_pro.sem, 1)
            pe.wait_ge(dve_pro.sem, dve_pro.at("aT"))
            for c, (t0, n) in enumerate(TOK):
                ins = tr(bank[5][0:n, c * H:(c + 1) * H], aT[:, t0:t0 + n], ident[0:H, 0:H])
            ins.then_inc(pe_pro.sem, 1)
            pe.wait_ge(dve_pro.sem, dve_pro.at("atok"))
            for c, (t0, n) in enumerate(TOK):
                m = tri if c < 2 else cst[0:NS, K_TRIS:K_TRIS + NS]
                ins = mm(bank[6][0:H, t0:t0 + n], atok[0:n, c, :], m, start=True, stop=True)
            ins.then_inc(pe_pro.sem, 1)
            pe.wait_ge(act_pro.sem, act_pro.at("dte"))
            for i, src in enumerate((sp[0][0:H, 0:T], cumT[:], dteT)):
                for c, (t0, n) in enumerate(TOK):
                    ins = tr(bank[7][0:n, (3 * i + c) * H:(3 * i + c + 1) * H], src[:, t0:t0 + n], ident[0:H, 0:H])
            ins.then_inc(pe_pro.sem, 1)
            for i in range(6):
                n = min(3, 16 - 3 * i)
                for j in range(n):
                    jj = 3 * i + j
                    ins = mm(bank[EB[i]][:, 161 * j:161 * j + 161], sel[0:H, jj * P:(jj + 1) * P], exr, start=True, stop=True)
                ins.then_inc(pe_pro.sem, 1)
            pe.wait_ge(dve_pro.sem, dve_pro.at("ex5"))
            pe.sem_inc(YO_ready.sem, 1)

            with pe.Fori(0, G) as g:
                def proj(i):
                    pe.wait_ge(landed[i], g * 16 + 16)
                    pe.wait_ge(proj_free.sem, proj_free.at(g, i - 1))
                    for k in range(KC):
                        ins = mm(bP[i % 2][:, 0:T], wb[:, i, k, :], hT[:, k, :], start=(k == 0), stop=(k == KC - 1))
                    ins.then_inc(used[i], 1)

                def token_major(c):
                    t0, n = TOK[c]
                    pe.wait_ge(T_free.sem, T_free.at(g, c))
                    for i in range(3):
                        ins = tr(bT[0:n, i * P:(i + 1) * P], xbc[i][:, t0:t0 + n], ident)
                    ins.then_inc(T_ready.sem, 1)

                def cum_rows(c):
                    t0, n = TOK[c]
                    pe.wait_ge(CU_free.sem, CU_free.at(g, c))
                    mm(bCU[:, 0:4 * n].rearrange("p (h q) -> p h q", h=4), cst[0:H, K_ONE:K_ONE + P], Dg[:, :, t0:t0 + n],
                       start=True, stop=True).then_inc(CU_ready.sem, 1)

                def y_diag(c):
                    t0, n = TOK[c]
                    pe.wait_ge(W_ready.sem, W_ready.at(g, c + 1))
                    w = (tw[:, c, :] if c < 2 else tws[:]).rearrange("p (h q) -> p h q", h=4)
                    for j in range(2):
                        for h in range(2):
                            ins = mm(bY[j][64 * h:64 * h + 64, t0:t0 + n], xdt[0:n, c, (2 * j + h) * 64:(2 * j + h + 1) * 64],
                                     w[:, 2 * j + h, :], start=True, stop=True)
                    return ins

                def state_T(j, hf):
                    k = 5 + 2 * j + hf
                    if j == 0 and hf == 0:
                        pe.wait_ge(sin_landed, g * 32 + 32)
                    pe.wait_ge(T_free.sem, T_free.at(g, k - 1))
                    for b in range(4):
                        ins = tr(bT[:, b * P:(b + 1) * P], Sin[:, j, 4 * hf + b, :], ident)
                    ins.then_inc(T_ready.sem, 1)

                def y_state(j):
                    pe.wait_ge(T_free.sem, T_free.at(g, 6 + 2 * j))
                    for b in range(NB):
                        ins = mm(bYO[:, j * 160 + P + NT * b:j * 160 + P + NT * b + NT], sT[:, b, :],
                                 xbc[3][:, NP + NT * b:NP + NT * b + NT], start=True, stop=True)
                    return ins

                for i in range(7):
                    proj(i)
                pe.wait_ge(gate_landed, g * 32 + 32)
                pe.wait_ge(conv_done.sem, conv_done.at(g, 5))
                pe.wait_ge(Y_free.sem, Y_free.at(g, 0))
                mm(bY[0][:, 0:T], wg[:, 0, :], u[:], start=True, stop=True)
                mm(bY[1][:, 0:T], wg[:, 1, :], u[:], start=True, stop=True).then_inc(Y_ready.sem, 1)
                pe.wait_ge(silu_done.sem, silu_done.at(g, 4))
                pe.wait_ge(CB_free.sem, CB_free.at(g, 0))
                for c, (t0, n) in enumerate(TOK):
                    ins = mm(bCB[0:n, t0:t0 + n], xbc[2][:, t0:t0 + n], xbc[3][:, t0:t0 + n], start=True, stop=True)
                ins.then_inc(CB_ready.sem, 1)
                token_major(0)
                pe.wait_ge(dg_ready.sem, dg_ready.at(g, 1))
                cum_rows(0)
                proj(7)
                token_major(1)
                cum_rows(1)
                token_major(2)
                cum_rows(2)
                proj(8)
                pe.wait_ge(xdte_ready.sem, xdte_ready.at(g, 1))
                pe.wait_ge(T_free.sem, T_free.at(g, 3))
                mm(bT[:, 0:256], btok[:, 0, :], xdte[:, 0, :], start=True, stop=True).then_inc(T_ready.sem, 1)
                pe.wait_ge(Y_free.sem, Y_free.at(g, 1))
                y_diag(0)
                state_T(0, 0)
                y_diag(1)
                state_T(0, 1)
                proj(9)
                pe.wait_ge(YO_free.sem, YO_free.at(g, 0))
                for j in range(2):
                    mm(bYO[:, 160 * j:160 * j + P], sprev[:, j * P:(j + 1) * P], xbc[3][:, P:2 * P], start=True, stop=True)
                y_diag(2).then_inc(Y_ready.sem, 1)
                y_state(0)
                state_T(1, 0)
                state_T(1, 1)
                y_state(1).then_inc(YO_ready.sem, 1)
                pe.wait_ge(xdte_ready.sem, xdte_ready.at(g, 3))
                pe.wait_ge(CU_free.sem, CU_free.at(g, 3))
                for j in range(2):
                    for c in range(QC):
                        ins = mm(bCU[:, 256 * j + P * c:256 * j + P * (c + 1)], xdte[:, c, j * P:(j + 1) * P], btok[:, c, :],
                                 start=True, stop=True)
                ins.then_inc(CU_ready.sem, 1)
                pe.wait_ge(bm_ready.sem, bm_ready.at(g, 1))
                for k in range(4):
                    j, hf = k // 2, k % 2
                    pe.wait_ge(CU_free.sem, CU_free.at(g, 4 + k))
                    mm(bCU[:, :], xdte[0:NS, 2, j * P:(j + 1) * P], Bm[:, 4 * hf:4 * hf + 4, :].rearrange("p b n -> p (b n)"),
                       start=True, stop=True).then_inc(CU_ready.sem, 1)
                pe.wait_ge(sq_ready.sem, sq_ready.at(g, 1))
                for j in range(2):
                    ins = mm(bCB[:, 0:T], ones, tw[:, j, 0:T], start=(j == 0), stop=(j == 1))
                ins.then_inc(CB_ready.sem, 1)

            pe.wait_ge(lru_tail.sem, lru_tail.at(G - 1, 1))
            with pe.Fori(0, 4) as i:
                for jj in range(2):
                    o = 3 * jj
                    pe.wait_ge(br_done.sem, br_done.at(i, jj - 1))
                    pe.wait_ge(landed[o], i * 16 + 16 * (G + 1))
                    for k in range(KC):
                        ins = mm(BR[jj][0][:, 0:T], wb[:, o, k, :], ya[:, k, :], start=(k == 0), stop=(k == KC - 1))
                    ins.then_inc(used[o], 1)
                    for hf in range(2):
                        pe.wait_ge(landed[o + 1 + hf], i * 16 + 16 * (G + 1))
                        for k in range(KC):
                            ins = mm(BR[jj][1][:, 0:T], wb[:, o + 1 + hf, k, :], yb[:, 8 * hf + k, :],
                                     start=(k == 0 and hf == 0), stop=(k == KC - 1 and hf == 1))
                        ins.then_inc(used[o + 1 + hf], 1)
            pe.wait_ge(br_done.sem, br_done.at(3, 2))
            for j in range(8):
                s = 6 + j % 4
                pe.wait_ge(landed[s], 16 * (G + 1 + j // 4))
                if j >= 4:
                    pe.wait_ge(dve_mid.sem, dve_mid.at(f"x2_{j - 4}"))
                for k in range(KC):
                    ins = mm(R4[j % 4][:, 0:T], wb[:, s, k, :], mg[:, k, :], start=(k == 0), stop=(k == KC - 1))
                ins.then_inc(used[s], 1)
            pe.wait_ge(stashed.sem, stashed.at(G - 1, 5))
            pe.wait_ge(dve_mid.sem, dve_mid.at("x2_6"))
            fS = stS[:].rearrange("p r c -> p (r c)")
            fL = stL[:].rearrange("p r c -> p (r c)")
            fH = hfin[:].rearrange("p r c -> p (r c)")
            tr(bT[0:96, 0:P], fS[:, 0:96], ident)
            for t in range(6):
                b, o = (bT, P * (1 + t)) if t < 3 else (bCB, P * (t - 3))
                tr(b[:, o:o + P], fS[:, 96 + P * t:96 + P * (t + 1)], ident)
            tr(bCB[0:24, 384:512], fL[:, 0:24], ident)
            tr(bCU[0:96, 0:P], fL[:, 24:120], ident)
            tr(bCU[0:96, P:2 * P], fL[:, 120:216], ident)
            tr(bCU[0:72, 256:384], fH, ident).then_inc(pe_mid.sem, 1)
            pe.wait_ge(d_plr, 48)
            for k in range(2):
                for c, (t0, n) in enumerate(TOK):
                    ins = tr(bY[k][:, t0:t0 + n], plr[0:n, c, k * P:(k + 1) * P], ident[0:n, 0:n])
            ins.then_inc(pe_mid.sem, 1)
            rms(bP[0], sq, pe_mid, (act_mid, "sqf"))
            pe.wait_ge(act_mid.sem, act_mid.at("pT"))
            pe.wait_ge(act_mid.sem, act_mid.at("st"))
            pe.wait_ge(dve_mid.sem, dve_mid.at("x2_7"))
            for j in range(8):
                s = 10 + j // 4
                if j % 4 == 0:
                    pe.wait_ge(landed[s], 16)
                if j >= 4:
                    pe.wait_ge(act_mid.sem, act_mid.at(f"e{j - 4}"))
                w = wb[:, s].rearrange("p a b -> p (a b)").rearrange("p (k c) -> p k c", k=2)
                for k in range(2):
                    ins = mm(R4[j % 4][:, 0:T], w[:, k, (j % 4) * P:(j % 4 + 1) * P], pT[:, k, :], start=(k == 0), stop=(k == 1))
                ins.then_inc(pe_mid.sem, 1)
            rms(bP[1], ga, pe_mid, (act_mid, "e"))
            pe.wait_ge(d_wr, 64)
            pe.wait_ge(dve_mid.sem, dve_mid.at("hf"))
            for c, (t0, n) in enumerate(TOK):
                for k in range(KC):
                    mm(bY[0][0:n, 20 * c:20 * c + 20], hT[:, k, t0:t0 + n], wr[:, k, :], start=(k == 0), stop=False)
                ins = mm(bY[0][0:n, 20 * c:20 * c + 20], cst[0:1, K_ONE:K_ONE + n], rb[:], start=False, stop=True)
            ins.then_inc(pe_mid.sem, 1)
            pe.wait_ge(dve_mid.sem, dve_mid.at("comb"))
            for c, (t0, n) in enumerate(TOK):
                ins = tr(bY[1][0:NE, t0:t0 + n], r_pr[0:n, c, :, :].rearrange("p g j -> p (g j)"), ident[0:n, 0:n])
            ins.then_inc(pe_mid.sem, 1)
            pe.wait_ge(dve_mid.sem, dve_mid.at("combT"))
            pe.wait_ge(act_mid.sem, act_mid.at("ers"))
            for e in range(NE):
                if e >= 4:
                    o = act_mid if e % 2 == 0 else dve_mid
                    pe.wait_ge(o.sem, o.at(f"cbc{e - 4}"))
                mm(R4[e % 4][:, 0:T], cst[0:NE, K_ID + e:K_ID + e + 1].to_broadcast([NE, P]), combT, start=True, stop=True).then_inc(pe_mid.sem, 1)
            pe.wait_ge(act_mid.sem, act_mid.at("cbc14"))
            pe.wait_ge(dve_mid.sem, dve_mid.at("cbc15"))
            with pe.Fori(0, NE) as e:
                for f in range(FC):
                    pe.wait_ge(act_ready.sem, act_ready.at(e, f - 1))
                    for s, b in ((f, UP[f % 2][0]), (FC + f, UP[f % 2][1])):
                        pe.wait_ge(landed[s], e * 16 + 16 * (base_land[s] + 1))
                        for k in range(KC):
                            ins = mm(b[:, 0:T], wb[:, s, k, :], hT[:, k, :], start=(k == 0), stop=(k == KC - 1))
                        ins.then_inc(used[s], 1)
                for half in range(2):
                    pe.wait_ge(act_ready.sem, act_ready.at(e, 3))
                    for j in range(4 * half, 4 * half + 4):
                        pe.wait_ge(dn_done.sem, dn_done.at(e, j - 3))
                        if j % 2 == 0:
                            pe.wait_ge(landed[8 + j // 2], e * 16 + 16 * (base_land[8 + j // 2] + 1))
                        w = wb[:, 8 + j // 2].rearrange("p a b -> p (a b)").rearrange("p (k c) -> p k c", k=FC)
                        for k in range(3):
                            mm(R4[j % 4][:, 0:T], w[:, k, (j % 2) * P:(j % 2 + 1) * P], actT[:, k, :], start=(k == 0), stop=False)
                    pe.wait_ge(act_ready.sem, act_ready.at(e, 4))
                    for j in range(4 * half, 4 * half + 4):
                        w = wb[:, 8 + j // 2].rearrange("p a b -> p (a b)").rearrange("p (k c) -> p k c", k=FC)
                        ins = mm(R4[j % 4][:, 0:T], w[:, 3, (j % 2) * P:(j % 2 + 1) * P], actT[:, 3, :], start=False, stop=True)
                        ins.then_inc(dn_ready.sem if j % 2 == 0 else used[8 + j // 2], 1)
            rms(bP[0], sq, pe_end, (act_end, "sg"))
            pe.wait_ge(dve_end.sem, dve_end.at("hg"))
            for j in range(8):
                pe.wait_ge(landed[j], 16 * end_use[j])
                if j >= 4:
                    pe.wait_ge(act_end.sem, act_end.at(f"sig{j - 4}"))
                for k in range(KC):
                    ins = mm(R4[j % 4][:, 0:T], wb[:, j, k, :], hT[:, k, :], start=(k == 0), stop=(k == KC - 1))
                ins.then_inc(used[j], 1)
            rms(bP[1], sq, pe_end, (act_end, "sy"))
            pe.wait_ge(dve_end.sem, dve_end.at("hy"))
            for i in range(6):
                c, hf = i // 2, i % 2
                t0, n = TOK[c]
                for k in range(4):
                    ins = tr(bank[EB[i]][0:n, k * P:(k + 1) * P], hT[:, 4 * hf + k, t0:t0 + n], ident)
                ins.then_inc(pe_end.sem, 1)


_INS = ["x_prompt", "x_sample", "state_lru_h", "state_lru_conv", "state_ssd", "state_ssd_conv", "p_prompt", "p_sample",
        "g_mix", "w_in", "lru_conv_w", "lru_conv_b", "lru_wa", "lru_ba", "lru_wx", "lru_bx", "lru_lambda",
        "ssd_conv_w", "ssd_conv_b", "ssd_dt_bias", "ssd_A_log", "ssd_D", "ssd_norm_g",
        "w_br_lru", "w_br_ssd", "w_out", "g_ffn", "w_router_g", "b_router_g", "w_router_e", "b_router_e",
        "w1", "w3", "w2", "w_ple_proj", "g_ple", "g_ple_gate", "w_ple_gate", "g_final"]
_OUTS = [("y_prompt", (1, NP, D)), ("y_sample", (NB, NT, D)), ("new_lru_h_p", (1, 1, D)), ("new_lru_conv_p", (1, 1, 3, D)),
         ("new_ssd_p", (1, 1, H, 64, P)), ("new_ssd_conv_p", (1, 1, 3, 4096)), ("new_lru_h_s", (1, NB, D)),
         ("new_lru_conv_s", (1, NB, 3, D)), ("new_ssd_s", (1, NB, H, 64, P)), ("new_ssd_conv_s", (1, NB, 3, 4096))]


def kernel(**inputs):
    import numpy as _np
    import concourse.bacc as _bacc
    from concourse import mybir as _mybir
    from concourse.bass_utils import run_bass_kernel_spmd as _run

    nc = _bacc.Bacc("TRN2", target_bir_lowering=False, num_devices=1)
    arrays, aps = {}, {}
    for name in _INS + ["constants"]:
        x = constants() if name == "constants" else _np.ascontiguousarray(inputs[name])
        arrays[f"in_{name}"] = x
        aps[name] = nc.dram_tensor(f"in_{name}", x.shape, _mybir.dt.from_np(x.dtype), kind="ExternalInput").ap()
    for name, shape in _OUTS:
        aps[name] = nc.dram_tensor(f"out_{name}", shape, _mybir.dt.float32, kind="ExternalOutput").ap()
    build(nc, aps)
    r = _run(nc, [arrays], core_ids=[0])
    return tuple(r.results[0][f"out_{name}"] for name, _ in _OUTS)
```

```python
from contextlib import ExitStack

import numpy as np

import concourse.bass as bass
from concourse import mybir

F32 = mybir.dt.float32
F32R = mybir.dt.float32r
I32 = mybir.dt.int32
ALU = mybir.AluOpType
ACT = mybir.ActivationFunctionType
AX = mybir.AxisListType
ds = bass.ds

P = 128
D = 1024
KC = D // P
NP = 256
NB, NT = 8, 4
NS = NB * NT
T = NP + NS
QC = 2
TOK = [(0, P), (P, P), (NP, NS)]
G = 8
H = 32
PAD = 3 + NP + NB * (3 + NT)
SMP = 3 + NP
CVW = PAD - 3
EPS = 1e-6
NE, NEG, EPG, FF = 16, 4, 4, 512
FC = FF // P
S = 64
XSTEPS = (2 * T - 1) // S
CPE = -(-T // S)
NBLK = 12
R = 4
LOD = 608

O_LRU, O_LGATE, O_Z, O_XS = 0, 1024, 2048, 4096
O_B, O_C, O_DT, O_GA, O_GB = 6144, 7168, 8192, 8224, 9248
IN_COLS = 10272

C_SW, C_SB, C_LW, C_NG, C_GMIX, C_GFFN, C_GPLE, C_GPG, C_GFIN, C_LB, C_BA, C_BX, C_LAM, C_END = (
    0, 128, 160, 192, 208, 216, 224, 232, 240, 248, 256, 264, 272, 280)

K_ID, K_TRI, K_NEG, K_TRIS, K_NEGS, K_BM, K_TIE, K_ONE = 0, 128, 256, 384, 416, 448, 456, 460
K_IOTA = 588
K_E64, K_D64, K_ROW, K_THR = K_IOTA + S, K_IOTA + S + 1, K_IOTA + S + 2, K_IOTA + S + 3
K_II = K_THR + CPE - 1
K_END = K_II + S


def constants():
    c = np.zeros((P, K_END), np.float32)
    s, q = np.arange(P)[:, None], np.arange(P)[None, :]
    c[:, K_ID:K_ID + P] = s == q
    c[:, K_TRI:K_TRI + P] = s <= q
    c[:, K_NEG:K_NEG + P] = np.where(s <= q, 0.0, -1e30)
    same = (s[:NS] // NT == q[:, :NS] // NT) & (s[:NS] <= q[:, :NS])
    c[:NS, K_TRIS:K_TRIS + NS] = same
    c[:NS, K_NEGS:K_NEGS + NS] = np.where(same, 0.0, -1e30)
    c[:NS, K_BM:K_BM + NB] = s[:NS] // NT == np.arange(NB)[None, :]
    c[:, K_TIE:K_TIE + 4] = 4.0 - np.arange(4)[None, :]
    c[:, K_ONE:K_ONE + P] = 1.0
    c[:, K_IOTA:K_IOTA + S] = np.arange(S)
    c[:, K_E64] = S * np.arange(P) - 1
    c[:, K_D64] = (NE - 1) * S - S * np.arange(P)
    c[:, K_ROW] = np.arange(P) % S
    c[:, K_THR:K_II] = S * np.arange(1, CPE)
    c[:, K_II:K_END] = s % S == np.arange(S)[None, :]
    return c


class Signal:

    def __init__(self, sem, per=0, credit=0):
        self.sem, self.per, self.credit = sem, per, credit

    def at(self, g, k):
        return g * self.per + (k + self.credit)


class Chain:

    def __init__(self, eng, sem):
        self.eng, self.sem, self.base, self.k, self.g, self.per = eng, sem, 0, 0, 0, 0

    def enter(self, g, per):
        self.base += self.k
        self.g, self.per, self.k = g, per, 0

    def leave(self, steps):
        assert self.k == self.per, (self.k, self.per)
        self.base += steps * self.per
        self.g, self.per, self.k = 0, 0, 0

    def __call__(self, ins):
        self.k += 1
        ins.then_inc(self.sem, 1)
        self.eng.wait_ge(self.sem, self.g * self.per + (self.base + self.k))

    def tell(self, ins, sig, k):
        ins.then_inc(sig.sem, 1)
        self.eng.wait_ge(sig.sem, sig.at(self.g, k))

    def step(self, ins, steps, name):
        ins.then_inc(steps.sem, 1)
        self.eng.wait_ge(steps.sem, steps.at(name))


class Steps:

    def __init__(self, sem, names):
        self.sem, self.names = sem, list(names)

    def at(self, name):
        return self.names.index(name) + 1


def build(nc, a):
    with ExitStack() as ctx:
        def sb(name, shape):
            return ctx.enter_context(nc.sbuf_tensor(name, shape, F32))

        def sem(name):
            return ctx.enter_context(nc.semaphore(name))

        def sig(name, per=0, credit=0):
            return Signal(sem(name), per, credit)

        bank = [ctx.enter_context(nc.psum_tensor(f"bank{i}", [P, 512], F32)) for i in range(8)]
        bP, bT, bCB, bCU, bY, bYO = bank[0:2], bank[2], bank[3], bank[4], bank[5:7], bank[7]

        NSLOT = 12
        mixer, moe = ExitStack(), ExitStack()

        def sbm(name, shape):
            return mixer.enter_context(nc.sbuf_tensor(name, shape, F32))

        def sbe(name, shape, dt=F32):
            return moe.enter_context(nc.sbuf_tensor(name, shape, dt))

        wb = sb("wb", [P, NSLOT, KC, P])
        wr = sb("wr", [P, KC, 20])
        cst = sb("cst", [P, K_END])
        par = sb("par", [P, C_END])
        xT = sb("xT", [P, KC, T])
        hT = sb("hT", [P, KC, T])
        ya = sb("ya", [P, KC, T])
        ga = sb("ga", [P, KC, T])
        gb = sb("gb", [P, KC, T])
        yb = sb("yb", [P, 16, T])
        stS = sb("stS", [P, 27, 32])
        stL = sb("stL", [P, 27, 8])
        hfin = sb("hfin", [P, 9, 8])
        rb = sb("rb", [1, 20])
        u = sb("u", [P, T])
        rr = sb("rr", [P, T])
        ii = sb("ii", [P, T])
        TT = sb("TT", [P, T])
        aS = sb("aS", [P, T])
        gl = sb("gl", [P, T])
        kc2 = sb("kc2", [P, 2, 8])
        steps = ctx.enter_context(nc.sbuf_tensor("steps", [1, NE + XSTEPS + 1], I32))
        arena = sbm("arena", [P, 7616])
        cstS = sbm("cstS", [P, 24, 32])
        cstL = sbm("cstL", [P, 24, 8])
        h0T = sbm("h0T", [P, NB, KC])
        wdt = sbm("wdt", [P, KC, H])
        wg = sbm("wg", [P, 2, P])
        ex = sbm("ex", [P, 2, 160])
        Dt = sbm("Dt", [P, 16])
        TM = sbm("TM", [P, 3, 3, H])
        cumT = sbm("cumT", [H, T])
        pads = [sbm(f"pad{i}", [P, PAD]) for i in range(5)]
        cv = [sbm(f"cv{i}", [P, PAD]) for i in range(2)]
        xbc = [sbm(f"xbc{i}", [P, T]) for i in range(4)]
        zs = sbm("zs", [P, 2, T])
        xdt = sbm("xdt", [P, 3, 256])
        xdte = sbm("xdte", [P, 3, 256])
        btok = sbm("btok", [P, 3, P])
        tw = sbm("tw", [P, 2, 512])
        tws = sbm("tws", [NS, 4 * NS])
        sprev = sbm("sprev", [P, 256])
        fin = sbm("fin", [P, 2, P])
        mixer.close()
        htok_hi = sbe("htok_hi", [P, 3, D], F32R)
        htok_lo = sbe("htok_lo", [P, 3, D], F32R)
        whi = [sbe(f"whi{i}", [P, D], F32R) for i in range(R)]
        wlo = [sbe(f"wlo{i}", [P, D], F32R) for i in range(R)]
        pick = sbe("pick", [P, 3, S], F32R)
        back = sbe("back", [P, T], F32R)
        x_hl = sbe("x_hl", [P, KC, 2, S], F32R)
        a_hl = sbe("a_hl", [P, FC, 2, S], F32R)
        y_hi = sbe("y_hi", [P, D], F32R)
        y_lo = sbe("y_lo", [P, D], F32R)
        AB = sbe("AB", [P, 2, 3])
        wAB = sbe("wAB", [P, 2, 3])
        rowid = sbe("rowid", [P, 1])
        ws = sbe("ws", [P, 1])
        wsn = sbe("wsn", [P, 1])
        rM = sbe("rM", [P, 3, 48])
        rG = sbe("rG", [P, 3, NE])
        rX = sbe("rX", [NE, 16])
        moe.close()
        ident = cst[:, K_ID:K_ID + P]
        tri = cst[:, K_TRI:K_TRI + P]
        ones = cst[:, K_ONE:K_ONE + P]
        sq = yb[:, 0:KC, :]

        def wflat(s_):
            return wb[:, s_].rearrange("p a b -> p (a b)")

        Sin = arena[:, 0:2048].rearrange("p (j b n) -> p j b n", j=2, b=NB)
        Snew = arena[:, 2048:4096].rearrange("p (j b n) -> p j b n", j=2, b=NB)
        sT = arena[:, 4096:5120].rearrange("p (b n) -> p b n", b=NB)
        Bm = arena[0:NS, 5120:6144].rearrange("p (b n) -> p b n", b=NB)
        Dg = arena[0:H, 6144:7296].rearrange("p (h t) -> p h t", h=4)
        yot = arena[:, 7296:7616].rearrange("p (j t) -> p j t", j=2)
        xrow = arena[:, 0:3072].rearrange("p (c n) -> p c n", c=3)
        prow = arena[:, 3072:3456].rearrange("p (c n) -> p c n", c=3)
        srow = arena[:, 3456:4224].rearrange("p (c n) -> p c n", c=6)
        lrow = arena[:, 4224:4480].rearrange("p (c n) -> p c n", c=2)
        hrow = arena[:, 4480:4608]
        sp = [arena[:, 4608 + 296 * i:4904 + 296 * i] for i in range(5)]
        aT = arena[0:H, 6249:6537]
        dteT = arena[0:H, 6537:6825]
        atok = arena[:, 6825:6921].rearrange("p (c h) -> p c h", c=3)
        hc = arena[0:H, 6921:6924]
        Acol = arena[0:H, 6924:6925]
        ybf = yb[:, :, :].rearrange("p a b -> p (a b)")
        res = ga[:].rearrange("p a b -> p (a b)")
        orow = res[:, 0:1280].rearrange("p (c n) -> p c n", c=10)
        lrowo = res[:, 1280:1408]
        plr = ybf[:, 2304:3072].rearrange("p (c n) -> p c n", c=3)
        pT = ybf[:, 3072:3648].rearrange("p (k t) -> p k t", k=2)
        rt = ybf[:, 3648:4148]
        rT, rC, rO = (ga[0:NE, 5 + i, :] for i in range(3))
        sg, sgu = [TT[:], aS[:]], ii[:]
        rs, rs2 = u[:], rr[:]
        ABrow = ybf[:, 0:576].rearrange("p (i t) -> p i t", i=2)
        backt = ybf[:, 576:864]
        eA, eB, eW = (ybf[:, 864 + 192 * i:1056 + 192 * i].rearrange("p (c s) -> p c s", c=3) for i in range(3))
        sgq, aq = (ybf[:, 1440 + 256 * i:1696 + 256 * i] for i in range(2))
        hTf = hT[:].rearrange("p a b -> p (a b)")
        xs, Gs = hTf[:, 0:1024], hTf[:, 1024:2048]
        yrow = yb[:, :, :].rearrange("p a b -> p (a b)")[:, 0:3072].rearrange("p (c n) -> p c n", c=3)
        acc = ya
        eT = gb
        mg = hT

        rsP = rr
        XB = [0, 1, 2, 4, 5, 6, 7, 0]
        EB = [0, 1, 2, 4, 5, 6]
        R4 = [bT, bCB, bCU, bYO]
        bX, bG1, bG3, bGT = bank[0], bank[1], bank[4], bank[7]
        BR = UP = [(bP[0], bP[1]), (bY[0], bY[1])]
        base_use = [G + 4] * 6 + [G + 2] * 4 + [0] * 2
        base_land = [G + 4] * 6 + [G + 2] * 4 + [1] * 2

        def rv(o, n, pat=None, **kw):
            w = rt[:, o:o + n]
            return w.rearrange(pat, **kw) if pat else w
        r_lg = rv(0, 60, "p (c n) -> p c n", c=3)
        r_goh, r_gs, r_es, r_o1, r_o2, r_e2 = (rv(64 + 12 * i, 12, "p (c n) -> p c n", c=3) for i in range(6))
        r_m, r_m2, r_gw = (rv(140 + 3 * i, 3) for i in range(3))
        r_pr = rv(152, 48, "p (c g j) -> p c g j", c=3, g=4)
        r_v1, r_v2 = rv(200, 3), rv(203, 3)

        landed = [sem(f"landed{s}") for s in range(NSLOT)]
        used = [sem(f"used{s}") for s in range(NSLOT)]
        nload = [0] * NSLOT
        ncons = [0] * NSLOT

        d_cst, d_x, d_par, d_row, d_small, d_wdt, d_wr = (
            sem("d_cst"), sem("d_x"), sem("d_par"), sem("d_row"), sem("d_small"), sem("d_wdt"), sem("d_wr"))
        d_plr = sem("d_plr")
        d_out = sem("d_out")
        gate_landed = sem("gate_landed")
        sin_landed, state_out = sem("sin_landed"), sem("state_out")
        pe_pro = Steps(sem("pe_pro"), [f"x{k}" for k in range(KC)] + ["par", "hist", "rms", "dt", "atok", "cum", "tm"])
        act_pro = Steps(sem("act_pro"), [f"sq{k}" for k in range(KC)] + ["rs", "A", "z", "ln", "dte"])
        dve_pro = Steps(sem("dve_pro"), [f"x{k}" for k in range(KC)] + ["par", "hist"] + [f"hT{k}" for k in range(KC)]
                        + ["ax", "u", "soft", "aT", "atok", "cum", "dteT", "tm"])
        dve_ch, act_ch, pool_ch = sem("dve_ch"), sem("act_ch"), sem("pool_ch")

        proj_free = sig("proj_free", 10, 2)
        pad_hist = sig("pad_hist", 5)
        conv_done = sig("conv_done", 5, 5)
        stashed = sig("stashed", 5, 5)
        silu_done = sig("silu_done", 4, 4)
        y_done = sig("y_done", 1, 1)
        T_ready, T_free = sig("T_ready", 10), sig("T_free", 10, 1)
        CU_ready, CU_free = sig("CU_ready", 6), sig("CU_free", 6, 1)
        CB_ready, CB_free = sig("CB_ready", 2), sig("CB_free", 1, 1)
        Y_ready, Y_free = sig("Y_ready", 2), sig("Y_free", 2, 1)
        YO_ready, YO_free = sig("YO_ready", 1, 1), sig("YO_free", 1, 1)
        diff_ready = sig("diff_ready", 2)
        dg_ready = sig("dg_ready", 1)
        masked = sig("masked", 3)
        decay_ready = sig("decay_ready", 3)
        W_ready = sig("W_ready", 3)
        xdte_ready = sig("xdte_ready", 3)
        bm_ready = sig("bm_ready", 1)
        sdec_ready = sig("sdec_ready", 2)
        lru_act = sig("lru_act", 1)
        m2_ready = sig("m2_ready", 1)
        m_ready = sig("m_ready", 1)
        gelu_ready = sig("gelu_ready", 1)
        lru_tail = sig("lru_tail", 1, 1)
        sq_ready = sig("sq_ready", 1)
        br_done = sig("br_done", 2, 2)
        gates_ready = sem("gates_ready")
        pe_mid = Steps(sem("pe_mid"), ["st", "pT", "frms"] + [f"e{j}" for j in range(8)]
                       + ["erms", "route"] + [f"ht{i}" for i in range(4)] + ["MT", "ht4", "ht5", "extra", "table", "slots", "rows"])
        act_mid = Steps(sem("act_mid"), [f"sqf{j}" for j in range(8)] + ["st", "pT", "frs"]
                        + [f"e{j}" for j in range(8)] + ["ers", "hi0", "hi1", "gexp", "eexp"] + [f"hi{i}" for i in range(2, 6)])
        dve_mid = Steps(sem("dve_mid"), [f"x2_{j}" for j in range(8)] + [f"hf{k}" for k in range(KC)] + [f"eN{k}" for k in range(KC)] + ["gsub", "esub", "lo0", "lo1", "M"]
                        + [f"lo{i}" for i in range(2, 6)] + ["count", "end", "steps", "slots", "AB", "rows", "pick0"])
        hi_ready, lo_dve, lo_pool = sig("hi_ready", NBLK), sig("lo_dve", NBLK), sig("lo_pool", NBLK)
        hl_free = sig("hl_free", NBLK, R)
        g1_out, g3_out, gt_ready = sig("g1_out", 1), sig("g3_out", 1), sig("gt_ready", 1)
        silu_e, act_ready = sig("silu_e", 1), sig("act_ready", 1)
        cmb_ready, cmb_done = sig("cmb_ready", 8, 1), sig("cmb_done", 8, 2)
        eq_ready = sig("eq_ready", 1)
        pick_ready, back_ready = sig("pick_ready", 1, 1), sig("back_ready", 1, 1)
        xa_gathered, xb_gathered, xt_ready = sig("xa_gathered", 1, 1), sig("xb_gathered", 1, 1), sig("xt_ready", 1, 1)
        xs0_out, xs1_out = sig("xs0_out", 1, 1), sig("xs1_out", 1, 1)
        xhi_ready, x_ready = sig("xhi_ready", 1, 1), sig("x_ready", 1, 1)
        yhi_ready, ylo_ready = sig("yhi_ready", 1), sig("ylo_ready", 1)
        ws_done, wsn_done = sig("ws_done", 1, 1), sig("wsn_done", 1, 1)
        dve_ch2, act_ch2, pool_ch2 = sem("dve_ch2"), sem("act_ch2"), sem("pool_ch2")
        pe_end = Steps(sem("pe_end"), ["grms", "yrms"] + [f"out{i}" for i in range(6)])
        act_end = Steps(sem("act_end"), [f"sg{j}" for j in range(8)] + ["grs"]
                        + [n for j in range(8) for n in (f"sig{j}", f"sy{j}")] + ["yrs"])
        dve_end = Steps(sem("dve_end"), [f"x3_{j}" for j in range(8)] + [f"hg{k}" for k in range(KC)] + [f"x4_{j}" for j in range(8)]
                        + [f"hy{k}" for k in range(KC)] + [f"out{i}" for i in range(6)])

        w_in = a["w_in"][0].rearrange("(k p) c -> p k c", p=P)
        w1 = a["w1"].rearrange("l e (k p) f -> (l e) p k f", p=P)
        w3 = a["w3"].rearrange("l e (k p) f -> (l e) p k f", p=P)
        w2 = a["w2"].rearrange("l e (k p) n -> (l e) p k n", p=P)
        w_lru = a["w_br_lru"][0].rearrange("(k p) c -> p k c", p=P)
        w_ssd = a["w_br_ssd"][0].rearrange("(k p) c -> p k c", p=P)
        w_out = a["w_out"][0].rearrange("(k p) c -> p k c", p=P)
        w_pp = a["w_ple_proj"][0].rearrange("(k p) c -> p k c", p=P)
        w_pg = a["w_ple_gate"][0].rearrange("(k p) c -> p k c", p=P)
        wa = a["lru_wa"][0].rearrange("n c d -> c n d")
        wx = a["lru_wx"][0].rearrange("n c d -> c n d")
        st_in = a["state_ssd"].rearrange("l b h p n -> (l h p) b n")
        st_out = a["new_ssd_s"].rearrange("l b h p n -> (l h p) b n")
        stp_out = a["new_ssd_p"].rearrange("l b h p n -> (l b h p) n")

        BLOCKS = [(O_XS, 256), (O_XS + 128, 256), (O_B, 128), (O_C, 128), (O_LRU, 128),
                  (O_Z, 256), (O_Z + 128, 256), (O_LGATE, 128), (O_GA, 128), (O_GB, 128)]

        iota = cst[:, K_IOTA:K_IOTA + S].unsqueeze(1).to_broadcast([P, 3, S])

        def slot(t, i):
            return t[:, i, :].unsqueeze(2).to_broadcast([P, 3, S])

        def weigh_slots(eng, ch):
            ch(eng.tensor_tensor(pick[:], eA, eB, ALU.add))
            ch(eng.tensor_tensor(eA, eA, slot(wAB, 0), ALU.mult))
            ch(eng.tensor_tensor(eB, eB, slot(wAB, 1), ALU.mult))

        block = ctx.enter_context(nc.Block())

        @block.sync
        def _(sp_):
            eng = nc.sync
            eng.dma_start(xrow[:, 0:2, :], a["x_prompt"][0].rearrange("(c p) d -> p c d", p=P)).then_inc(d_x, 16)
            eng.dma_start(xrow[0:NS, 2, :], a["x_sample"].rearrange("b t d -> (b t) d")).then_inc(d_x, 16)
            rows = {
                0: [("ssd_conv_w", "l k (c x) -> (l k c) x")],
                1: [("ssd_conv_b", "l (c x) -> (l c) x"), ("lru_conv_w", "l k (c x) -> (l k c) x"),
                    ("ssd_norm_g", "l (c x) -> (l c) x"), ("g_mix", "l (c x) -> (l c) x"), ("g_ffn", "l (c x) -> (l c) x"),
                    ("g_ple", "l (c x) -> (l c) x"), ("g_ple_gate", "l (c x) -> (l c) x"), ("g_final", "(c x) -> c x"),
                    ("lru_conv_b", "l (c x) -> (l c) x")],
                2: [("lru_ba", "l (c x) -> (l c) x"), ("lru_bx", "l (c x) -> (l c) x"), ("lru_lambda", "l (c x) -> (l c) x")],
            }
            for t, ps in rows.items():
                r = 0
                for name, pat in ps:
                    src = a[name].rearrange(pat, x=P)
                    n = src.shape[0]
                    eng.dma_start(prow[r:r + n, t, :], src).then_inc(d_par, 16)
                    r += n
            for i, name in enumerate(("ssd_dt_bias", "ssd_A_log", "ssd_D")):
                eng.dma_start(hc[:, i:i + 1], a[name].rearrange("l h -> h l")).then_inc(d_small, 16)
            eng.dma_start(wdt[:], w_in[:, :, O_DT:O_DT + H]).then_inc(d_wdt, 16)

            def load(s, dst, src):
                if nload[s] > 0:
                    sp_.wait_ge(used[s], nload[s])
                eng.dma_start(dst, src).then_inc(landed[s], 16)
                nload[s] += 1

            for s in range(10):
                o, w = BLOCKS[s]
                load(s, wb[:, s], w_in[:, :, o:o + P])
            eng.dma_start(wg[:, 0, :], wa[:, 0, :]).then_inc(gate_landed, 16)
            eng.dma_start(wg[:, 1, :], wx[:, 0, :]).then_inc(gate_landed, 16)
            eng.dma_start(rb[:, 0:4], a["b_router_g"]).then_inc(d_wr, 16)
            eng.dma_start(rb[:, 4:20], a["b_router_e"]).then_inc(d_wr, 16)
            eng.dma_start(wr[:, :, 0:4], a["w_router_g"][0].rearrange("(k p) c -> p k c", p=P)).then_inc(d_wr, 16)
            eng.dma_start(wr[:, :, 4:20], a["w_router_e"][0].rearrange("(k p) c -> p k c", p=P)).then_inc(d_wr, 16)
            sp_.sem_inc(state_out, 1)
            sp_.wait_ge(act_pro.sem, act_pro.at("dte"))
            sp_.wait_ge(dve_pro.sem, dve_pro.at("tm"))
            sp_.wait_ge(pe_pro.sem, pe_pro.at("tm"))
            for j in range(2):
                eng.dma_start(Sin[:, j], st_in[j * P:(j + 1) * P]).then_inc(sin_landed, 16)
            with sp_.Fori(1, G) as g:
                col1, col2, row2 = sp_.snap(g * 128), sp_.snap(g * 256), sp_.snap(g * 256 + P)
                for s in range(10):
                    o, w = BLOCKS[s]
                    col = {128: col1, 256: col2}[w]
                    sp_.wait_ge(used[s], g)
                    if s == 4:
                        sp_.wait_ge(Y_ready.sem, Y_ready.at(g - 1, 1))
                        eng.dma_start(wg[:, 0, :], wa[:, ds(g, 1), :]).then_inc(gate_landed, 16)
                        eng.dma_start(wg[:, 1, :], wx[:, ds(g, 1), :]).then_inc(gate_landed, 16)
                    eng.dma_start(wb[:, s], w_in[:, :, ds(col + o, P)]).then_inc(landed[s], 16)
                sp_.wait_ge(T_free.sem, T_free.at(g - 1, 10))
                for j in range(2):
                    eng.dma_start(Sin[:, j], st_in[ds((col2, row2)[j], P)]).then_inc(sin_landed, 16)
                eng.dma_start(stp_out[ds((g - 1) * 256, 256)].rearrange("(j q) n -> q j n", j=2), fin[:]).then_inc(state_out, 16)
                for j in range(2):
                    eng.dma_start(st_out[ds((g - 1) * 256 + j * P, P)], Snew[:, j]).then_inc(state_out, 16)
            for s in range(10):
                nload[s] = G
            sp_.wait_ge(CU_free.sem, CU_free.at(G - 1, 4))
            eng.dma_start(stp_out[7 * 256:8 * 256].rearrange("(j q) n -> q j n", j=2), fin[:]).then_inc(state_out, 16)
            sp_.wait_ge(CU_free.sem, CU_free.at(G - 1, 6))
            sp_.wait_ge(T_free.sem, T_free.at(G - 1, 10))
            for j in range(2):
                eng.dma_start(st_out[7 * 256 + j * P:7 * 256 + (j + 1) * P], Snew[:, j]).then_inc(state_out, 16)

            def branch(j, o, wait):
                for s, src in ((o, w_lru[:, :, ds(j * P, P)]), (o + 1, w_ssd[:, 0:8, ds(j * P, P)]),
                               (o + 2, w_ssd[:, 8:16, ds(j * P, P)])):
                    sp_.wait_ge(used[s], wait)
                    eng.dma_start(wb[:, s], src).then_inc(landed[s], 16)
            branch(0, 0, G)
            branch(1, 3, G)
            for i in range(4):
                load(6 + i, wb[:, 6 + i], w_out[:, :, i * P:(i + 1) * P])
            with sp_.Fori(1, 4) as i:
                branch(2 * i, 0, G + i)
                branch(2 * i + 1, 3, G + i)
            for s in range(6):
                nload[s] = G + 4
            for i in range(4):
                load(6 + i, wb[:, 6 + i], w_out[:, :, (4 + i) * P:(5 + i) * P])
            sp_.wait_ge(used[2], G + 4)
            sp_.wait_ge(used[5], G + 4)
            for c in range(2):
                eng.dma_start(plr[:, c, :], a["p_prompt"][0, 0, c * P:(c + 1) * P, :]).then_inc(d_plr, 16)
            eng.dma_start(plr[0:NS, 2, :], a["p_sample"][0].rearrange("b t d -> (b t) d")).then_inc(d_plr, 16)
            for i in range(2):
                load(10 + i, wb[:, 10 + i].rearrange("p a b -> p (a b)").rearrange("p (k c) -> p k c", k=2),
                     w_pp[:, :, i * 512:(i + 1) * 512])
            def expert_block(s, e):
                if s < 8:
                    w, b = (w1, w3)[s % 2], s // 2
                    return wflat(s).rearrange("p (k f) -> p k f", k=2), w[e, :, 2 * b:2 * b + 2, :]
                return wflat(s), w2[e, :, s - 8, :]
            for s in range(10):
                load(s, *expert_block(s, 0))
            for f in range(2, 4):
                sp_.wait_ge(pe_mid.sem, pe_mid.at(f"e{4 * f - 5}"))
                eng.dma_start(*expert_block(8 + f, 0)).then_inc(landed[8 + f], 16)
            assert nload[0:10] == [b + 1 for b in base_use[0:10]]
            sp_.wait_ge(dve_mid.sem, dve_mid.at("steps"))
            n_steps = sp_.value_load(steps[0:1, NE + XSTEPS:NE + XSTEPS + 1], min_val=NE, max_val=NE + XSTEPS)
            with sp_.Fori(1, n_steps) as q:
                e = sp_.value_load(steps[0:1, ds(q, 1)], min_val=0, max_val=NE - 1)
                for s in range(NBLK):
                    sp_.wait_ge(lo_dve.sem, lo_dve.at(q, s + 1 - NBLK))
                    sp_.wait_ge(lo_pool.sem, lo_pool.at(q, s + 1 - NBLK))
                    eng.dma_start(*expert_block(s, ds(e, 1))).then_inc(landed[s], 16)
            sp_.wait_ge(lo_dve.sem, lo_dve.at(n_steps, 0))
            sp_.wait_ge(lo_pool.sem, lo_pool.at(n_steps, 0))
            for i in range(8):
                eng.dma_start(wb[:, i], w_pg[:, :, i * P:(i + 1) * P]).then_inc(landed[i], 16)
            sp_.wait_ge(act_mid.sem, act_mid.at("st"))
            eng.dma_start(a["new_ssd_conv_p"].rearrange("l b r (c x) -> (l b r c) x", x=P), orow[0:96, 0, :]).then_inc(d_out, 16)
            eng.dma_start(a["new_ssd_conv_s"].rearrange("l b r (c x) -> (l b r c) x", x=P).rearrange("(t q) x -> q t x", q=P),
                          orow[:, 1:7, :]).then_inc(d_out, 16)
            eng.dma_start(a["new_lru_conv_p"].rearrange("l b r (c x) -> (l b r c) x", x=P), orow[0:24, 7, :]).then_inc(d_out, 16)
            eng.dma_start(a["new_lru_conv_s"].rearrange("l b r (c x) -> (l b r c) x", x=P).rearrange("(t q) x -> q t x", q=96),
                          orow[0:96, 8:10, :]).then_inc(d_out, 16)
            eng.dma_start(a["new_lru_h_p"].rearrange("l b (c x) -> (l b c) x", x=P), lrowo[0:8, :]).then_inc(d_out, 16)
            eng.dma_start(a["new_lru_h_s"].rearrange("l b (c x) -> (l b c) x", x=P), lrowo[8:72, :]).then_inc(d_out, 16)
            sp_.wait_ge(dve_end.sem, dve_end.at("out5"))
            eng.dma_start(a["y_prompt"][0].rearrange("(c p) d -> p c d", p=P), yrow[:, 0:2, :]).then_inc(d_out, 16)
            eng.dma_start(a["y_sample"].rearrange("b t d -> (b t) d"), yrow[0:NS, 2, :]).then_inc(d_out, 16)
            sp_.wait_ge(d_out, 16 * 8)
            sp_.wait_ge(state_out, 16 * 3 * G + 1)

        @block.gpsimd
        def _(pool):
            eng = nc.gpsimd
            ch = Chain(pool, pool_ch)
            pool.sem_inc(stashed.sem, 5)
            pool.wait_ge(dve_pro.sem, dve_pro.at("tm"))
            pool.wait_ge(pe_pro.sem, pe_pro.at("tm"))
            with pool.Fori(0, G) as g:
                ch.enter(g, 5)
                for i, (src, at) in enumerate(((cstS, 2 * g), (cstS, 2 * g + 1), (cstS, g + 16), (cstS, g + 24), (cstL, g))):
                    pool.wait_ge(conv_done.sem, g * 5 + (i + 1))
                    pool.wait_ge(stashed.sem, g * 5 + (i + 1))
                    v = pads[i][:, SMP:PAD].rearrange("p (b r) -> p b r", r=7)[:, :, 0:3]
                    ch.tell(eng.tensor_copy(v, src[:, :, ds(at, 1)].rearrange("p (b r) o -> p b (r o)", r=3)), pad_hist, i + 1)
                pool.wait_ge(YO_ready.sem, YO_ready.at(g, 0))
                ch.tell(eng.tensor_tensor(Dg, cumT[:].unsqueeze(1).to_broadcast([H, 4, T]),
                                          cst[0:H, ds(g * 4, 4)].unsqueeze(2).to_broadcast([H, 4, T]), ALU.mult), dg_ready, 1)
                for i, (dst, at) in enumerate(((stS, 2 * g), (stS, 2 * g + 1), (stS, g + 16), (stS, g + 24), (stL, g))):
                    pool.wait_ge(proj_free.sem, proj_free.at(g, i + 1))
                    ch(eng.tensor_copy(dst[:, 0:3, ds(at, 1)].rearrange("p r o -> p (r o)"), pads[i][:, NP:NP + 3]))
                    v = pads[i][:, SMP:PAD].rearrange("p (b r) -> p b r", r=7)[:, :, 4:7]
                    ch.tell(eng.tensor_copy(dst[:, 3:27, ds(at, 1)].rearrange("p (b r) o -> p b (r o)", r=3), v), stashed, i + 1)
                for c, (t0, n) in enumerate(TOK):
                    if c == 0:
                        pool.wait_ge(CU_free.sem, CU_free.at(g, 1))
                    else:
                        pool.wait_ge(diff_ready.sem, diff_ready.at(g, c))
                    t = tw[:, c, :] if c < 2 else tws[:]
                    m = cst[0:n, K_NEG:K_NEG + P] if c < 2 else cst[0:n, K_NEGS:K_NEGS + NS]
                    t4 = t.rearrange("p (h q) -> p h q", h=4)
                    ch.tell(eng.tensor_tensor(t4, t4, m.unsqueeze(1).to_broadcast([n, 4, n]), ALU.add), masked, c + 1)
                    pool.wait_ge(T_free.sem, T_free.at(g, c + 1))
                    ch.tell(eng.tensor_tensor(xdte[0:n, c, :].rearrange("p (h e) -> p h e", h=4),
                                              xdt[0:n, c, :].rearrange("p (h e) -> p h e", h=4),
                                              TM[0:n, 2, c, ds(g * 4, 4)].unsqueeze(2).to_broadcast([n, 4, 64]), ALU.mult),
                            xdte_ready, c + 1)
                ch.tell(eng.tensor_tensor(Bm, btok[0:NS, 2, :].unsqueeze(1).to_broadcast([NS, NB, P]),
                                          cst[0:NS, K_BM:K_BM + NB].unsqueeze(2).to_broadcast([NS, NB, P]), ALU.mult), bm_ready, 1)
                pool.wait_ge(CU_free.sem, CU_free.at(g, 3))
                for j in range(2):
                    pool.wait_ge(sin_landed, g * 32 + 32)
                    if j == 0:
                        pool.wait_ge(state_out, g * 48 + 1)
                    dec = ex[:, j, P + NT - 1:P + NS:NT]
                    ch.tell(eng.tensor_tensor(Snew[:, j], Sin[:, j], dec.unsqueeze(2).to_broadcast([P, NB, P]), ALU.mult), sdec_ready, j + 1)
            ch.leave(G)

            pool.wait_ge(dve_mid.sem, dve_mid.at("pick0"))
            n_steps = pool.value_load(steps[0:1, NE + XSTEPS:NE + XSTEPS + 1], min_val=NE, max_val=NE + XSTEPS)
            ch2 = Chain(pool, pool_ch2)
            with pool.Fori(0, n_steps) as q:
                ch2.enter(q, 3)

                def small(s):
                    pool.wait_ge(hi_ready.sem, hi_ready.at(q, s + 1))
                    eng.tensor_tensor(wlo[s % R][:, LOD:D], wflat(s)[:, LOD:D], whi[s % R][:, LOD:D].bitcast(F32),
                                      ALU.subtract).then_inc(lo_pool.sem, 1)

                for s in range(4):
                    small(s)
                pool.wait_ge(xb_gathered.sem, xb_gathered.at(q, 0))
                pool.wait_ge(eq_ready.sem, eq_ready.at(q, 1))
                weigh_slots(eng, ch2)
                ch2.tell(eng.tensor_tensor(eW, eA, eB, ALU.add), pick_ready, 1)
                for s in range(4, 8):
                    small(s)
                for s in range(8, NBLK):
                    small(s)
            ch2.leave(0)

        @block.scalar
        def _(act):
            eng = nc.scalar
            ch = Chain(act, act_ch)
            act_f = eng.activation
            q = nc.scalar
            q.dma_start(cst[:], a["constants"]).then_inc(d_cst, 16)
            q.dma_start(srow, a["state_ssd_conv"].rearrange("l b r (c x) -> (l b r c) x", x=P).rearrange("(t q) x -> q t x", q=P)).then_inc(d_row, 16)
            q.dma_start(lrow[0:96], a["state_lru_conv"].rearrange("l b r (c x) -> (l b r c) x", x=P).rearrange("(t q) x -> q t x", q=96)).then_inc(d_row, 16)
            q.dma_start(hrow[0:64], a["state_lru_h"].rearrange("l b (c x) -> (l b c) x", x=P)).then_inc(d_row, 16)
            for k in range(KC):
                act.wait_ge(dve_pro.sem, dve_pro.at(f"x{k}"))
                act_f(sq[:, k, :], xT[:, k, :], ACT.Square).then_inc(act_pro.sem, 1)
            act.wait_ge(pe_pro.sem, pe_pro.at("rms"))
            ch(act_f(rsP[:], bCB[:, 0:T], ACT.Ln, bias=EPS, scale=1.0 / D))
            ch.step(act_f(rsP[:], rsP[:], ACT.Exp, scale=-0.5), act_pro, "rs")
            act.wait_ge(d_small, 48)
            ch.step(act_f(Acol, hc[:, 1:2], ACT.Exp), act_pro, "A")
            act.wait_ge(dve_pro.sem, dve_pro.at("ax"))
            ch.step(act_f(sp[2], sp[1], ACT.Exp, scale=-1.0), act_pro, "z")
            act.wait_ge(dve_pro.sem, dve_pro.at("u"))
            ch.step(act_f(sp[4], sp[3], ACT.Ln), act_pro, "ln")
            act.wait_ge(dve_pro.sem, dve_pro.at("dteT"))
            ch.step(act_f(dteT, dteT, ACT.Exp), act_pro, "dte")

            act.sem_inc(proj_free.sem, 2)
            act.sem_inc(silu_done.sem, 4)
            act.sem_inc(T_free.sem, 1)
            act.sem_inc(CB_free.sem, 1)

            def samples(v):
                return v.rearrange("p (b t) -> p b t", t=NT)

            def new_tokens(v, r0):
                return v[:, SMP:PAD].rearrange("p (b r) -> p b r", r=7)[:, :, r0:r0 + NT]

            with act.Fori(0, G) as g:
                ch.enter(g, 11)

                def evac(i):
                    act.wait_ge(used[i], g + 1)
                    act.wait_ge(conv_done.sem, conv_done.at(g, i + 1 - 5))
                    act.wait_ge(stashed.sem, stashed.at(g, i + 1 - 5))
                    ch(act_f(pads[i][:, 3:SMP], bP[i % 2][:, 0:NP], ACT.Copy))
                    ch.tell(act_f(new_tokens(pads[i], 3), samples(bP[i % 2][:, NP:T]), ACT.Copy), proj_free, i + 1)

                def silu(i):
                    act.wait_ge(conv_done.sem, conv_done.at(g, i + 1))
                    ch(act_f(xbc[i][:, 0:NP], cv[i % 2][:, 0:NP], ACT.Silu))
                    ch.tell(act_f(samples(xbc[i][:, NP:T]), new_tokens(cv[i % 2], 0), ACT.Silu), silu_done, i + 1)

                def decay(c):
                    act.wait_ge(masked.sem, masked.at(g, c + 1))
                    t = tw[:, c, :] if c < 2 else tws[:]
                    ch.tell(act_f(t, t, ACT.Exp), decay_ready, c + 1)

                def raw(i, dst):
                    act.wait_ge(used[i], g + 1)
                    ch.tell(act_f(dst, bP[i % 2][:, 0:T], ACT.Copy), proj_free, i + 1)

                def from_T(k, dst, n):
                    act.wait_ge(T_ready.sem, T_ready.at(g, k))
                    ch.tell(act_f(dst, bT[:, 0:n], ACT.Copy), T_free, k)

                evac(0)
                evac(1)
                act.wait_ge(YO_ready.sem, YO_ready.at(g, 0))
                act.wait_ge(y_done.sem, y_done.at(g, 0))
                silu(0)
                evac(2)
                silu(1)
                evac(3)
                silu(2)
                evac(4)
                silu(3)
                act.wait_ge(lru_tail.sem, lru_tail.at(g, 0))
                for j in range(2):
                    act.wait_ge(used[5 + j], g + 1)
                    ch.tell(act_f(zs[:, j, :], bP[(5 + j) % 2][:, 0:T], ACT.Silu), proj_free, 6 + j)
                act.wait_ge(Y_ready.sem, Y_ready.at(g, 1))
                ch(act_f(rr[:], bY[0][:, 0:T], ACT.Sigmoid, bias=par[:, ds(g + C_BA, 1)]))
                ch.tell(act_f(ii[:], bY[1][:, 0:T], ACT.Sigmoid, bias=par[:, ds(g + C_BX, 1)]), Y_free, 1)
                ch(act_f(TT[:], rr[:], ACT.Tanh, scale=kc2[:, 1, ds(g, 1)]))
                ch.tell(act_f(aS[:], rr[:], ACT.Exp, scale=kc2[:, 0, ds(g, 1)]), lru_act, 1)
                def decay_rows(c):
                    n = TOK[c][1]
                    act.wait_ge(diff_ready.sem, diff_ready.at(g, c))
                    for h in range(2):
                        p = slice(64 * h, 64 * h + 64)
                        ins = act_f(ex[p, :, P * (c - 1):P * (c - 1) + n],
                                    bCU[p, 0:4 * n].rearrange("p (j h q) -> p j h q", j=2, h=2)[:, :, h, :], ACT.Exp)
                    ch.tell(ins, CU_free, c + 1)

                decay(0)
                decay_rows(1)
                decay(1)
                raw(7, gl[:])
                decay_rows(2)
                decay(2)
                act.wait_ge(m2_ready.sem, m2_ready.at(g, 1))
                ch.tell(act_f(TT[:], TT[:], ACT.Sqrt), m_ready, 1)
                raw(8, ga[:, ds(g, 1), :].rearrange("p o t -> p (o t)"))
                from_T(4, sprev[:], 256)
                from_T(5, sT[:, 0:4, :].rearrange("p b n -> p (b n)"), 512)
                from_T(6, sT[:, 4:8, :].rearrange("p b n -> p (b n)"), 512)
                from_T(7, sT[:, 0:4, :].rearrange("p b n -> p (b n)"), 512)
                from_T(8, sT[:, 4:8, :].rearrange("p b n -> p (b n)"), 512)
                raw(9, gb[:, ds(g, 1), :].rearrange("p o t -> p (o t)"))
                act.wait_ge(y_done.sem, y_done.at(g, 1))
                ch.tell(act_f(tw[:, :, 0:T], yb[:, ds(2 * g, 2), :], ACT.Square), sq_ready, 1)
                act.wait_ge(CB_ready.sem, CB_ready.at(g, 2))
                ch.tell(act_f(zs[:, 0, :], bCB[:, 0:T], ACT.Sqrt, bias=EPS, scale=1.0 / 256), CB_free, 1)
                ch.tell(act_f(gl[:], gl[:], ACT.Gelu_apprx_tanh), gelu_ready, 1)
            ch.leave(G)

            ch(act_f(ga[:], ga[:], ACT.Sigmoid))
            act_f(gb[:], gb[:], ACT.Sigmoid).then_inc(gates_ready, 1)
            act.wait_ge(gates_ready, 1)
            for j in range(8):
                act.wait_ge(dve_mid.sem, dve_mid.at(f"x2_{j}"))
                ch.step(act_f(sq[:, j, :], xT[:, j, :], ACT.Square), act_mid, f"sqf{j}")
            act.wait_ge(pe_mid.sem, pe_mid.at("st"))
            act.wait_ge(state_out, 16 * 3 * G + 1)
            ch(act_f(orow[0:96, 0, :], bT[0:96, 0:P], ACT.Copy))
            ch(act_f(orow[:, 1:4, :].rearrange("p c n -> p (c n)"), bT[:, P:512], ACT.Copy))
            ch(act_f(orow[:, 4:7, :].rearrange("p c n -> p (c n)"), bCB[:, 0:384], ACT.Copy))
            ch(act_f(orow[0:24, 7, :], bCB[0:24, 384:512], ACT.Copy))
            ch(act_f(orow[0:96, 8:10, :].rearrange("p c n -> p (c n)"), bCU[0:96, 0:256], ACT.Copy))
            ch.step(act_f(lrowo[0:72], bCU[0:72, 256:384], ACT.Copy), act_mid, "st")
            act.wait_ge(pe_mid.sem, pe_mid.at("pT"))
            ch(act_f(pT[:, 0, :], bY[0][:, 0:T], ACT.Copy))
            ch.step(act_f(pT[:, 1, :], bY[1][:, 0:T], ACT.Copy), act_mid, "pT")
            act.wait_ge(pe_mid.sem, pe_mid.at("frms"))
            ch(act_f(rs, bP[0][:, 0:T], ACT.Ln, bias=EPS, scale=1.0 / D))
            ch.step(act_f(rs, rs, ACT.Exp, scale=-0.5), act_mid, "frs")
            for j in range(8):
                act.wait_ge(pe_mid.sem, pe_mid.at(f"e{j}"))
                ch(act_f(eT[:, j, :], R4[j % 4][:, 0:T], ACT.Copy))
                ch.step(act_f(sq[:, j, :], R4[j % 4][:, 0:T], ACT.Square), act_mid, f"e{j}")
            act.wait_ge(pe_mid.sem, pe_mid.at("erms"))
            ch(act_f(rs2, bP[1][:, 0:T], ACT.Ln, bias=EPS, scale=1.0 / D))
            ch.step(act_f(rs2, rs2, ACT.Exp, scale=-0.5), act_mid, "ers")
            def hi(i):
                c, hf = i // 2, i % 2
                n = TOK[c][1]
                act.wait_ge(pe_mid.sem, pe_mid.at(f"ht{i}"))
                ch.step(act_f(htok_hi[0:n, c, 512 * hf:512 * hf + 512], R4[i % 4][0:n, :], ACT.Copy), act_mid, f"hi{i}")
            hi(0)
            hi(1)
            act.wait_ge(dve_mid.sem, dve_mid.at("gsub"))
            ch.step(act_f(r_gs, r_gs, ACT.Exp), act_mid, "gexp")
            act.wait_ge(dve_mid.sem, dve_mid.at("esub"))
            ch.step(act_f(r_es, r_es, ACT.Exp), act_mid, "eexp")
            for i in range(2, 6):
                hi(i)
            act.wait_ge(dve_mid.sem, dve_mid.at("steps"))
            n_steps = act.value_load(steps[0:1, NE + XSTEPS:NE + XSTEPS + 1], min_val=NE, max_val=NE + XSTEPS)

            def slots_out(q, k, hf):
                act.wait_ge((xa_gathered, xb_gathered)[hf].sem, xa_gathered.at(q, k))
                act_f(xs[0:S, 512 * hf:512 * hf + 512], bY[hf][0:S, :], ACT.Copy).then_inc((xs0_out, xs1_out)[hf].sem, 1)

            def tokens_hi(q, k):
                act.wait_ge(xt_ready.sem, xt_ready.at(q, k))
                act_f(x_hl[:, :, 0, :], bX[:, :].rearrange("p (k s) -> p k s", k=KC), ACT.Copy).then_inc(xhi_ready.sem, 1)

            def results_hi(q):
                act.wait_ge(hl_free.sem, hl_free.at(q, 0))
                act.wait_ge(ws_done.sem, ws_done.at(q, 0))
                act.wait_ge(cmb_ready.sem, cmb_ready.at(q, 0))
                act_f(y_hi[:, 0:512], bY[0][:, :], ACT.Copy, scale=ws[:, 0:1])
                act_f(y_hi[:, 512:1024], bY[1][:, :], ACT.Copy, scale=ws[:, 0:1]).then_inc(yhi_ready.sem, 1)

            slots_out(0, 0, 0)
            slots_out(0, 0, 1)
            tokens_hi(0, 0)
            act.wait_ge(dve_mid.sem, dve_mid.at("pick0"))
            ch(act_f(sgq[:, 0:1], wAB[:, 0, 0:1], ACT.Silu))
            with act.Fori(0, n_steps) as q:
                def large(s):
                    act.wait_ge(landed[s], q * 16 + 16 * (base_land[s] + 1))
                    act.wait_ge(hl_free.sem, hl_free.at(q, s + 1 - R))
                    act_f(whi[s % R][:], wflat(s), ACT.Copy).then_inc(hi_ready.sem, 1)

                large(0)
                large(1)
                results_hi(q)
                for s in range(2, 8):
                    large(s)
                act.wait_ge(hl_free.sem, hl_free.at(q, 7))
                act_f(Gs[:, 0:512], bG1[:, :], ACT.Copy).then_inc(g1_out.sem, 1)
                act.wait_ge(hl_free.sem, hl_free.at(q, 8))
                act_f(Gs[:, 512:1024], bG3[:, :], ACT.Copy).then_inc(g3_out.sem, 1)
                large(8)
                slots_out(q, 1, 0)
                large(9)
                act.wait_ge(gt_ready.sem, gt_ready.at(q, 1))
                act_f(sgq, bGT[:, 0:256], ACT.Silu).then_inc(silu_e.sem, 1)
                slots_out(q, 1, 1)
                large(10)
                tokens_hi(q, 1)
                large(11)
            results_hi(n_steps)
            ch = Chain(act, act_ch2)
            for j in range(8):
                act.wait_ge(dve_end.sem, dve_end.at(f"x3_{j}"))
                ch.step(act_f(sq[:, j, :], xT[:, j, :], ACT.Square), act_end, f"sg{j}")
            act.wait_ge(pe_end.sem, pe_end.at("grms"))
            ch(act_f(rs, bP[0][:, 0:T], ACT.Ln, bias=EPS, scale=1.0 / D))
            ch.step(act_f(rs, rs, ACT.Exp, scale=-0.5), act_end, "grs")
            for j in range(8):
                act.wait_ge(used[j], base_use[j] + 1)
                if j >= 2:
                    act.wait_ge(dve_end.sem, dve_end.at(f"x4_{j - 2}"))
                ch.step(act_f(sg[j % 2], R4[j % 4][:, 0:T], ACT.Sigmoid), act_end, f"sig{j}")
                act.wait_ge(dve_end.sem, dve_end.at(f"x4_{j}"))
                ch.step(act_f(sq[:, j, :], xT[:, j, :], ACT.Square), act_end, f"sy{j}")
            act.wait_ge(pe_end.sem, pe_end.at("yrms"))
            ch(act_f(rs, bP[1][:, 0:T], ACT.Ln, bias=EPS, scale=1.0 / D))
            ch.step(act_f(rs, rs, ACT.Exp, scale=-0.5), act_end, "yrs")

        @block.vector
        def _(dve):
            v = nc.vector
            ch = Chain(dve, dve_ch)
            for k in range(KC):
                dve.wait_ge(pe_pro.sem, pe_pro.at(f"x{k}"))
                v.tensor_copy(xT[:, k, :], bank[XB[k]][:, 0:T]).then_inc(dve_pro.sem, 1)
            dve.wait_ge(pe_pro.sem, pe_pro.at("par"))
            ch.step(v.tensor_copy(par[:], bank[4][:, 0:C_END]), dve_pro, "par")
            for i in range(5):
                ch(v.memset(pads[i][:, 0:3], 0.0))
            ch(v.memset(sp[0], 0.0))
            dve.wait_ge(pe_pro.sem, pe_pro.at("hist"))
            cs = cstS[:].rearrange("p a b -> p (a b)")
            ch(v.tensor_copy(cs[:, 0:512], bank[1][:, :]))
            ch(v.tensor_copy(cs[:, 512:768], bank[2][:, 0:256]))
            ch(v.tensor_copy(cstL[:].rearrange("p a b -> p (a b)"), bank[2][:, 256:448]))
            ch.step(v.tensor_copy(h0T[:].rearrange("p a b -> p (a b)"), bank[2][:, 448:512]), dve_pro, "hist")

            def norm(dst, src, col, r, steps, name):
                for k in range(KC):
                    v.scalar_tensor_tensor(out=dst[:, k, :], in0=src[:, k, :], scalar=par[:, col + k:col + k + 1],
                                           in1=r, op0=ALU.mult, op1=ALU.mult).then_inc(steps.sem, 1)
                assert steps.at(f"{name}{KC - 1}") == steps.at(f"{name}0") + KC - 1

            dve.wait_ge(act_pro.sem, act_pro.at("rs"))
            norm(hT, xT, C_GMIX, rsP[:], dve_pro, "hT")
            dve.wait_ge(pe_pro.sem, pe_pro.at("dt"))
            dve.wait_ge(d_small, 48)
            ch(v.tensor_scalar(sp[0][0:H, 0:T], bank[4][0:H, 0:T], hc[:, 0:1], None, ALU.add))
            ch(v.tensor_scalar(sp[0][:, T:T + 8], par[:, C_LAM:C_LAM + 8], -1.0, None, ALU.mult))
            ch.step(v.scalar_tensor_tensor(out=sp[1], in0=sp[0], scalar=-1.0, in1=sp[0], op0=ALU.mult, op1=ALU.max), dve_pro, "ax")
            dve.wait_ge(act_pro.sem, act_pro.at("z"))
            ch.step(v.tensor_scalar(sp[3], sp[2], 1.0, None, ALU.add), dve_pro, "u")
            dve.wait_ge(act_pro.sem, act_pro.at("ln"))
            ch(v.tensor_scalar(sp[3], sp[3], -1.0, 1e-30, ALU.add, ALU.add))
            ch(v.reciprocal(sp[3], sp[3]))
            ch(v.scalar_tensor_tensor(out=sp[4], in0=sp[4], scalar=1e-30, in1=sp[3], op0=ALU.add, op1=ALU.mult))
            ch(v.tensor_tensor(sp[4], sp[4], sp[2], ALU.mult))
            ch.step(v.scalar_tensor_tensor(out=sp[0], in0=sp[0], scalar=0.0, in1=sp[4], op0=ALU.max, op1=ALU.add), dve_pro, "soft")
            ch(v.tensor_scalar(kc2[:, 0, :], sp[0][:, T:T + 8], -8.0, None, ALU.mult))
            ch(v.tensor_scalar(kc2[:, 1, :], sp[0][:, T:T + 8], 8.0, None, ALU.mult))
            dve.wait_ge(act_pro.sem, act_pro.at("A"))
            ch.step(v.tensor_scalar(aT, sp[0][0:H, 0:T], Acol, -1.0, ALU.mult, ALU.mult), dve_pro, "aT")
            dve.wait_ge(pe_pro.sem, pe_pro.at("atok"))
            ch(v.tensor_copy(Dt[:], bank[5][:, P:P + 16]))
            ch(v.tensor_copy(atok[:, 0:2, :].rearrange("p c h -> p (c h)"), bank[5][:, 0:2 * H]))
            ch.step(v.tensor_copy(atok[0:NS, 2, :], bank[5][0:NS, 2 * H:3 * H]), dve_pro, "atok")
            dve.wait_ge(pe_pro.sem, pe_pro.at("cum"))
            ch.step(v.tensor_copy(cumT[:], bank[6][0:H, 0:T]), dve_pro, "cum")
            for c in range(QC):
                ch(v.tensor_scalar(dteT[:, c * P:(c + 1) * P], cumT[:, c * P:(c + 1) * P], -1.0,
                                   cumT[:, (c + 1) * P - 1:(c + 1) * P], ALU.mult, ALU.add))
            ct = cumT[:, NP:T].rearrange("p (b t) -> p b t", t=NT)
            ch.step(v.tensor_tensor(dteT[:, NP:T].rearrange("p (b t) -> p b t", t=NT), ct[:, :, NT - 1:NT].to_broadcast([H, NB, NT]),
                                    ct, ALU.subtract), dve_pro, "dteT")
            dve.wait_ge(pe_pro.sem, pe_pro.at("tm"))
            tmb = bank[7][:, 0:9 * H].rearrange("p (k c h) -> p k c h", k=3, c=3)
            ch(v.tensor_copy(TM[:, :, 0:2, :].rearrange("p k c h -> p k (c h)"), tmb[:, :, 0:2, :].rearrange("p k c h -> p k (c h)")))
            ch.step(v.tensor_copy(TM[0:NS, :, 2, :], tmb[0:NS, :, 2, :]), dve_pro, "tm")
            dve.sem_inc(conv_done.sem, 5)
            dve.sem_inc(y_done.sem, 1)
            dve.sem_inc(CU_free.sem, 1)
            dve.sem_inc(Y_free.sem, 1)
            dve.sem_inc(YO_free.sem, 1)
            dve.sem_inc(lru_tail.sem, 1)

            def new_tokens(w):
                return w[:, SMP:PAD].rearrange("p (b r) -> p b r", r=7)[:, :, 0:NT]

            def samples(w):
                return w.rearrange("p (b t) -> p b t", t=NT)

            with dve.Fori(0, G) as g:
                ch.enter(g, 38)

                def conv(i, wcol, stride, bcol, at):
                    dve.wait_ge(proj_free.sem, proj_free.at(g, i + 1))
                    dve.wait_ge(pad_hist.sem, pad_hist.at(g, i + 1))
                    dve.wait_ge(silu_done.sem, silu_done.at(g, i - 1))
                    x, y = pads[i], cv[i % 2]
                    w = lambda k: par[:, ds(at + (wcol + k * stride), 1)]
                    ch(v.tensor_scalar(y[:, 0:CVW], x[:, 0:CVW], w(0), par[:, ds(at + bcol, 1)], ALU.mult, ALU.add))
                    for k in (1, 2):
                        ch(v.scalar_tensor_tensor(out=y[:, 0:CVW], in0=x[:, k:k + CVW], scalar=w(k), in1=y[:, 0:CVW],
                                                  op0=ALU.mult, op1=ALU.add))
                    if i < 4:
                        ch.tell(v.scalar_tensor_tensor(out=y[:, 0:CVW], in0=x[:, 3:3 + CVW], scalar=w(3), in1=y[:, 0:CVW],
                                                       op0=ALU.mult, op1=ALU.add), conv_done, i + 1)
                    else:
                        ch(v.scalar_tensor_tensor(out=u[:, 0:NP], in0=x[:, 3:3 + NP], scalar=w(3), in1=y[:, 0:NP],
                                                  op0=ALU.mult, op1=ALU.add))
                        xs_ = x[:, SMP:PAD].rearrange("p (b r) -> p b r", r=7)[:, :, 3:7]
                        ch.tell(v.scalar_tensor_tensor(out=samples(u[:, NP:T]), in0=xs_, scalar=w(3), in1=new_tokens(y),
                                                       op0=ALU.mult, op1=ALU.add), conv_done, i + 1)

                def tokens(c):
                    n = TOK[c][1]
                    dve.wait_ge(T_ready.sem, T_ready.at(g, c + 1))
                    ch(v.tensor_tensor(xdt[0:n, c, :].rearrange("p (h e) -> p h e", h=4), bT[0:n, 0:256].rearrange("p (h e) -> p h e", h=4),
                                       TM[0:n, 0, c, ds(g * 4, 4)].unsqueeze(2).to_broadcast([n, 4, 64]), ALU.mult))
                    ch.tell(v.tensor_copy(btok[0:n, c, :], bT[0:n, 256:384]), T_free, c + 1)

                def diff(c):
                    n = TOK[c][1]
                    t = tw[:, c, :] if c < 2 else tws[:]
                    dve.wait_ge(CU_ready.sem, CU_ready.at(g, c + 1))
                    ins = v.tensor_tensor(t.rearrange("p (h q) -> p h q", h=4), bCU[0:n, 0:4 * n].rearrange("p (h q) -> p h q", h=4),
                                          TM[0:n, 1, c, ds(g * 4, 4)].unsqueeze(2).to_broadcast([n, 4, n]), ALU.subtract)
                    ch.tell(ins, CU_free, 1) if c == 0 else ch.tell(ins, diff_ready, c)

                def weights(c):
                    t0, n = TOK[c]
                    t = tw[:, c, :] if c < 2 else tws[:]
                    dve.wait_ge(decay_ready.sem, decay_ready.at(g, c + 1))
                    dve.wait_ge(CB_ready.sem, CB_ready.at(g, 1))
                    t4 = t.rearrange("p (h q) -> p h q", h=4)
                    ch.tell(v.tensor_tensor(t4, t4, bCB[0:n, t0:t0 + n].unsqueeze(1).to_broadcast([n, 4, n]), ALU.mult), W_ready, c + 1)

                conv(0, C_SW, 32, C_SB, 2 * g)
                conv(1, C_SW, 32, C_SB, 2 * g + 1)
                conv(2, C_SW, 32, C_SB, g + 16)
                conv(3, C_SW, 32, C_SB, g + 24)
                conv(4, C_LW, 8, C_LB, g)
                tokens(0)
                diff(0)
                tokens(1)
                diff(1)
                dve.wait_ge(lru_act.sem, lru_act.at(g, 1))
                ch(v.tensor_tensor(rr[:], aS[:], aS[:], ALU.mult))
                ch.tell(v.scalar_tensor_tensor(out=TT[:], in0=rr[:], scalar=1.0, in1=TT[:], op0=ALU.add, op1=ALU.mult), m2_ready, 1)
                weights(0)
                weights(1)
                tokens(2)
                diff(2)
                weights(2)
                dve.wait_ge(m_ready.sem, m_ready.at(g, 1))
                ch(v.memset(TT[:, 0:1], 1.0))
                ch(v.tensor_tensor(ii[:], ii[:], u[:], ALU.mult))
                ch(v.tensor_tensor(ii[:], ii[:], TT[:], ALU.mult))
                h0 = h0T[:, :, ds(g, 1)].rearrange("p b o -> p (b o)")
                ch(v.tensor_tensor(rr[:, 0:NB], aS[:, NP:T:NT], h0, ALU.mult))
                ch(v.tensor_tensor(ii[:, NP:T:NT], ii[:, NP:T:NT], rr[:, 0:NB], ALU.add))
                ch(v.memset(aS[:, 0:1], 0.0))
                ch(v.memset(aS[:, NP:T:NT], 0.0))
                ch(v.tensor_tensor_scan(rr[:], aS[:], ii[:], 0.0, ALU.mult, ALU.add))
                dve.wait_ge(Y_ready.sem, Y_ready.at(g, 2))
                for j in range(2):
                    ins = v.scalar_tensor_tensor(out=yb[:, ds(2 * g + j, 1), :].rearrange("p o t -> p (o t)"), in0=xbc[j][:],
                                                 scalar=Dt[:, ds(2 * g + j, 1)],
                                                 in1=bY[j][:, 0:T], op0=ALU.mult, op1=ALU.add)
                    ch(ins) if j == 0 else ch.tell(ins, Y_free, 2)
                dve.wait_ge(CU_ready.sem, CU_ready.at(g, 4))
                dve.wait_ge(state_out, g * 48 + 1)
                for j in range(2):
                    ch(v.tensor_scalar(fin[:, j, :], bCU[:, 256 * j:256 * j + P],
                                       ex[:, j, P - 1:P], None, ALU.mult))
                    ins = v.tensor_tensor(fin[:, j, :], fin[:, j, :], bCU[:, 256 * j + P:256 * j + 2 * P], ALU.add)
                    ch(ins) if j == 0 else ch.tell(ins, CU_free, 4)

                def new_states(k):
                    j, hf = k // 2, k % 2
                    b, ready, free, n = ((bCU, CU_ready, CU_free, 5 + k // 2), (bT, T_ready, T_free, 9 + k // 2))[k % 2]
                    dve.wait_ge(ready.sem, ready.at(g, n))
                    dve.wait_ge(sdec_ready.sem, sdec_ready.at(g, j + 1))
                    t = Snew[:, j, 4 * hf:4 * hf + 4, :].rearrange("p b n -> p (b n)")
                    ch.tell(v.tensor_tensor(t, t, b[:, :], ALU.add), free, n)

                new_states(0)
                dve.wait_ge(YO_ready.sem, YO_ready.at(g, 1))
                ch.tell(v.tensor_tensor(yot, bYO[:, 0:320].rearrange("p (j t) -> p j t", j=2), ex[:], ALU.mult), YO_free, 1)
                ch(v.tensor_tensor(yb[:, ds(2 * g, 2), P:T], yb[:, ds(2 * g, 2), P:T], yot, ALU.add))
                dve.wait_ge(proj_free.sem, proj_free.at(g, 7))
                ch.tell(v.tensor_tensor(yb[:, ds(2 * g, 2), :], yb[:, ds(2 * g, 2), :], zs[:], ALU.mult), y_done, 1)
                new_states(1)
                new_states(2)
                new_states(3)
                ch(v.tensor_copy(hfin[:, 0:1, ds(g, 1)].rearrange("p b o -> p (b o)"), rr[:, NP - 1:NP]))
                ch(v.tensor_copy(hfin[:, 1:9, ds(g, 1)].rearrange("p b o -> p (b o)"), rr[:, NP + NT - 1:T:NT]))
                dve.wait_ge(CB_free.sem, CB_free.at(g, 1))
                ch(v.reciprocal(zs[:, 0, :], zs[:, 0, :]))
                for j in range(2):
                    t = yb[:, ds(2 * g + j, 1), :].rearrange("p o t -> p (o t)")
                    ch(v.scalar_tensor_tensor(out=t, in0=t, scalar=par[:, ds(2 * g + (C_NG + j), 1)], in1=zs[:, 0, :],
                                              op0=ALU.mult, op1=ALU.mult))
                dve.wait_ge(gelu_ready.sem, gelu_ready.at(g, 1))
                ch.tell(v.tensor_tensor(ya[:, ds(g, 1), :].rearrange("p o t -> p (o t)"), rr[:], gl[:], ALU.mult), lru_tail, 1)
            ch.leave(G)

            dve.wait_ge(gates_ready, 1)
            dve.sem_inc(br_done.sem, 2)
            with dve.Fori(0, 4) as i:
                ch.enter(i, 4)
                for jj in range(2):
                    dve.wait_ge(used[3 * jj + 2], i + (G + 1))
                    ch(v.tensor_tensor(u[:], BR[jj][0][:, 0:T], ga[:, ds(2 * i + jj, 1), :].rearrange("p o t -> p (o t)"), ALU.mult))
                    ch(v.tensor_tensor(ii[:], BR[jj][1][:, 0:T], gb[:, ds(2 * i + jj, 1), :].rearrange("p o t -> p (o t)"), ALU.mult))
                    ch.tell(v.tensor_tensor(mg[:, ds(2 * i + jj, 1), :].rearrange("p o t -> p (o t)"), u[:], ii[:], ALU.add), br_done, jj + 1)
            ch.leave(4)
            for j in range(8):
                dve.wait_ge(used[6 + j % 4], G + 1 + j // 4)
                ch.step(v.tensor_tensor(xT[:, j, :], xT[:, j, :], R4[j % 4][:, 0:T], ALU.add), dve_mid, f"x2_{j}")
            dve.wait_ge(act_mid.sem, act_mid.at("frs"))
            norm(hT, xT, C_GFFN, rs, dve_mid, "hf")
            dve.wait_ge(act_mid.sem, act_mid.at("ers"))
            norm(eT, eT, C_GPLE, rs2, dve_mid, "eN")
            def lo(i):
                c, hf = i // 2, i % 2
                n = TOK[c][1]
                dve.wait_ge(act_mid.sem, act_mid.at(f"hi{i}"))
                ch.step(v.tensor_tensor(htok_lo[0:n, c, 512 * hf:512 * hf + 512], R4[i % 4][0:n, :],
                                        htok_hi[0:n, c, 512 * hf:512 * hf + 512].bitcast(F32), ALU.subtract), dve_mid, f"lo{i}")

            ch(v.memset(r_lg, 0.0))
            dve.wait_ge(pe_mid.sem, pe_mid.at("route"))
            ch(v.tensor_copy(r_lg[:, 0:2, :].rearrange("p c n -> p (c n)"), bY[0][:, 0:40]))
            ch(v.tensor_copy(r_lg[0:NS, 2, :], bY[0][0:NS, 40:60]))
            bc = lambda t, n: t.unsqueeze(2).to_broadcast([P, 3, n])
            tie = cst[:, K_TIE:K_TIE + 4].unsqueeze(1).to_broadcast([P, 3, 4])

            def first_max(oh, x, m):
                ch(v.tensor_reduce(m, x, AX.X, ALU.max))
                ch(v.tensor_tensor(oh, x, bc(m, 4), ALU.is_equal))
                ch(v.tensor_tensor(oh, oh, tie, ALU.mult))
                ch(v.tensor_reduce(r_m2, oh, AX.X, ALU.max))
                ch(v.tensor_tensor(oh, oh, bc(r_m2, 4), ALU.is_equal))

            first_max(r_goh, r_lg[:, :, 0:4], r_m)
            ch.step(v.tensor_tensor(r_gs, r_lg[:, :, 0:4], bc(r_m, 4), ALU.subtract), dve_mid, "gsub")
            e4 = r_lg[:, :, 4:20].rearrange("p c (g j) -> p c g j", g=4)
            ch(v.tensor_tensor(r_pr, e4, r_goh.unsqueeze(3).to_broadcast([P, 3, 4, 4]), ALU.mult))
            ch(v.tensor_reduce(r_es, r_pr.rearrange("p c g j -> p c j g"), AX.X, ALU.add))
            ch(v.tensor_reduce(r_m, r_es, AX.X, ALU.max))
            ch.step(v.tensor_tensor(r_es, r_es, bc(r_m, 4), ALU.subtract), dve_mid, "esub")
            lo(0)
            lo(1)
            dve.wait_ge(act_mid.sem, act_mid.at("gexp"))
            ch(v.tensor_reduce(r_gw, r_gs, AX.X, ALU.add))
            dve.wait_ge(act_mid.sem, act_mid.at("eexp"))
            first_max(r_o1, r_es, r_m)
            ch(v.scalar_tensor_tensor(out=r_e2, in0=r_o1, scalar=-2.0, in1=r_es, op0=ALU.mult, op1=ALU.add))
            first_max(r_o2, r_e2, r_m)
            ch(v.tensor_tensor(r_e2, r_o1, r_es, ALU.mult))
            ch(v.tensor_reduce(r_v1, r_e2, AX.X, ALU.add))
            ch(v.tensor_tensor(r_e2, r_o2, r_es, ALU.mult))
            ch(v.tensor_reduce(r_v2, r_e2, AX.X, ALU.add))
            ch(v.tensor_tensor(r_m, r_v1, r_v2, ALU.add))
            ch(v.tensor_tensor(r_m, r_m, r_gw, ALU.mult))
            ch(v.reciprocal(r_m, r_m))
            ch(v.tensor_tensor(wAB[:, 0, :], r_v1, r_m, ALU.mult))
            ch(v.tensor_tensor(wAB[:, 1, :], r_v2, r_m, ALU.mult))
            oh = lambda i: rM[:, :, 16 * i:16 * i + 16]
            oh4 = lambda i: oh(i).rearrange("p c (g j) -> p c g j", g=4)
            for i, o in enumerate((r_o1, r_o2)):
                ch(v.tensor_tensor(oh4(i), r_goh.unsqueeze(3).to_broadcast([P, 3, 4, 4]), o.unsqueeze(2).to_broadcast([P, 3, 4, 4]), ALU.mult))
            ch.step(v.tensor_tensor(oh(2), oh(0), oh(1), ALU.add), dve_mid, "M")
            for i in range(2, 6):
                lo(i)
            dve.wait_ge(pe_mid.sem, pe_mid.at("MT"))
            ch(v.tensor_copy(rT, bY[1][0:NE, 0:T]))
            ch(v.tensor_tensor_scan(rC, rT, rT, 0.0, ALU.add, ALU.max))
            cnt, xs_, xe, xb = rC[:, T - 1:T], rX[:, 8:9], rX[:, 9:10], rX[:, 10:11]
            ch(v.tensor_scalar(rX[:, 0:CPE - 1], cst[0:NE, K_THR:K_II], cnt, None, ALU.is_lt))
            ch.step(v.tensor_reduce(xs_, rX[:, 0:CPE - 1], AX.X, ALU.add), dve_mid, "count")
            dve.wait_ge(pe_mid.sem, pe_mid.at("extra"))
            ch(v.tensor_copy(xe, bY[1][0:NE, T:T + 1]))
            ch(v.tensor_scalar(rX[:, 0:XSTEPS], cst[0:NE, K_IOTA:K_IOTA + XSTEPS], xe, None, ALU.is_ge))
            ch.step(v.tensor_tensor(xb, xe, xs_, ALU.subtract), dve_mid, "end")
            dve.wait_ge(pe_mid.sem, pe_mid.at("table"))
            ch(v.tensor_copy(steps[:, 0:NE], cst[0:1, K_IOTA:K_IOTA + NE]))
            ch(v.tensor_scalar(steps[:, NE:NE + XSTEPS], bY[1][0:1, 320:320 + XSTEPS], float(NE - 1), None, ALU.min))
            ch.step(v.tensor_scalar(steps[:, NE + XSTEPS:NE + XSTEPS + 1], bY[1][0:1, 330:331], float(NE), None, ALU.add), dve_mid, "steps")
            ch(v.tensor_scalar(xb, xb, float(S), cst[0:NE, K_D64:K_D64 + 1], ALU.mult, ALU.add))
            ch(v.tensor_scalar(rO, rC, float(S), xb, ALU.is_gt, ALU.mult))
            ch.step(v.scalar_tensor_tensor(out=rC, in0=rC, scalar=cst[0:NE, K_E64:K_E64 + 1], in1=rO, op0=ALU.add, op1=ALU.add),
                    dve_mid, "slots")
            ch(v.memset(rG[:], 0.0))
            dve.wait_ge(pe_mid.sem, pe_mid.at("slots"))
            ch(v.tensor_copy(rG[:, 0:2, :].rearrange("p c n -> p (c n)"), bY[0][:, 0:32]))
            ch(v.tensor_copy(rG[0:NS, 2, :], bY[0][0:NS, 32:48]))
            for i in range(2):
                ch(v.tensor_tensor(oh(i), oh(i), rG[:], ALU.mult))
                ins = v.tensor_reduce(AB[:, i, :], oh(i), AX.X, ALU.add)
                ch(ins) if i == 0 else ch.step(ins, dve_mid, "AB")
            dve.wait_ge(pe_mid.sem, pe_mid.at("rows"))
            ch(v.tensor_copy(ABrow[:, 0, :], bP[0][:, 0:T]))
            ch.step(v.tensor_copy(ABrow[:, 1, :], bP[1][:, 0:T]), dve_mid, "rows")
            def match_slots(last):
                ch(v.tensor_tensor(eA, iota, slot(AB, 0), ALU.is_equal))
                ch(v.tensor_tensor(eB, iota, slot(AB, 1), ALU.is_equal))
                last(v.tensor_scalar(AB[:], AB[:], -float(S), None, ALU.add))

            match_slots(ch)
            weigh_slots(v, ch)
            ch.step(v.tensor_tensor(eW, eA, eB, ALU.add), dve_mid, "pick0")
            ch(v.memset(ws[:], 0.0))
            ch.tell(v.memset(acc[:], 0.0), ws_done, 0)
            ch(v.tensor_copy(rowid[:], cst[:, K_ROW:K_ROW + 1]))
            ch(v.memset(xs[S:P, :], 0.0))
            ch.tell(v.memset(back[:].bitcast(F32), 0.0), back_ready, 0)
            n_steps = dve.value_load(steps[0:1, NE + XSTEPS:NE + XSTEPS + 1], min_val=NE, max_val=NE + XSTEPS)
            dve.sem_inc(cmb_done.sem, 2)
            dve.sem_inc(pick_ready.sem, 1)

            def slot_weights(q, k):
                dve.wait_ge(xb_gathered.sem, xb_gathered.at(q, k))
                v.tensor_copy(wsn[:], bank[2][:, 500:501]).then_inc(wsn_done.sem, 1)

            def tokens_lo(q, k):
                dve.wait_ge(xhi_ready.sem, xhi_ready.at(q, k))
                v.tensor_tensor(x_hl[:, :, 1, :], bX[:, :].rearrange("p (k s) -> p k s", k=KC),
                                x_hl[:, :, 0, :].bitcast(F32), ALU.subtract).then_inc(x_ready.sem, 1)

            def results_lo(q):
                dve.wait_ge(yhi_ready.sem, yhi_ready.at(q, 1))
                for hf in range(2):
                    ins = v.scalar_tensor_tensor(out=y_lo[:, 512 * hf:512 * hf + 512], in0=bY[hf][:, :], scalar=ws[:, 0:1],
                                                 in1=y_hi[:, 512 * hf:512 * hf + 512].bitcast(F32), op0=ALU.mult, op1=ALU.subtract)
                ins.then_inc(ylo_ready.sem, 1)

            slot_weights(0, 0)
            tokens_lo(0, 0)
            with dve.Fori(0, n_steps) as q:
                ch.enter(q, 6)

                def small(s):
                    dve.wait_ge(hi_ready.sem, hi_ready.at(q, s + 1))
                    v.tensor_tensor(wlo[s % R][:, 0:LOD], wflat(s)[:, 0:LOD], whi[s % R][:, 0:LOD].bitcast(F32),
                                    ALU.subtract).then_inc(lo_dve.sem, 1)

                def add_combined(j):
                    dve.wait_ge(cmb_ready.sem, cmb_ready.at(q, j + 1))
                    v.tensor_tensor(acc[:, j, :], acc[:, j, :], bank[2 + j % 2][:, 0:T], ALU.add).then_inc(cmb_done.sem, 1)

                small(0)
                small(1)
                results_lo(q)
                small(2)
                dve.wait_ge(pick_ready.sem, pick_ready.at(q, 0))
                match_slots(lambda ins: ch.tell(ins, eq_ready, 1))
                add_combined(0)
                small(3)
                dve.wait_ge(ylo_ready.sem, ylo_ready.at(q, 1))
                dve.wait_ge(wsn_done.sem, wsn_done.at(q, 0))
                v.tensor_copy(ws[:], wsn[:]).then_inc(ws_done.sem, 1)
                for j in range(1, 5):
                    add_combined(j)
                    small(j + 3)
                for j in range(5, 8):
                    add_combined(j)
                ch(v.tensor_scalar(backt, ABrow[:, 0, :], rowid[:, 0:1], None, ALU.is_equal))
                ch.tell(v.scalar_tensor_tensor(out=back[:], in0=ABrow[:, 1, :], scalar=rowid[:, 0:1], in1=backt,
                                               op0=ALU.is_equal, op1=ALU.add), back_ready, 1)
                ch(v.tensor_scalar(rowid[:], rowid[:], float(S), None, ALU.add))
                small(8)
                small(9)
                dve.wait_ge(silu_e.sem, silu_e.at(q, 1))
                ch(v.tensor_tensor(aq, sgq, bGT[:, 256:512], ALU.mult))
                a4 = aq.rearrange("p (f s) -> p f s", f=FC)
                ch(v.tensor_copy(a_hl[:, :, 0, :], a4))
                v.tensor_tensor(a_hl[:, :, 1, :], a4, a_hl[:, :, 0, :].bitcast(F32), ALU.subtract).then_inc(act_ready.sem, 1)
                slot_weights(q, 1)
                small(10)
                tokens_lo(q, 1)
                small(11)
            ch.leave(0)
            results_lo(n_steps)
            ch = Chain(dve, dve_ch2)
            for j in range(8):
                dve.wait_ge(cmb_ready.sem, cmb_ready.at(n_steps, j + 1))
                ch(v.tensor_tensor(acc[:, j, :], acc[:, j, :], bank[[2, 3, 4, 7, 0, 1, 5, 6][j]][:, 0:T], ALU.add))
            for j in range(8):
                ch.step(v.tensor_tensor(xT[:, j, :], xT[:, j, :], acc[:, j, :], ALU.add), dve_end, f"x3_{j}")
            dve.wait_ge(act_end.sem, act_end.at("grs"))
            norm(hT, xT, C_GPG, rs, dve_end, "hg")
            for j in range(8):
                dve.wait_ge(act_end.sem, act_end.at(f"sig{j}"))
                ch(v.tensor_tensor(sgu, sg[j % 2], eT[:, j, :], ALU.mult))
                ch.step(v.tensor_tensor(xT[:, j, :], xT[:, j, :], sgu, ALU.add), dve_end, f"x4_{j}")
            dve.wait_ge(act_end.sem, act_end.at("yrs"))
            norm(hT, xT, C_GFIN, rs, dve_end, "hy")
            for i in range(6):
                c, hf = i // 2, i % 2
                n = TOK[c][1]
                dve.wait_ge(pe_end.sem, pe_end.at(f"out{i}"))
                ch.step(v.tensor_copy(yrow[0:n, c, 512 * hf:512 * hf + 512], bank[EB[i]][0:n, :]), dve_end, f"out{i}")

        @block.tensor
        def _(pe):
            mm, tr = nc.tensor.matmul, nc.tensor.transpose
            pe.wait_ge(d_cst, 16)
            pe.wait_ge(d_x, 32)
            for k in range(KC):
                if k == 7:
                    pe.wait_ge(dve_pro.sem, dve_pro.at("x0"))
                for c, (t0, n) in enumerate(TOK):
                    ins = tr(bank[XB[k]][:, t0:t0 + n], xrow[0:n, c, k * P:(k + 1) * P], ident[0:n, 0:n])
                ins.then_inc(pe_pro.sem, 1)
            pe.wait_ge(d_par, 16 * 13)
            pe.wait_ge(dve_pro.sem, dve_pro.at("x3"))
            for t, n in enumerate((P, P, 24)):
                ins = tr(bank[4][:, t * P:t * P + n], prow[0:n, t, :], ident[0:n, 0:n])
            ins.then_inc(pe_pro.sem, 1)
            pe.wait_ge(d_row, 48)
            for t in range(4):
                tr(bank[1][:, t * P:(t + 1) * P], srow[:, t, :], ident)
            for t in range(2):
                tr(bank[2][:, t * P:(t + 1) * P], srow[:, 4 + t, :], ident)
            for t in range(2):
                tr(bank[2][:, 256 + 96 * t:352 + 96 * t], lrow[0:96, t, :], ident[0:96, 0:96])
            tr(bank[2][:, 448:512], hrow[0:64], ident[0:64, 0:64]).then_inc(pe_pro.sem, 1)

            def rms(b, src, steps, names):
                for k in range(KC):
                    if names:
                        pe.wait_ge(names[0].sem, names[0].at(f"{names[1]}{k}"))
                    ins = mm(b[:, 0:T], ones, src[:, k, :], start=(k == 0), stop=(k == KC - 1))
                ins.then_inc(steps.sem, 1)

            rms(bCB, sq, pe_pro, (act_pro, "sq"))
            pe.wait_ge(d_wdt, 16)
            for k in range(KC):
                pe.wait_ge(dve_pro.sem, dve_pro.at(f"hT{k}"))
                ins = mm(bank[4][0:H, 0:T], wdt[:, k, :], hT[:, k, :], start=(k == 0), stop=(k == KC - 1))
            ins.then_inc(pe_pro.sem, 1)
            pe.wait_ge(dve_pro.sem, dve_pro.at("aT"))
            for c, (t0, n) in enumerate(TOK):
                tr(bank[5][0:n, c * H:(c + 1) * H], aT[:, t0:t0 + n], ident[0:H, 0:H])
            for h in range(2):
                ins = mm(bank[5][64 * h:64 * h + 64, P:P + 16], hc[:, 2:3].to_broadcast([H, 64]), ident[0:H, h:H:2], start=True, stop=True)
            ins.then_inc(pe_pro.sem, 1)
            pe.wait_ge(dve_pro.sem, dve_pro.at("atok"))
            for c, (t0, n) in enumerate(TOK):
                m = tri if c < 2 else cst[0:NS, K_TRIS:K_TRIS + NS]
                ins = mm(bank[6][0:H, t0:t0 + n], atok[0:n, c, :], m, start=True, stop=True)
            ins.then_inc(pe_pro.sem, 1)
            pe.wait_ge(act_pro.sem, act_pro.at("dte"))
            for i, src in enumerate((sp[0][0:H, 0:T], cumT[:], dteT)):
                for c, (t0, n) in enumerate(TOK):
                    ins = tr(bank[7][0:n, (3 * i + c) * H:(3 * i + c + 1) * H], src[:, t0:t0 + n], ident[0:H, 0:H])
            ins.then_inc(pe_pro.sem, 1)
            pe.wait_ge(dve_pro.sem, dve_pro.at("tm"))
            pe.sem_inc(YO_ready.sem, 1)

            with pe.Fori(0, G) as g:
                def proj(i):
                    pe.wait_ge(landed[i], g * 16 + 16)
                    pe.wait_ge(proj_free.sem, proj_free.at(g, i - 1))
                    for k in range(KC):
                        ins = mm(bP[i % 2][:, 0:T], wb[:, i, k, :], hT[:, k, :], start=(k == 0), stop=(k == KC - 1))
                    ins.then_inc(used[i], 1)

                def token_major(c):
                    t0, n = TOK[c]
                    pe.wait_ge(T_free.sem, T_free.at(g, c))
                    for i in range(3):
                        ins = tr(bT[0:n, i * P:(i + 1) * P], xbc[i][:, t0:t0 + n], ident)
                    ins.then_inc(T_ready.sem, 1)

                def cum_rows(c):
                    t0, n = TOK[c]
                    pe.wait_ge(CU_free.sem, CU_free.at(g, c))
                    mm(bCU[:, 0:4 * n].rearrange("p (h q) -> p h q", h=4), cst[0:H, K_ONE:K_ONE + P], Dg[:, :, t0:t0 + n],
                       start=True, stop=True).then_inc(CU_ready.sem, 1)

                def y_diag(c):
                    t0, n = TOK[c]
                    pe.wait_ge(W_ready.sem, W_ready.at(g, c + 1))
                    w = (tw[:, c, :] if c < 2 else tws[:]).rearrange("p (h q) -> p h q", h=4)
                    for j in range(2):
                        for h in range(2):
                            ins = mm(bY[j][64 * h:64 * h + 64, t0:t0 + n], xdt[0:n, c, (2 * j + h) * 64:(2 * j + h + 1) * 64],
                                     w[:, 2 * j + h, :], start=True, stop=True)
                    return ins

                def state_T(j, hf):
                    k = 5 + 2 * j + hf
                    if j == 0 and hf == 0:
                        pe.wait_ge(sin_landed, g * 32 + 32)
                    pe.wait_ge(T_free.sem, T_free.at(g, k - 1))
                    for b in range(4):
                        ins = tr(bT[:, b * P:(b + 1) * P], Sin[:, j, 4 * hf + b, :], ident)
                    ins.then_inc(T_ready.sem, 1)

                def y_state(j):
                    pe.wait_ge(T_free.sem, T_free.at(g, 6 + 2 * j))
                    for b in range(NB):
                        ins = mm(bYO[:, j * 160 + P + NT * b:j * 160 + P + NT * b + NT], sT[:, b, :],
                                 xbc[3][:, NP + NT * b:NP + NT * b + NT], start=True, stop=True)
                    return ins

                def new_states(k):
                    j, hf = k // 2, k % 2
                    b, ready, free, n = ((bCU, CU_ready, CU_free, 5 + k // 2), (bT, T_ready, T_free, 9 + k // 2))[k % 2]
                    pe.wait_ge(free.sem, free.at(g, n - 1))
                    mm(b[:, :], xdte[0:NS, 2, j * P:(j + 1) * P], Bm[:, 4 * hf:4 * hf + 4, :].rearrange("p b n -> p (b n)"),
                       start=True, stop=True).then_inc(ready.sem, 1)

                for i in range(6):
                    proj(i)
                pe.wait_ge(silu_done.sem, silu_done.at(g, 4))
                pe.wait_ge(CB_free.sem, CB_free.at(g, 0))
                for c, (t0, n) in enumerate(TOK):
                    ins = mm(bCB[0:n, t0:t0 + n], xbc[2][:, t0:t0 + n], xbc[3][:, t0:t0 + n], start=True, stop=True)
                ins.then_inc(CB_ready.sem, 1)
                token_major(0)
                pe.wait_ge(dg_ready.sem, dg_ready.at(g, 1))
                cum_rows(0)
                proj(6)
                pe.wait_ge(gate_landed, g * 32 + 32)
                pe.wait_ge(conv_done.sem, conv_done.at(g, 5))
                pe.wait_ge(Y_free.sem, Y_free.at(g, 0))
                mm(bY[0][:, 0:T], wg[:, 0, :], u[:], start=True, stop=True)
                mm(bY[1][:, 0:T], wg[:, 1, :], u[:], start=True, stop=True).then_inc(Y_ready.sem, 1)
                token_major(1)
                cum_rows(1)
                proj(7)
                token_major(2)
                cum_rows(2)
                proj(8)
                pe.wait_ge(xdte_ready.sem, xdte_ready.at(g, 1))
                pe.wait_ge(T_free.sem, T_free.at(g, 3))
                mm(bT[:, 0:256], btok[:, 0, :], xdte[:, 0, :], start=True, stop=True).then_inc(T_ready.sem, 1)
                pe.wait_ge(Y_free.sem, Y_free.at(g, 1))
                y_diag(0)
                state_T(0, 0)
                y_diag(1)
                pe.wait_ge(YO_free.sem, YO_free.at(g, 0))
                for j in range(2):
                    mm(bYO[:, 160 * j:160 * j + P], sprev[:, j * P:(j + 1) * P], xbc[3][:, P:2 * P], start=True, stop=True)
                state_T(0, 1)
                y_diag(2).then_inc(Y_ready.sem, 1)
                pe.wait_ge(xdte_ready.sem, xdte_ready.at(g, 3))
                pe.wait_ge(CU_free.sem, CU_free.at(g, 3))
                for j in range(2):
                    for c in range(QC):
                        ins = mm(bCU[:, 256 * j + P * c:256 * j + P * (c + 1)], xdte[:, c, j * P:(j + 1) * P], btok[:, c, :],
                                 start=True, stop=True)
                ins.then_inc(CU_ready.sem, 1)
                y_state(0)
                state_T(1, 0)
                pe.wait_ge(bm_ready.sem, bm_ready.at(g, 1))
                new_states(0)
                state_T(1, 1)
                proj(9)
                y_state(1).then_inc(YO_ready.sem, 1)
                for k in range(1, 4):
                    new_states(k)
                pe.wait_ge(sq_ready.sem, sq_ready.at(g, 1))
                for j in range(2):
                    ins = mm(bCB[:, 0:T], ones, tw[:, j, 0:T], start=(j == 0), stop=(j == 1))
                ins.then_inc(CB_ready.sem, 1)

            pe.wait_ge(lru_tail.sem, lru_tail.at(G - 1, 1))
            with pe.Fori(0, 4) as i:
                for jj in range(2):
                    o = 3 * jj
                    pe.wait_ge(br_done.sem, br_done.at(i, jj - 1))
                    pe.wait_ge(landed[o], i * 16 + 16 * (G + 1))
                    for k in range(KC):
                        ins = mm(BR[jj][0][:, 0:T], wb[:, o, k, :], ya[:, k, :], start=(k == 0), stop=(k == KC - 1))
                    ins.then_inc(used[o], 1)
                    for hf in range(2):
                        pe.wait_ge(landed[o + 1 + hf], i * 16 + 16 * (G + 1))
                        for k in range(KC):
                            ins = mm(BR[jj][1][:, 0:T], wb[:, o + 1 + hf, k, :], yb[:, 8 * hf + k, :],
                                     start=(k == 0 and hf == 0), stop=(k == KC - 1 and hf == 1))
                        ins.then_inc(used[o + 1 + hf], 1)
            pe.wait_ge(br_done.sem, br_done.at(3, 2))
            for j in range(8):
                s = 6 + j % 4
                pe.wait_ge(landed[s], 16 * (G + 1 + j // 4))
                if j >= 4:
                    pe.wait_ge(dve_mid.sem, dve_mid.at(f"x2_{j - 4}"))
                for k in range(KC):
                    ins = mm(R4[j % 4][:, 0:T], wb[:, s, k, :], mg[:, k, :], start=(k == 0), stop=(k == KC - 1))
                ins.then_inc(used[s], 1)
            pe.wait_ge(stashed.sem, stashed.at(G - 1, 5))
            pe.wait_ge(dve_mid.sem, dve_mid.at("x2_6"))
            fS = stS[:].rearrange("p r c -> p (r c)")
            fL = stL[:].rearrange("p r c -> p (r c)")
            fH = hfin[:].rearrange("p r c -> p (r c)")
            tr(bT[0:96, 0:P], fS[:, 0:96], ident)
            for t in range(6):
                b, o = (bT, P * (1 + t)) if t < 3 else (bCB, P * (t - 3))
                tr(b[:, o:o + P], fS[:, 96 + P * t:96 + P * (t + 1)], ident)
            tr(bCB[0:24, 384:512], fL[:, 0:24], ident)
            tr(bCU[0:96, 0:P], fL[:, 24:120], ident)
            tr(bCU[0:96, P:2 * P], fL[:, 120:216], ident)
            tr(bCU[0:72, 256:384], fH, ident).then_inc(pe_mid.sem, 1)
            pe.wait_ge(d_plr, 48)
            for k in range(2):
                for c, (t0, n) in enumerate(TOK):
                    ins = tr(bY[k][:, t0:t0 + n], plr[0:n, c, k * P:(k + 1) * P], ident[0:n, 0:n])
            ins.then_inc(pe_mid.sem, 1)
            rms(bP[0], sq, pe_mid, (act_mid, "sqf"))
            pe.wait_ge(act_mid.sem, act_mid.at("pT"))
            pe.wait_ge(act_mid.sem, act_mid.at("st"))
            pe.wait_ge(dve_mid.sem, dve_mid.at("x2_7"))
            for j in range(8):
                s = 10 + j // 4
                if j % 4 == 0:
                    pe.wait_ge(landed[s], 16)
                if j >= 4:
                    pe.wait_ge(act_mid.sem, act_mid.at(f"e{j - 4}"))
                w = wb[:, s].rearrange("p a b -> p (a b)").rearrange("p (k c) -> p k c", k=2)
                for k in range(2):
                    ins = mm(R4[j % 4][:, 0:T], w[:, k, (j % 4) * P:(j % 4 + 1) * P], pT[:, k, :], start=(k == 0), stop=(k == 1))
                ins.then_inc(pe_mid.sem, 1)
            rms(bP[1], sq, pe_mid, (act_mid, "e"))
            pe.wait_ge(d_wr, 64)
            pe.wait_ge(dve_mid.sem, dve_mid.at("hf7"))
            for c, (t0, n) in enumerate(TOK):
                for k in range(KC):
                    mm(bY[0][0:n, 20 * c:20 * c + 20], hT[:, k, t0:t0 + n], wr[:, k, :], start=(k == 0), stop=False)
                ins = mm(bY[0][0:n, 20 * c:20 * c + 20], cst[0:1, K_ONE:K_ONE + n], rb[:], start=False, stop=True)
            ins.then_inc(pe_mid.sem, 1)
            def tokens_T(i):
                c, hf = i // 2, i % 2
                t0, n = TOK[c]
                for k in range(4):
                    ins = tr(R4[i % 4][0:n, k * P:(k + 1) * P], hT[:, 4 * hf + k, t0:t0 + n], ident)
                ins.then_inc(pe_mid.sem, 1)

            pe.wait_ge(act_mid.sem, act_mid.at("ers"))
            for i in range(4):
                tokens_T(i)
            pe.wait_ge(dve_mid.sem, dve_mid.at("M"))
            for c, (t0, n) in enumerate(TOK):
                ins = tr(bY[1][0:NE, t0:t0 + n], rM[0:n, c, 32:48], ident[0:n, 0:n])
            ins.then_inc(pe_mid.sem, 1)
            for i in range(4, 6):
                pe.wait_ge(dve_mid.sem, dve_mid.at(f"lo{i - 4}"))
                tokens_T(i)
            pe.wait_ge(dve_mid.sem, dve_mid.at("count"))
            mm(bY[1][0:NE, T:T + 1], tri[0:NE, 0:NE], rX[:, 8:9], start=True, stop=True).then_inc(pe_mid.sem, 1)
            pe.wait_ge(dve_mid.sem, dve_mid.at("end"))
            mm(bY[1][0:1, 320:320 + XSTEPS], ones[0:NE, 0:1], rX[:, 0:XSTEPS], start=True, stop=True)
            mm(bY[1][0:1, 330:331], ones[0:NE, 0:1], rX[:, 8:9], start=True, stop=True).then_inc(pe_mid.sem, 1)
            pe.wait_ge(dve_mid.sem, dve_mid.at("slots"))
            for c, (t0, n) in enumerate(TOK):
                ins = tr(bY[0][0:n, NE * c:NE * c + NE], rC[:, t0:t0 + n], ident[0:NE, 0:NE])
            ins.then_inc(pe_mid.sem, 1)
            pe.wait_ge(dve_mid.sem, dve_mid.at("AB"))
            for i in range(2):
                for c, (t0, n) in enumerate(TOK):
                    ins = mm(bP[i][:, t0:t0 + n], AB[0:n, i, c:c + 1].to_broadcast([n, P]), ident[0:n, 0:n], start=True, stop=True)
            ins.then_inc(pe_mid.sem, 1)

            II = cst[:, K_II:K_II + S]

            def gather(hf):
                for i, h in enumerate((htok_hi, htok_lo)):
                    for c, (t0, n) in enumerate(TOK):
                        ins = mm(bY[hf][0:S, :], pick[0:n, c, :], h[0:n, c, 512 * hf:512 * hf + 512],
                                 start=(i == 0 and c == 0), stop=(i == 1 and c == 2))
                return ins

            def gather_weights():
                for i in range(2):
                    for c, (t0, n) in enumerate(TOK):
                        ins = mm(bank[2][S * i:S * i + S, 500:501], eW[0:n, c, :], ones[0:n, 0:1], start=(c == 0), stop=(c == 2))
                return ins

            def tokens_by_feature(q, kk):
                for k in range(KC):
                    if k % 4 == 0:
                        out = (xs0_out, xs1_out)[k // 4]
                        pe.wait_ge(out.sem, out.at(q, kk))
                    ins = mm(bX[:, k * S:(k + 1) * S], xs[:, k * P:(k + 1) * P], ident[:, 0:S], start=True, stop=True)
                ins.then_inc(xt_ready.sem, 1)

            pe.wait_ge(dve_mid.sem, dve_mid.at("pick0"))
            pe.wait_ge(dve_mid.sem, dve_mid.at("rows"))
            for hf in range(2):
                mm(bY[hf][:, :], ones, xT[:].rearrange("p a b -> p (a b)")[:, 0:512], start=True, stop=True)
            gather(0).then_inc(xa_gathered.sem, 1)
            gather(1)
            gather_weights().then_inc(xb_gathered.sem, 1)
            pe.wait_ge(back_ready.sem, back_ready.at(0, 0))
            tokens_by_feature(0, 0)
            pe.sem_inc(hl_free.sem, R)
            pe.sem_inc(cmb_ready.sem, 1)
            n_steps = pe.value_load(steps[0:1, NE + XSTEPS:NE + XSTEPS + 1], min_val=NE, max_val=NE + XSTEPS)

            def combine(j, b):
                mm(b[:, 0:T], y_hi[:, j * P:(j + 1) * P], back[:], start=True, stop=False)
                mm(b[:, 0:T], y_lo[:, j * P:(j + 1) * P], back[:], start=False, stop=True).then_inc(cmb_ready.sem, 1)

            with pe.Fori(0, n_steps) as q:
                def split(s):
                    pe.wait_ge(lo_dve.sem, lo_dve.at(q, s + 1))
                    pe.wait_ge(lo_pool.sem, lo_pool.at(q, s + 1))

                def up(s):
                    split(s)
                    for k in range(2):
                        for i, w in enumerate((whi, wlo)):
                            kk = 2 * (s // 2) + k
                            ins = mm((bG1, bG3)[s % 2][:, :], x_hl[:, kk, :, :], w[s % R][:, 512 * k:512 * k + 512],
                                     start=(kk == 0 and i == 0), stop=(kk == KC - 1 and i == 1))
                    ins.then_inc(hl_free.sem, 1)

                def put_back(j):
                    pe.wait_ge(cmb_done.sem, cmb_done.at(q, j - 1))
                    combine(j, bank[2 + j % 2])

                pe.wait_ge(x_ready.sem, x_ready.at(q, 0))
                up(0)
                up(1)
                pe.wait_ge(ylo_ready.sem, ylo_ready.at(q, 1))
                pe.wait_ge(wsn_done.sem, wsn_done.at(q, 0))
                pe.wait_ge(back_ready.sem, back_ready.at(q, 0))
                for j in range(6):
                    put_back(j)
                    up(2 + j)
                put_back(6)
                put_back(7)
                pe.wait_ge(pick_ready.sem, pick_ready.at(q, 1))
                gather(0).then_inc(xa_gathered.sem, 1)
                for i, (out, o) in enumerate(((g1_out, 0), (g3_out, 512))):
                    pe.wait_ge(out.sem, out.at(q, 1))
                    for f in range(FC):
                        ins = mm(bGT[:, 256 * i + f * S:256 * i + (f + 1) * S], Gs[:, o + f * P:o + (f + 1) * P], II,
                                 start=True, stop=True)
                ins.then_inc(gt_ready.sem, 1)
                gather(1)
                pe.wait_ge(cmb_done.sem, cmb_done.at(q, 7))
                gather_weights().then_inc(xb_gathered.sem, 1)
                tokens_by_feature(q, 1)
                pe.wait_ge(act_ready.sem, act_ready.at(q, 1))
                for f in range(FC):
                    split(8 + f)
                    for i, w in enumerate((whi, wlo)):
                        for hf in range(2):
                            ins = mm(bY[hf][:, :], a_hl[:, f, :, :], w[(8 + f) % R][:, 512 * hf:512 * hf + 512],
                                     start=(f == 0 and i == 0), stop=(f == FC - 1 and i == 1))
                    ins.then_inc(hl_free.sem, 1)
            pe.wait_ge(ylo_ready.sem, ylo_ready.at(n_steps, 1))
            pe.wait_ge(back_ready.sem, back_ready.at(n_steps, 0))
            pe.wait_ge(cmb_done.sem, cmb_done.at(n_steps, 0))
            pe.wait_ge(wsn_done.sem, wsn_done.at(n_steps, 0))
            for j in range(8):
                combine(j, bank[[2, 3, 4, 7, 0, 1, 5, 6][j]])
            pe.wait_ge(dve_end.sem, dve_end.at("x3_0"))
            rms(bP[0], sq, pe_end, (act_end, "sg"))
            for j in range(8):
                pe.wait_ge(landed[j], n_steps * 16 + 16 * (base_land[j] + 1))
                if j >= 4:
                    pe.wait_ge(act_end.sem, act_end.at(f"sig{j - 4}"))
                for k in range(KC):
                    if j == 0:
                        pe.wait_ge(dve_end.sem, dve_end.at(f"hg{k}"))
                    ins = mm(R4[j % 4][:, 0:T], wb[:, j, k, :], hT[:, k, :], start=(k == 0), stop=(k == KC - 1))
                ins.then_inc(used[j], 1)
            rms(bP[1], sq, pe_end, (act_end, "sy"))
            for i in range(6):
                c, hf = i // 2, i % 2
                pe.wait_ge(dve_end.sem, dve_end.at(f"hy{4 * hf + 3}"))
                t0, n = TOK[c]
                for k in range(4):
                    ins = tr(bank[EB[i]][0:n, k * P:(k + 1) * P], hT[:, 4 * hf + k, t0:t0 + n], ident)
                ins.then_inc(pe_end.sem, 1)


_INS = ["x_prompt", "x_sample", "state_lru_h", "state_lru_conv", "state_ssd", "state_ssd_conv", "p_prompt", "p_sample",
        "g_mix", "w_in", "lru_conv_w", "lru_conv_b", "lru_wa", "lru_ba", "lru_wx", "lru_bx", "lru_lambda",
        "ssd_conv_w", "ssd_conv_b", "ssd_dt_bias", "ssd_A_log", "ssd_D", "ssd_norm_g",
        "w_br_lru", "w_br_ssd", "w_out", "g_ffn", "w_router_g", "b_router_g", "w_router_e", "b_router_e",
        "w1", "w3", "w2", "w_ple_proj", "g_ple", "g_ple_gate", "w_ple_gate", "g_final"]
_OUTS = [("y_prompt", (1, NP, D)), ("y_sample", (NB, NT, D)), ("new_lru_h_p", (1, 1, D)), ("new_lru_conv_p", (1, 1, 3, D)),
         ("new_ssd_p", (1, 1, H, 64, P)), ("new_ssd_conv_p", (1, 1, 3, 4096)), ("new_lru_h_s", (1, NB, D)),
         ("new_lru_conv_s", (1, NB, 3, D)), ("new_ssd_s", (1, NB, H, 64, P)), ("new_ssd_conv_s", (1, NB, 3, 4096))]


def kernel(**inputs):
    import numpy as _np
    import concourse.bacc as _bacc
    from concourse import mybir as _mybir
    from concourse.bass_utils import run_bass_kernel_spmd as _run

    nc = _bacc.Bacc("TRN2", target_bir_lowering=False, num_devices=1)
    arrays, aps = {}, {}
    for name in _INS + ["constants"]:
        x = constants() if name == "constants" else _np.ascontiguousarray(inputs[name])
        arrays[f"in_{name}"] = x
        aps[name] = nc.dram_tensor(f"in_{name}", x.shape, _mybir.dt.from_np(x.dtype), kind="ExternalInput").ap()
    for name, shape in _OUTS:
        aps[name] = nc.dram_tensor(f"out_{name}", shape, _mybir.dt.float32, kind="ExternalOutput").ap()
    build(nc, aps)
    r = _run(nc, [arrays], core_ids=[0])
    return tuple(r.results[0][f"out_{name}"] for name, _ in _OUTS)
```

```python
from contextlib import ExitStack

import numpy as np

import concourse.bass as bass
from concourse import mybir

F32 = mybir.dt.float32
F32R = mybir.dt.float32r
I32 = mybir.dt.int32
ALU = mybir.AluOpType
ACT = mybir.ActivationFunctionType
AX = mybir.AxisListType
ds = bass.ds

P = 128
D = 1024
KC = D // P
NP = 256
NB, NT = 8, 4
NS = NB * NT
T = NP + NS
QC = 2
TOK = [(0, P), (P, P), (NP, NS)]
G = 8
H = 32
PAD = 3 + NP + NB * (3 + NT)
SMP = 3 + NP
CVW = PAD - 3
EPS = 1e-6
NE, NEG, EPG, FF = 16, 4, 4, 512
FC = FF // P
S = 64
XSTEPS = (2 * T - 1) // S
CPE = -(-T // S)
NBLK = 12
R = 4
WLOD = 256
LOD = 704

O_LRU, O_LGATE, O_Z, O_XS = 0, 1024, 2048, 4096
O_B, O_C, O_DT, O_GA, O_GB = 6144, 7168, 8192, 8224, 9248
IN_COLS = 10272

C_SW, C_SB, C_LW, C_NG, C_GMIX, C_GFFN, C_GPLE, C_GPG, C_GFIN, C_LB, C_BA, C_BX, C_LAM, C_END = (
    0, 128, 160, 192, 208, 216, 224, 232, 240, 248, 256, 264, 272, 280)

K_ID, K_TRI, K_NEG, K_TRIS, K_NEGS, K_BM, K_TIE, K_ONE = 0, 128, 256, 384, 416, 448, 456, 460
K_IOTA = 588
K_E64, K_D64, K_ROW, K_THR = K_IOTA + S, K_IOTA + S + 1, K_IOTA + S + 2, K_IOTA + S + 3
K_II = K_THR + CPE - 1
K_END = K_II + S


def constants():
    c = np.zeros((P, K_END), np.float32)
    s, q = np.arange(P)[:, None], np.arange(P)[None, :]
    c[:, K_ID:K_ID + P] = s == q
    c[:, K_TRI:K_TRI + P] = s <= q
    c[:, K_NEG:K_NEG + P] = np.where(s <= q, 0.0, -1e30)
    same = (s[:NS] // NT == q[:, :NS] // NT) & (s[:NS] <= q[:, :NS])
    c[:NS, K_TRIS:K_TRIS + NS] = same
    c[:NS, K_NEGS:K_NEGS + NS] = np.where(same, 0.0, -1e30)
    c[:NS, K_BM:K_BM + NB] = s[:NS] // NT == np.arange(NB)[None, :]
    c[:, K_TIE:K_TIE + 4] = 4.0 - np.arange(4)[None, :]
    c[:, K_ONE:K_ONE + P] = 1.0
    c[:, K_IOTA:K_IOTA + S] = np.arange(S)
    c[:, K_E64] = S * np.arange(P) - 1
    c[:, K_D64] = (NE - 1) * S - S * np.arange(P)
    c[:, K_ROW] = np.arange(P) % S
    c[:, K_THR:K_II] = S * np.arange(1, CPE)
    c[:, K_II:K_END] = s % S == np.arange(S)[None, :]
    return c


class Signal:

    def __init__(self, sem, per=0, credit=0):
        self.sem, self.per, self.credit = sem, per, credit

    def at(self, g, k):
        return g * self.per + (k + self.credit)


class Chain:

    def __init__(self, eng, sem):
        self.eng, self.sem, self.base, self.k, self.g, self.per = eng, sem, 0, 0, 0, 0

    def enter(self, g, per):
        self.base += self.k
        self.g, self.per, self.k = g, per, 0

    def peel(self, g):
        self.g, self.k = g, 0

    def leave(self, steps):
        assert self.k == self.per, (self.k, self.per)
        self.base += steps * self.per
        self.g, self.per, self.k = 0, 0, 0

    def __call__(self, ins):
        self.k += 1
        ins.then_inc(self.sem, 1)
        self.eng.wait_ge(self.sem, self.g * self.per + (self.base + self.k))

    def tell(self, ins, sig, k):
        ins.then_inc(sig.sem, 1)
        self.eng.wait_ge(sig.sem, sig.at(self.g, k))

    def step(self, ins, steps, name):
        ins.then_inc(steps.sem, 1)
        self.eng.wait_ge(steps.sem, steps.at(name))


class Steps:

    def __init__(self, sem, names):
        self.sem, self.names = sem, list(names)

    def at(self, name):
        return self.names.index(name) + 1


def build(nc, a):
    with ExitStack() as ctx:
        def sb(name, shape):
            return ctx.enter_context(nc.sbuf_tensor(name, shape, F32))

        def sem(name):
            return ctx.enter_context(nc.semaphore(name))

        def sig(name, per=0, credit=0):
            return Signal(sem(name), per, credit)

        bank = [ctx.enter_context(nc.psum_tensor(f"bank{i}", [P, 512], F32)) for i in range(8)]
        bP, bT, bCB, bCU, bY, bYO = bank[0:2], bank[2], bank[3], bank[4], bank[5:7], bank[7]

        NSLOT = 12
        mixer, moe = ExitStack(), ExitStack()

        def sbm(name, shape):
            return mixer.enter_context(nc.sbuf_tensor(name, shape, F32))

        def sbe(name, shape, dt=F32):
            return moe.enter_context(nc.sbuf_tensor(name, shape, dt))

        wb = sb("wb", [P, 6, KC, P])
        whi = [ctx.enter_context(nc.sbuf_tensor(f"whi{i}", [P, D], F32R)) for i in range(2)]
        wlo = [ctx.enter_context(nc.sbuf_tensor(f"wlo{i}", [P, D], F32R)) for i in range(2)]
        wr = sb("wr", [P, KC, 20])
        cst = sb("cst", [P, K_END])
        par = sb("par", [P, C_END])
        xT = sb("xT", [P, KC, T])
        hT = sb("hT", [P, KC, T])
        ya = sb("ya", [P, KC, T])
        ga = sb("ga", [P, KC, T])
        gb = sb("gb", [P, KC, T])
        yb = sb("yb", [P, 16, T])
        stS = sb("stS", [P, 27, 32])
        stL = sb("stL", [P, 27, 8])
        hfin = sb("hfin", [P, 9, 8])
        rb = sb("rb", [1, 20])
        u = sb("u", [P, T])
        rr = sb("rr", [P, T])
        ii = sb("ii", [P, T])
        TT = sb("TT", [P, T])
        aS = sb("aS", [P, T])
        gl = sb("gl", [P, T])
        kc2 = sb("kc2", [P, 2, 8])
        steps = ctx.enter_context(nc.sbuf_tensor("steps", [1, NE + XSTEPS + 1], I32))
        arena = sbm("arena", [P, 7616])
        cstS = sbm("cstS", [P, 24, 32])
        cstL = sbm("cstL", [P, 24, 8])
        h0T = sbm("h0T", [P, NB, KC])
        h_hi = mixer.enter_context(nc.sbuf_tensor("h_hi", [P, KC, T], F32R))
        h_lo = mixer.enter_context(nc.sbuf_tensor("h_lo", [P, KC, T], F32R))
        wdt = sbm("wdt", [P, KC, H])
        wg = sbm("wg", [P, 2, P])
        ex = sbm("ex", [P, 2, 160])
        Dt = sbm("Dt", [P, 16])
        TM = sbm("TM", [P, 3, 3, H])
        cumT = sbm("cumT", [H, T])
        pads = [sbm(f"pad{i}", [P, PAD]) for i in range(5)]
        cv = [sbm(f"cv{i}", [P, PAD]) for i in range(2)]
        xbc = [sbm(f"xbc{i}", [P, T]) for i in range(4)]
        zs = sbm("zs", [P, 2, T])
        xdt = sbm("xdt", [P, 3, 256])
        xdte = sbm("xdte", [P, 3, 256])
        btok = sbm("btok", [P, 3, P])
        tw = sbm("tw", [P, 2, 512])
        tws = sbm("tws", [NS, 4 * NS])
        sprev = sbm("sprev", [P, 256])
        fin = sbm("fin", [P, 2, P])
        mixer.close()
        smalls = ExitStack()
        br_lo = smalls.enter_context(nc.sbuf_tensor("br_lo", [P, 24, T], F32R))
        smalls.close()
        htok_hi = sbe("htok_hi", [P, 3, D], F32R)
        htok_lo = sbe("htok_lo", [P, 3, D], F32R)
        wb2 = sbe("wb2", [P, 6, KC, P])
        halves = ExitStack()
        br_hi = halves.enter_context(nc.sbuf_tensor("br_hi", [P, 24, T], F32R))
        halves.close()
        whi += [sbe(f"whi{i}", [P, D], F32R) for i in range(2, R)]
        wlo += [sbe(f"wlo{i}", [P, D], F32R) for i in range(2, R)]
        pick = sbe("pick", [P, 3, S], F32R)
        back = sbe("back", [P, T], F32R)
        x_hl = sbe("x_hl", [P, KC, 2, S], F32R)
        a_hl = sbe("a_hl", [P, FC, 2, S], F32R)
        y_hi = sbe("y_hi", [P, D], F32R)
        y_lo = sbe("y_lo", [P, D], F32R)
        AB = sbe("AB", [P, 2, 3])
        wAB = sbe("wAB", [P, 2, 3])
        rowid = sbe("rowid", [P, 1])
        ws = sbe("ws", [P, 1])
        wsn = sbe("wsn", [P, 1])
        rM = sbe("rM", [P, 3, 48])
        rG = sbe("rG", [P, 3, NE])
        rX = sbe("rX", [NE, 16])
        moe.close()
        ident = cst[:, K_ID:K_ID + P]
        tri = cst[:, K_TRI:K_TRI + P]
        ones = cst[:, K_ONE:K_ONE + P]
        sq = yb[:, 0:KC, :]

        def wblk(s_):
            return wb[:, s_] if s_ < 6 else wb2[:, (s_ - 4) % 6]

        def wflat(s_):
            return wblk(s_).rearrange("p a b -> p (a b)")

        Sin = arena[:, 0:2048].rearrange("p (j b n) -> p j b n", j=2, b=NB)
        Snew = arena[:, 2048:4096].rearrange("p (j b n) -> p j b n", j=2, b=NB)
        sT = arena[:, 4096:5120].rearrange("p (b n) -> p b n", b=NB)
        Bm = arena[0:NS, 5120:6144].rearrange("p (b n) -> p b n", b=NB)
        Dg = arena[0:H, 6144:7296].rearrange("p (h t) -> p h t", h=4)
        yot = arena[:, 7296:7616].rearrange("p (j t) -> p j t", j=2)
        xrow = arena[:, 0:3072].rearrange("p (c n) -> p c n", c=3)
        prow = arena[:, 3072:3456].rearrange("p (c n) -> p c n", c=3)
        srow = arena[:, 3456:4224].rearrange("p (c n) -> p c n", c=6)
        lrow = arena[:, 4224:4480].rearrange("p (c n) -> p c n", c=2)
        hrow = arena[:, 4480:4608]
        sp = [arena[:, 4608 + 296 * i:4904 + 296 * i] for i in range(5)]
        aT = arena[0:H, 6249:6537]
        dteT = arena[0:H, 6537:6825]
        atok = arena[:, 6825:6921].rearrange("p (c h) -> p c h", c=3)
        hc = arena[0:H, 6921:6924]
        Acol = arena[0:H, 6924:6925]
        ybf = yb[:, :, :].rearrange("p a b -> p (a b)")
        res = ga[:].rearrange("p a b -> p (a b)")
        orow = res[:, 0:1280].rearrange("p (c n) -> p c n", c=10)
        lrowo = res[:, 1280:1408]
        plr = ybf[:, 2304:3072].rearrange("p (c n) -> p c n", c=3)
        pT = ybf[:, 3072:3648].rearrange("p (k t) -> p k t", k=2)
        rt = ybf[:, 3648:4148]
        rT, rC, rO = (ga[0:NE, 5 + i, :] for i in range(3))
        sg, sgu = [TT[:], aS[:]], ii[:]
        rs, rs2 = u[:], rr[:]
        ABrow = ybf[:, 0:576].rearrange("p (i t) -> p i t", i=2)
        backt = ybf[:, 576:864]
        eA, eB, eW = (ybf[:, 864 + 192 * i:1056 + 192 * i].rearrange("p (c s) -> p c s", c=3) for i in range(3))
        sgq, aq = (ybf[:, 1440 + 256 * i:1696 + 256 * i] for i in range(2))
        hTf = hT[:].rearrange("p a b -> p (a b)")
        xs, Gs = hTf[:, 0:1024], hTf[:, 1024:2048]
        yrow = yb[:, :, :].rearrange("p a b -> p (a b)")[:, 0:3072].rearrange("p (c n) -> p c n", c=3)
        acc = ya
        hg_hi, hg_lo = (t[:].rearrange("p a b -> p (a b)")[:, 0:KC * T].rearrange("p (k t) -> p k t", k=KC) for t in (htok_hi, htok_lo))
        eT = gb
        mg = hT

        rsP = rr
        XB = [0, 1, 2, 4, 5, 6, 7, 0]
        EB = [0, 1, 2, 4, 5, 6]
        R4 = [bT, bCB, bCU, bYO]
        bX, bG1, bG3, bGT = bank[0], bank[1], bank[4], bank[7]
        BR = UP = [(bP[0], bP[1]), (bY[0], bY[1])]
        BR_LO = [0, 4, 5, 1, 2, 3]
        base_use = [0] * 6 + [2] * 4 + [0] * 2
        base_land = [2 * G + 4] * 5 + [4] + [2] * 4 + [1] * 2

        def rv(o, n, pat=None, **kw):
            w = rt[:, o:o + n]
            return w.rearrange(pat, **kw) if pat else w
        r_lg = rv(0, 60, "p (c n) -> p c n", c=3)
        r_goh, r_gs, r_es, r_o1, r_o2, r_e2 = (rv(64 + 12 * i, 12, "p (c n) -> p c n", c=3) for i in range(6))
        r_m, r_m2, r_gw = (rv(140 + 3 * i, 3) for i in range(3))
        r_pr = rv(152, 48, "p (c g j) -> p c g j", c=3, g=4)
        r_v1, r_v2 = rv(200, 3), rv(203, 3)

        landed = [sem(f"landed{s}") for s in range(NSLOT)]
        used = [sem(f"used{s}") for s in range(NSLOT)]
        nload = [0] * NSLOT
        ncons = [0] * NSLOT

        d_cst, d_x, d_par, d_row, d_small, d_wdt, d_wr = (
            sem("d_cst"), sem("d_x"), sem("d_par"), sem("d_row"), sem("d_small"), sem("d_wdt"), sem("d_wr"))
        d_plr = sem("d_plr")
        d_out = sem("d_out")
        gate_landed = sem("gate_landed")
        sin_landed, state_out = sem("sin_landed"), sem("state_out")
        pe_pro = Steps(sem("pe_pro"), [f"x{k}" for k in range(KC)] + ["par", "hist", "rms", "dt", "atok", "cum", "tm"])
        act_pro = Steps(sem("act_pro"), [f"sq{k}" for k in range(KC)] + ["rs", "A"] + [f"hh{k}" for k in range(KC)] + ["z", "ln", "dte"])
        dve_pro = Steps(sem("dve_pro"), [f"x{k}" for k in range(KC)] + ["par", "hist"] + [f"hT{k}" for k in range(KC)]
                        + ["hl", "ax", "u", "soft", "aT", "atok", "cum", "dteT", "tm"])
        dve_ch, act_ch, pool_ch = sem("dve_ch"), sem("act_ch"), sem("pool_ch")

        w_large, w_small_dve, w_small_pool = sig("w_large", 10), sig("w_small_dve", 10), sig("w_small_pool", 10)
        projected = sig("projected", 10, 2)
        proj_free = sig("proj_free", 10, 2)
        pad_hist = sig("pad_hist", 5)
        conv_done = sig("conv_done", 5, 5)
        stashed = sig("stashed", 5, 5)
        silu_done = sig("silu_done", 4, 4)
        y_done = sig("y_done", 1, 1)
        T_ready, T_free = sig("T_ready", 9), sig("T_free", 9, 1)
        CU_ready, CU_free = sig("CU_ready", 6), sig("CU_free", 6, 1)
        CB_ready, CB_free = sig("CB_ready", 2), sig("CB_free", 1, 1)
        Y_ready, Y_free = sig("Y_ready", 3), sig("Y_free", 3, 1)
        YO_ready, YO_free = sig("YO_ready", 1, 1), sig("YO_free", 1, 1)
        diff_ready = sig("diff_ready", 2)
        dg_ready = sig("dg_ready", 1)
        SN = [(bCU, CU_ready, CU_free, 5), (bT, T_ready, T_free, 9), (bCU, CU_ready, CU_free, 6), (bY[0], Y_ready, Y_free, 3)]
        masked = sig("masked", 3)
        decay_ready = sig("decay_ready", 3)
        W_ready = sig("W_ready", 3)
        xdte_ready = sig("xdte_ready", 3)
        bm_ready = sig("bm_ready", 1)
        sdec_ready = sig("sdec_ready", 2)
        lru_act = sig("lru_act", 1)
        m2_ready = sig("m2_ready", 1)
        m_ready = sig("m_ready", 1)
        gelu_ready = sig("gelu_ready", 1)
        lru_tail = sig("lru_tail", 1, 1)
        sq_ready = sig("sq_ready", 1)
        br_done = sig("br_done", 2, 2)
        gates_ready = sem("gates_ready")
        b_large, b_small_dve, b_small_pool = sig("b_large", 6, 6), sig("b_small_dve", 6, 6), sig("b_small_pool", 6, 6)
        b_done = sig("b_done", 6)
        br_large, br_small = sig("br_large", 6), sig("br_small", 6)
        pe_mid = Steps(sem("pe_mid"), ["st", "pT", "frms"] + [f"e{j}" for j in range(8)]
                       + ["erms", "route"] + [f"ht{i}" for i in range(4)] + ["MT", "ht4", "ht5", "extra", "table", "slots", "rows"])
        act_mid = Steps(sem("act_mid"), [f"sqf{j}" for j in range(8)] + ["st", "pT", "frs"]
                        + [f"e{j}" for j in range(8)] + ["ers", "hi0", "hi1", "gexp", "eexp"] + [f"hi{i}" for i in range(2, 6)])
        dve_mid = Steps(sem("dve_mid"), [f"x2_{j}" for j in range(8)] + [f"hf{k}" for k in range(KC)] + ["gsub", "esub", "lo0", "lo1", "M"]
                        + [f"lo{i}" for i in range(2, 6)] + ["count", "end", "steps", "slots", "AB", "rows", "pick0"])
        hi_ready, lo_dve, lo_pool = sig("hi_ready", NBLK), sig("lo_dve", NBLK, NBLK), sig("lo_pool", NBLK, NBLK)
        hl_free = sig("hl_free", NBLK, R)
        g1_out, g3_out, gt_ready = sig("g1_out", 1), sig("g3_out", 1), sig("gt_ready", 1)
        silu_e, act_ready = sig("silu_e", 1), sig("act_ready", 1)
        cmb_ready, cmb_done = sig("cmb_ready", 8, 1), sig("cmb_done", 8, 2)
        eq_ready = sig("eq_ready", 1)
        pick_ready, back_ready = sig("pick_ready", 1, 1), sig("back_ready", 1, 1)
        xa_gathered, xb_gathered, xt_ready = sig("xa_gathered", 1, 1), sig("xb_gathered", 1, 1), sig("xt_ready", 1, 1)
        xs0_out, xs1_out = sig("xs0_out", 1, 1), sig("xs1_out", 1, 1)
        xhi_ready, x_ready = sig("xhi_ready", 1, 1), sig("x_ready", 1, 1)
        yhi_ready, ylo_ready = sig("yhi_ready", 2), sig("ylo_ready", 2)
        ws_done, wsn_done = sig("ws_done", 1, 1), sig("wsn_done", 1, 1)
        dve_ch2, act_ch2, pool_ch2 = sem("dve_ch2"), sem("act_ch2"), sem("pool_ch2")
        pe_end = Steps(sem("pe_end"), ["grms", "yrms"] + [f"out{i}" for i in range(6)])
        act_end = Steps(sem("act_end"), [f"sg{j}" for j in range(8)] + ["grs"] + [f"hh{k}" for k in range(KC)]
                        + ["sig0"] + [n for j in range(1, 8) for n in (f"sig{j}", f"sy{j - 1}")] + ["sy7", "yrs"])
        dve_end = Steps(sem("dve_end"), [f"x3_{j}" for j in range(8)] + [f"hg{k}" for k in range(KC)] + [f"hl{k}" for k in range(KC)] + [f"eN{k}" for k in range(KC)] + [f"x4_{j}" for j in range(8)]
                        + [f"hy{k}" for k in range(KC)] + [f"out{i}" for i in range(6)])

        w_in = a["w_in"][0].rearrange("(k p) c -> p k c", p=P)
        w1 = a["w1"].rearrange("l e (k p) f -> (l e) p k f", p=P)
        w3 = a["w3"].rearrange("l e (k p) f -> (l e) p k f", p=P)
        w2 = a["w2"].rearrange("l e (k p) n -> (l e) p k n", p=P)
        w_lru = a["w_br_lru"][0].rearrange("(k p) c -> p k c", p=P)
        w_ssd = a["w_br_ssd"][0].rearrange("(k p) c -> p k c", p=P)
        w_out = a["w_out"][0].rearrange("(k p) c -> p k c", p=P)
        w_pp = a["w_ple_proj"][0].rearrange("(k p) c -> p k c", p=P)
        w_pg = a["w_ple_gate"][0].rearrange("(k p) c -> p k c", p=P)
        wa = a["lru_wa"][0].rearrange("n c d -> c n d")
        wx = a["lru_wx"][0].rearrange("n c d -> c n d")
        st_in = a["state_ssd"].rearrange("l b h p n -> (l h p) b n")
        st_out = a["new_ssd_s"].rearrange("l b h p n -> (l h p) b n")
        stp_out = a["new_ssd_p"].rearrange("l b h p n -> (l b h p) n")

        BLOCKS = [(O_XS, 256), (O_XS + 128, 256), (O_B, 128), (O_C, 128), (O_LRU, 128),
                  (O_Z, 256), (O_Z + 128, 256), (O_LGATE, 128), (O_GA, 128), (O_GB, 128)]

        iota = cst[:, K_IOTA:K_IOTA + S].unsqueeze(1).to_broadcast([P, 3, S])

        def slot(t, i):
            return t[:, i, :].unsqueeze(2).to_broadcast([P, 3, S])

        def weigh_slots(eng, ch):
            ch(eng.tensor_tensor(pick[:], eA, eB, ALU.add))
            ch(eng.tensor_tensor(eA, eA, slot(wAB, 0), ALU.mult))
            ch(eng.tensor_tensor(eB, eB, slot(wAB, 1), ALU.mult))

        def branch_blocks(eng, split):
            with eng.Fori(0, 3) as i:
                for s in range(6):
                    split(i, s, (s + 2) % 6)
            for s in range(4):
                split(3, s, s + 2)

        block = ctx.enter_context(nc.Block())

        @block.sync
        def _(sp_):
            eng = nc.sync
            eng.dma_start(xrow[:, 0:2, :], a["x_prompt"][0].rearrange("(c p) d -> p c d", p=P)).then_inc(d_x, 16)
            eng.dma_start(xrow[0:NS, 2, :], a["x_sample"].rearrange("b t d -> (b t) d")).then_inc(d_x, 16)
            rows = {
                0: [("ssd_conv_w", "l k (c x) -> (l k c) x")],
                1: [("ssd_conv_b", "l (c x) -> (l c) x"), ("lru_conv_w", "l k (c x) -> (l k c) x"),
                    ("ssd_norm_g", "l (c x) -> (l c) x"), ("g_mix", "l (c x) -> (l c) x"), ("g_ffn", "l (c x) -> (l c) x"),
                    ("g_ple", "l (c x) -> (l c) x"), ("g_ple_gate", "l (c x) -> (l c) x"), ("g_final", "(c x) -> c x"),
                    ("lru_conv_b", "l (c x) -> (l c) x")],
                2: [("lru_ba", "l (c x) -> (l c) x"), ("lru_bx", "l (c x) -> (l c) x"), ("lru_lambda", "l (c x) -> (l c) x")],
            }
            for t, ps in rows.items():
                r = 0
                for name, pat in ps:
                    src = a[name].rearrange(pat, x=P)
                    n = src.shape[0]
                    eng.dma_start(prow[r:r + n, t, :], src).then_inc(d_par, 16)
                    r += n
            for i, name in enumerate(("ssd_dt_bias", "ssd_A_log", "ssd_D")):
                eng.dma_start(hc[:, i:i + 1], a[name].rearrange("l h -> h l")).then_inc(d_small, 16)
            eng.dma_start(wdt[:], w_in[:, :, O_DT:O_DT + H]).then_inc(d_wdt, 16)

            def load(s, dst, src):
                if nload[s] > 0:
                    sp_.wait_ge(used[s], nload[s])
                eng.dma_start(dst, src).then_inc(landed[s], 16)
                nload[s] += 1

            for s in range(10):
                o, w = BLOCKS[s]
                if s >= 5:
                    sp_.wait_ge(w_small_dve.sem, w_small_dve.at(0, s - 4))
                    sp_.wait_ge(w_small_pool.sem, w_small_pool.at(0, s - 4))
                eng.dma_start(wblk(s % 5), w_in[:, :, o:o + P]).then_inc(landed[s % 5], 16)
            eng.dma_start(wg[:, 0, :], wa[:, 0, :]).then_inc(gate_landed, 16)
            eng.dma_start(wg[:, 1, :], wx[:, 0, :]).then_inc(gate_landed, 16)
            eng.dma_start(rb[:, 0:4], a["b_router_g"]).then_inc(d_wr, 16)
            eng.dma_start(rb[:, 4:20], a["b_router_e"]).then_inc(d_wr, 16)
            eng.dma_start(wr[:, :, 0:4], a["w_router_g"][0].rearrange("(k p) c -> p k c", p=P)).then_inc(d_wr, 16)
            eng.dma_start(wr[:, :, 4:20], a["w_router_e"][0].rearrange("(k p) c -> p k c", p=P)).then_inc(d_wr, 16)
            sp_.sem_inc(state_out, 1)
            sp_.wait_ge(act_pro.sem, act_pro.at("dte"))
            sp_.wait_ge(dve_pro.sem, dve_pro.at("tm"))
            sp_.wait_ge(pe_pro.sem, pe_pro.at("tm"))
            for j in range(2):
                eng.dma_start(Sin[:, j], st_in[j * P:(j + 1) * P]).then_inc(sin_landed, 16)
            with sp_.Fori(1, G) as g:
                col1, col2, row2 = sp_.snap(g * 128), sp_.snap(g * 256), sp_.snap(g * 256 + P)
                for s in range(10):
                    o, w = BLOCKS[s]
                    col = {128: col1, 256: col2}[w]
                    sp_.wait_ge(w_small_dve.sem, w_small_dve.at(g, s - 4))
                    sp_.wait_ge(w_small_pool.sem, w_small_pool.at(g, s - 4))
                    if s == 4:
                        sp_.wait_ge(Y_ready.sem, Y_ready.at(g - 1, 1))
                        eng.dma_start(wg[:, 0, :], wa[:, ds(g, 1), :]).then_inc(gate_landed, 16)
                        eng.dma_start(wg[:, 1, :], wx[:, ds(g, 1), :]).then_inc(gate_landed, 16)
                    eng.dma_start(wblk(s % 5), w_in[:, :, ds(col + o, P)]).then_inc(landed[s % 5], 16)
                sp_.wait_ge(Y_free.sem, Y_free.at(g - 1, 3))
                for j in range(2):
                    eng.dma_start(Sin[:, j], st_in[ds((col2, row2)[j], P)]).then_inc(sin_landed, 16)
                eng.dma_start(stp_out[ds((g - 1) * 256, 256)].rearrange("(j q) n -> q j n", j=2), fin[:]).then_inc(state_out, 16)
                for j in range(2):
                    eng.dma_start(st_out[ds((g - 1) * 256 + j * P, P)], Snew[:, j]).then_inc(state_out, 16)
            def branch(j, o, free):
                for s, src in ((o, w_lru[:, :, ds(j * P, P)]), (o + 1, w_ssd[:, 0:8, ds(j * P, P)]),
                               (o + 2, w_ssd[:, 8:16, ds(j * P, P)])):
                    free(s)
                    eng.dma_start(wblk(s), src).then_inc(landed[s], 16)

            def last_step(s):
                if s < 5:
                    sp_.wait_ge(w_small_dve.sem, w_small_dve.at(G, s - 4))
                    sp_.wait_ge(w_small_pool.sem, w_small_pool.at(G, s - 4))

            branch(0, 0, last_step)
            branch(1, 3, last_step)
            sp_.wait_ge(Y_free.sem, Y_free.at(G - 1, 3))
            eng.dma_start(stp_out[7 * 256:8 * 256].rearrange("(j q) n -> q j n", j=2), fin[:]).then_inc(state_out, 16)
            for j in range(2):
                eng.dma_start(st_out[7 * 256 + j * P:7 * 256 + (j + 1) * P], Snew[:, j]).then_inc(state_out, 16)
            sp_.wait_ge(lru_tail.sem, lru_tail.at(G - 1, 1))
            sp_.wait_ge(state_out, 16 * 3 * G + 1)
            for s in range(6, 10):
                eng.dma_start(wblk(s), w_out[:, :, (s - 6) * P:(s - 5) * P]).then_inc(landed[s], 16)
            sp_.wait_ge(w_small_dve.sem, w_small_dve.at(G, 2))
            sp_.wait_ge(w_small_pool.sem, w_small_pool.at(G, 2))
            with sp_.Fori(1, 4) as i:
                def split_before(s):
                    sp_.wait_ge(b_small_dve.sem, b_small_dve.at(i, s + 1 - 6))
                    sp_.wait_ge(b_small_pool.sem, b_small_pool.at(i, s + 1 - 6))

                branch(2 * i, 0, split_before)
                branch(2 * i + 1, 3, split_before)
            nload[0:6], nload[6:10] = [0] * 6, [1] * 4
            for i in range(4):
                load(6 + i, wblk(6 + i), w_out[:, :, (4 + i) * P:(5 + i) * P])
            sp_.wait_ge(b_done.sem, b_done.at(3, 6))
            for c in range(2):
                eng.dma_start(plr[:, c, :], a["p_prompt"][0, 0, c * P:(c + 1) * P, :]).then_inc(d_plr, 16)
            eng.dma_start(plr[0:NS, 2, :], a["p_sample"][0].rearrange("b t d -> (b t) d")).then_inc(d_plr, 16)
            for i in range(2):
                load(10 + i, wblk(10 + i).rearrange("p a b -> p (a b)").rearrange("p (k c) -> p k c", k=2),
                     w_pp[:, :, i * 512:(i + 1) * 512])
            def expert_block(s, e):
                if s < 8:
                    w, b = (w1, w3)[s % 2], s // 2
                    return wflat(s).rearrange("p (k f) -> p k f", k=2), w[e, :, 2 * b:2 * b + 2, :]
                return wflat(s), w2[e, :, s - 8, :]
            for s in range(10):
                if s < 6:
                    sp_.wait_ge(b_small_dve.sem, b_small_dve.at(3, s + 1))
                    sp_.wait_ge(b_small_pool.sem, b_small_pool.at(3, s + 1))
                load(s, *expert_block(s, 0))
            for f in range(2, 4):
                sp_.wait_ge(pe_mid.sem, pe_mid.at(f"e{4 * f - 5}"))
                eng.dma_start(*expert_block(8 + f, 0)).then_inc(landed[8 + f], 16)
            assert nload[0:10] == [b + 1 for b in base_use[0:10]]
            sp_.wait_ge(dve_mid.sem, dve_mid.at("steps"))
            n_steps = sp_.value_load(steps[0:1, NE + XSTEPS:NE + XSTEPS + 1], min_val=NE, max_val=NE + XSTEPS)
            with sp_.Fori(1, n_steps) as q:
                e = sp_.value_load(steps[0:1, ds(q, 1)], min_val=0, max_val=NE - 1)
                for s in range(NBLK):
                    sp_.wait_ge(lo_dve.sem, lo_dve.at(q, s + 1 - NBLK))
                    sp_.wait_ge(lo_pool.sem, lo_pool.at(q, s + 1 - NBLK))
                    eng.dma_start(*expert_block(s, ds(e, 1))).then_inc(landed[s], 16)
            for i in range(8):
                sp_.wait_ge(lo_dve.sem, lo_dve.at(n_steps, i + 1 - NBLK))
                sp_.wait_ge(lo_pool.sem, lo_pool.at(n_steps, i + 1 - NBLK))
                eng.dma_start(wblk(i), w_pg[:, :, i * P:(i + 1) * P]).then_inc(landed[i], 16)
            sp_.wait_ge(act_mid.sem, act_mid.at("st"))
            eng.dma_start(a["new_ssd_conv_p"].rearrange("l b r (c x) -> (l b r c) x", x=P), orow[0:96, 0, :]).then_inc(d_out, 16)
            eng.dma_start(a["new_ssd_conv_s"].rearrange("l b r (c x) -> (l b r c) x", x=P).rearrange("(t q) x -> q t x", q=P),
                          orow[:, 1:7, :]).then_inc(d_out, 16)
            eng.dma_start(a["new_lru_conv_p"].rearrange("l b r (c x) -> (l b r c) x", x=P), orow[0:24, 7, :]).then_inc(d_out, 16)
            eng.dma_start(a["new_lru_conv_s"].rearrange("l b r (c x) -> (l b r c) x", x=P).rearrange("(t q) x -> q t x", q=96),
                          orow[0:96, 8:10, :]).then_inc(d_out, 16)
            eng.dma_start(a["new_lru_h_p"].rearrange("l b (c x) -> (l b c) x", x=P), lrowo[0:8, :]).then_inc(d_out, 16)
            eng.dma_start(a["new_lru_h_s"].rearrange("l b (c x) -> (l b c) x", x=P), lrowo[8:72, :]).then_inc(d_out, 16)
            sp_.wait_ge(dve_end.sem, dve_end.at("out5"))
            eng.dma_start(a["y_prompt"][0].rearrange("(c p) d -> p c d", p=P), yrow[:, 0:2, :]).then_inc(d_out, 16)
            eng.dma_start(a["y_sample"].rearrange("b t d -> (b t) d"), yrow[0:NS, 2, :]).then_inc(d_out, 16)
            sp_.wait_ge(d_out, 16 * 8)
            sp_.wait_ge(state_out, 16 * 3 * G + 1)

        @block.gpsimd
        def _(pool):
            eng = nc.gpsimd
            ch = Chain(pool, pool_ch)
            pool.sem_inc(stashed.sem, 5)
            pool.wait_ge(dve_pro.sem, dve_pro.at("tm"))
            pool.wait_ge(pe_pro.sem, pe_pro.at("tm"))
            def small(g, b):
                s = b % 10 % 5
                pool.wait_ge(w_large.sem, w_large.at(g, b + 1))
                eng.tensor_tensor(wlo[b % 2][:, WLOD:D], wflat(s)[:, WLOD:D], whi[b % 2][:, WLOD:D].bitcast(F32),
                                  ALU.subtract).then_inc(w_small_pool.sem, 1)

            small(0, 0)
            small(0, 1)
            with pool.Fori(0, G) as g:
                ch.enter(g, 5)
                for i, (src, at) in enumerate(((cstS, 2 * g), (cstS, 2 * g + 1), (cstS, g + 16), (cstS, g + 24), (cstL, g))):
                    pool.wait_ge(conv_done.sem, g * 5 + (i + 1))
                    pool.wait_ge(stashed.sem, g * 5 + (i + 1))
                    v = pads[i][:, SMP:PAD].rearrange("p (b r) -> p b r", r=7)[:, :, 0:3]
                    ch.tell(eng.tensor_copy(v, src[:, :, ds(at, 1)].rearrange("p (b r) o -> p b (r o)", r=3)), pad_hist, i + 1)
                pool.wait_ge(YO_ready.sem, YO_ready.at(g, 0))
                ch.tell(eng.tensor_tensor(Dg, cumT[:].unsqueeze(1).to_broadcast([H, 4, T]),
                                          cst[0:H, ds(g * 4, 4)].unsqueeze(2).to_broadcast([H, 4, T]), ALU.mult), dg_ready, 1)
                for i, (dst, at) in enumerate(((stS, 2 * g), (stS, 2 * g + 1), (stS, g + 16), (stS, g + 24), (stL, g))):
                    small(g, i + 2)
                    pool.wait_ge(proj_free.sem, proj_free.at(g, i + 1))
                    ch(eng.tensor_copy(dst[:, 0:3, ds(at, 1)].rearrange("p r o -> p (r o)"), pads[i][:, NP:NP + 3]))
                    v = pads[i][:, SMP:PAD].rearrange("p (b r) -> p b r", r=7)[:, :, 4:7]
                    ch.tell(eng.tensor_copy(dst[:, 3:27, ds(at, 1)].rearrange("p (b r) o -> p b (r o)", r=3), v), stashed, i + 1)
                small(g, 7)
                for c, (t0, n) in enumerate(TOK):
                    if c == 0:
                        pool.wait_ge(CU_free.sem, CU_free.at(g, 1))
                    else:
                        pool.wait_ge(diff_ready.sem, diff_ready.at(g, c))
                    t = tw[:, c, :] if c < 2 else tws[:]
                    m = cst[0:n, K_NEG:K_NEG + P] if c < 2 else cst[0:n, K_NEGS:K_NEGS + NS]
                    t4 = t.rearrange("p (h q) -> p h q", h=4)
                    ch.tell(eng.tensor_tensor(t4, t4, m.unsqueeze(1).to_broadcast([n, 4, n]), ALU.add), masked, c + 1)
                    pool.wait_ge(T_free.sem, T_free.at(g, c + 1))
                    ch.tell(eng.tensor_tensor(xdte[0:n, c, :].rearrange("p (h e) -> p h e", h=4),
                                              xdt[0:n, c, :].rearrange("p (h e) -> p h e", h=4),
                                              TM[0:n, 2, c, ds(g * 4, 4)].unsqueeze(2).to_broadcast([n, 4, 64]), ALU.mult),
                            xdte_ready, c + 1)
                    if c > 0:
                        small(g, 7 + c)
                ch.tell(eng.tensor_tensor(Bm, btok[0:NS, 2, :].unsqueeze(1).to_broadcast([NS, NB, P]),
                                          cst[0:NS, K_BM:K_BM + NB].unsqueeze(2).to_broadcast([NS, NB, P]), ALU.mult), bm_ready, 1)
                small(g, 10)
                pool.wait_ge(CU_free.sem, CU_free.at(g, 3))
                for j in range(2):
                    pool.wait_ge(sin_landed, g * 32 + 32)
                    if j == 0:
                        pool.wait_ge(state_out, g * 48 + 1)
                    dec = ex[:, j, P + NT - 1:P + NS:NT]
                    ch.tell(eng.tensor_tensor(Snew[:, j], Sin[:, j], dec.unsqueeze(2).to_broadcast([P, NB, P]), ALU.mult), sdec_ready, j + 1)
                small(g, 11)
            ch.leave(G)

            def branch_small(i, s, slot):
                pool.wait_ge(b_large.sem, b_large.at(i, s + 3))
                eng.tensor_tensor(wlo[s % 2][:, LOD:D], wflat(slot)[:, LOD:D], whi[s % 2][:, LOD:D].bitcast(F32),
                                  ALU.subtract).then_inc(b_small_pool.sem, 1)

            pool.sem_inc(b_small_pool.sem, 6 + 2)
            branch_blocks(pool, branch_small)

            pool.wait_ge(dve_mid.sem, dve_mid.at("pick0"))
            n_steps = pool.value_load(steps[0:1, NE + XSTEPS:NE + XSTEPS + 1], min_val=NE, max_val=NE + XSTEPS)
            ch2 = Chain(pool, pool_ch2)
            pool.sem_inc(lo_pool.sem, NBLK)
            with pool.Fori(0, n_steps) as q:
                ch2.enter(q, 3)

                def small(s):
                    pool.wait_ge(hi_ready.sem, hi_ready.at(q, s + 1))
                    eng.tensor_tensor(wlo[s % R][:, LOD:D], wflat(s)[:, LOD:D], whi[s % R][:, LOD:D].bitcast(F32),
                                      ALU.subtract).then_inc(lo_pool.sem, 1)

                for s in range(10):
                    small(s)
                pool.wait_ge(xb_gathered.sem, xb_gathered.at(q, 1))
                pool.wait_ge(eq_ready.sem, eq_ready.at(q, 1))
                weigh_slots(eng, ch2)
                ch2.tell(eng.tensor_tensor(eW, eA, eB, ALU.add), pick_ready, 2)
                small(10)
                small(11)
            ch2.leave(0)
            for s in range(8):
                pool.wait_ge(hi_ready.sem, hi_ready.at(n_steps, s + 1))
                eng.tensor_tensor(wlo[s % R][:, LOD:D], wflat(s)[:, LOD:D], whi[s % R][:, LOD:D].bitcast(F32),
                                  ALU.subtract).then_inc(lo_pool.sem, 1)

        @block.scalar
        def _(act):
            eng = nc.scalar
            ch = Chain(act, act_ch)
            act_f = eng.activation
            q = nc.scalar
            q.dma_start(cst[:], a["constants"]).then_inc(d_cst, 16)
            q.dma_start(srow, a["state_ssd_conv"].rearrange("l b r (c x) -> (l b r c) x", x=P).rearrange("(t q) x -> q t x", q=P)).then_inc(d_row, 16)
            q.dma_start(lrow[0:96], a["state_lru_conv"].rearrange("l b r (c x) -> (l b r c) x", x=P).rearrange("(t q) x -> q t x", q=96)).then_inc(d_row, 16)
            q.dma_start(hrow[0:64], a["state_lru_h"].rearrange("l b (c x) -> (l b c) x", x=P)).then_inc(d_row, 16)
            for k in range(KC):
                act.wait_ge(dve_pro.sem, dve_pro.at(f"x{k}"))
                act_f(sq[:, k, :], xT[:, k, :], ACT.Square).then_inc(act_pro.sem, 1)
            act.wait_ge(pe_pro.sem, pe_pro.at("rms"))
            ch(act_f(rsP[:], bCB[:, 0:T], ACT.Ln, bias=EPS, scale=1.0 / D))
            ch.step(act_f(rsP[:], rsP[:], ACT.Exp, scale=-0.5), act_pro, "rs")
            act.wait_ge(d_small, 48)
            ch.step(act_f(Acol, hc[:, 1:2], ACT.Exp), act_pro, "A")
            for k in range(KC):
                act.wait_ge(dve_pro.sem, dve_pro.at(f"hT{k}"))
                act_f(h_hi[:, k, :], ya[:, k, :], ACT.Copy).then_inc(act_pro.sem, 1)

            def large(g, b):
                act.wait_ge(landed[b % 10 % 5], g * 32 + 16 * (1 + b // 5))
                act_f(whi[b % 2][:], wflat(b % 10 % 5), ACT.Copy).then_inc(w_large.sem, 1)

            large(0, 0)
            large(0, 1)
            act.wait_ge(dve_pro.sem, dve_pro.at("ax"))
            ch.step(act_f(sp[2], sp[1], ACT.Exp, scale=-1.0), act_pro, "z")
            act.wait_ge(dve_pro.sem, dve_pro.at("u"))
            ch.step(act_f(sp[4], sp[3], ACT.Ln), act_pro, "ln")
            act.wait_ge(dve_pro.sem, dve_pro.at("dteT"))
            ch.step(act_f(dteT, dteT, ACT.Exp), act_pro, "dte")

            act.sem_inc(proj_free.sem, 2)
            act.sem_inc(silu_done.sem, 4)
            act.sem_inc(T_free.sem, 1)
            act.sem_inc(CB_free.sem, 1)

            def samples(v):
                return v.rearrange("p (b t) -> p b t", t=NT)

            def new_tokens(v, r0):
                return v[:, SMP:PAD].rearrange("p (b r) -> p b r", r=7)[:, :, r0:r0 + NT]

            with act.Fori(0, G) as g:
                ch.enter(g, 11)

                def evac(i):
                    act.wait_ge(projected.sem, projected.at(g, i + 1))
                    large(g, i + 2)
                    act.wait_ge(conv_done.sem, conv_done.at(g, i + 1 - 5))
                    act.wait_ge(stashed.sem, stashed.at(g, i + 1 - 5))
                    ch(act_f(pads[i][:, 3:SMP], bP[i % 2][:, 0:NP], ACT.Copy))
                    ch.tell(act_f(new_tokens(pads[i], 3), samples(bP[i % 2][:, NP:T]), ACT.Copy), proj_free, i + 1)

                def silu(i):
                    act.wait_ge(conv_done.sem, conv_done.at(g, i + 1))
                    ch(act_f(xbc[i][:, 0:NP], cv[i % 2][:, 0:NP], ACT.Silu))
                    ch.tell(act_f(samples(xbc[i][:, NP:T]), new_tokens(cv[i % 2], 0), ACT.Silu), silu_done, i + 1)

                def decay(c):
                    act.wait_ge(masked.sem, masked.at(g, c + 1))
                    t = tw[:, c, :] if c < 2 else tws[:]
                    ch.tell(act_f(t, t, ACT.Exp), decay_ready, c + 1)

                def raw(i, dst):
                    act.wait_ge(projected.sem, projected.at(g, i + 1))
                    large(g, i + 2)
                    ch.tell(act_f(dst, bP[i % 2][:, 0:T], ACT.Copy), proj_free, i + 1)

                def from_T(k, dst, n):
                    act.wait_ge(T_ready.sem, T_ready.at(g, k))
                    ch.tell(act_f(dst, bT[:, 0:n], ACT.Copy), T_free, k)

                evac(0)
                evac(1)
                act.wait_ge(YO_ready.sem, YO_ready.at(g, 0))
                act.wait_ge(y_done.sem, y_done.at(g, 0))
                silu(0)
                evac(2)
                silu(1)
                evac(3)
                silu(2)
                evac(4)
                silu(3)
                for j in range(2):
                    act.wait_ge(projected.sem, projected.at(g, 6 + j))
                    large(g, 7 + j)
                    if j == 0:
                        act.wait_ge(lru_tail.sem, lru_tail.at(g, 0))
                    ch.tell(act_f(zs[:, j, :], bP[(5 + j) % 2][:, 0:T], ACT.Silu), proj_free, 6 + j)
                act.wait_ge(Y_ready.sem, Y_ready.at(g, 1))
                ch(act_f(rr[:], bY[0][:, 0:T], ACT.Sigmoid, bias=par[:, ds(g + C_BA, 1)]))
                ch.tell(act_f(ii[:], bY[1][:, 0:T], ACT.Sigmoid, bias=par[:, ds(g + C_BX, 1)]), Y_free, 1)
                ch(act_f(TT[:], rr[:], ACT.Tanh, scale=kc2[:, 1, ds(g, 1)]))
                ch.tell(act_f(aS[:], rr[:], ACT.Exp, scale=kc2[:, 0, ds(g, 1)]), lru_act, 1)
                def decay_rows(c):
                    n = TOK[c][1]
                    act.wait_ge(diff_ready.sem, diff_ready.at(g, c))
                    for h in range(2):
                        p = slice(64 * h, 64 * h + 64)
                        ins = act_f(ex[p, :, P * (c - 1):P * (c - 1) + n],
                                    bCU[p, 0:4 * n].rearrange("p (j h q) -> p j h q", j=2, h=2)[:, :, h, :], ACT.Exp)
                    ch.tell(ins, CU_free, c + 1)

                decay(0)
                decay_rows(1)
                decay(1)
                raw(7, gl[:])
                decay_rows(2)
                decay(2)
                act.wait_ge(m2_ready.sem, m2_ready.at(g, 1))
                ch.tell(act_f(TT[:], TT[:], ACT.Sqrt), m_ready, 1)
                raw(8, ga[:, ds(g, 1), :].rearrange("p o t -> p (o t)"))
                from_T(4, sprev[:], 256)
                from_T(5, sT[:, 0:4, :].rearrange("p b n -> p (b n)"), 512)
                from_T(6, sT[:, 4:8, :].rearrange("p b n -> p (b n)"), 512)
                from_T(7, sT[:, 0:4, :].rearrange("p b n -> p (b n)"), 512)
                from_T(8, sT[:, 4:8, :].rearrange("p b n -> p (b n)"), 512)
                raw(9, gb[:, ds(g, 1), :].rearrange("p o t -> p (o t)"))
                act.wait_ge(y_done.sem, y_done.at(g, 1))
                ch.tell(act_f(tw[:, :, 0:T], yb[:, ds(2 * g, 2), :], ACT.Square), sq_ready, 1)
                act.wait_ge(CB_ready.sem, CB_ready.at(g, 2))
                ch.tell(act_f(zs[:, 0, :], bCB[:, 0:T], ACT.Sqrt, bias=EPS, scale=1.0 / 256), CB_free, 1)
                ch.tell(act_f(gl[:], gl[:], ACT.Gelu_apprx_tanh), gelu_ready, 1)
            ch.leave(G)

            act_f(ga[:], ga[:], ACT.Sigmoid).then_inc(gates_ready, 1)
            act.wait_ge(lru_tail.sem, lru_tail.at(G - 1, 1))
            for t in range(6):
                src = ya[:, 4 * t:4 * t + 4, :] if t < 2 else yb[:, 4 * t - 8:4 * t - 4, :]
                act_f(br_hi[:, 4 * t:4 * t + 4, :], src, ACT.Copy).then_inc(br_large.sem, 1)
            act.sem_inc(b_large.sem, 6 + 2)
            act_f(gb[:], gb[:], ACT.Sigmoid).then_inc(gates_ready, 1)

            def branch_large(i, s, slot):
                act.wait_ge(landed[slot], i * 16 + 16 * (2 * G * (slot < 5) + (s + 2) // 6 + 1))
                act.wait_ge(b_done.sem, b_done.at(i, s + 1))
                act_f(whi[s % 2][:], wflat(slot), ACT.Copy).then_inc(b_large.sem, 1)

            branch_blocks(act, branch_large)
            act.wait_ge(gates_ready, 2)
            for j in range(8):
                act.wait_ge(dve_mid.sem, dve_mid.at(f"x2_{j}"))
                ch.step(act_f(sq[:, j, :], xT[:, j, :], ACT.Square), act_mid, f"sqf{j}")
            act.wait_ge(pe_mid.sem, pe_mid.at("st"))
            act.wait_ge(state_out, 16 * 3 * G + 1)
            ch(act_f(orow[0:96, 0, :], bT[0:96, 0:P], ACT.Copy))
            ch(act_f(orow[:, 1:4, :].rearrange("p c n -> p (c n)"), bT[:, P:512], ACT.Copy))
            ch(act_f(orow[:, 4:7, :].rearrange("p c n -> p (c n)"), bCB[:, 0:384], ACT.Copy))
            ch(act_f(orow[0:24, 7, :], bCB[0:24, 384:512], ACT.Copy))
            ch(act_f(orow[0:96, 8:10, :].rearrange("p c n -> p (c n)"), bCU[0:96, 0:256], ACT.Copy))
            ch.step(act_f(lrowo[0:72], bCU[0:72, 256:384], ACT.Copy), act_mid, "st")
            act.wait_ge(pe_mid.sem, pe_mid.at("pT"))
            ch(act_f(pT[:, 0, :], bY[0][:, 0:T], ACT.Copy))
            ch.step(act_f(pT[:, 1, :], bY[1][:, 0:T], ACT.Copy), act_mid, "pT")
            act.wait_ge(pe_mid.sem, pe_mid.at("frms"))
            ch(act_f(rs, bP[0][:, 0:T], ACT.Ln, bias=EPS, scale=1.0 / D))
            ch.step(act_f(rs, rs, ACT.Exp, scale=-0.5), act_mid, "frs")
            for j in range(8):
                act.wait_ge(pe_mid.sem, pe_mid.at(f"e{j}"))
                ch(act_f(eT[:, j, :], R4[j % 4][:, 0:T], ACT.Copy))
                ch.step(act_f(sq[:, j, :], R4[j % 4][:, 0:T], ACT.Square), act_mid, f"e{j}")
            act.wait_ge(pe_mid.sem, pe_mid.at("erms"))
            ch(act_f(rs2, bP[1][:, 0:T], ACT.Ln, bias=EPS, scale=1.0 / D))
            ch.step(act_f(rs2, rs2, ACT.Exp, scale=-0.5), act_mid, "ers")
            def hi(i):
                c, hf = i // 2, i % 2
                n = TOK[c][1]
                act.wait_ge(pe_mid.sem, pe_mid.at(f"ht{i}"))
                ch.step(act_f(htok_hi[0:n, c, 512 * hf:512 * hf + 512], R4[i % 4][0:n, :], ACT.Copy), act_mid, f"hi{i}")
            hi(0)
            hi(1)
            act.wait_ge(dve_mid.sem, dve_mid.at("gsub"))
            ch.step(act_f(r_gs, r_gs, ACT.Exp), act_mid, "gexp")
            act.wait_ge(dve_mid.sem, dve_mid.at("esub"))
            ch.step(act_f(r_es, r_es, ACT.Exp), act_mid, "eexp")
            for i in range(2, 6):
                hi(i)
            act.wait_ge(dve_mid.sem, dve_mid.at("steps"))
            n_steps = act.value_load(steps[0:1, NE + XSTEPS:NE + XSTEPS + 1], min_val=NE, max_val=NE + XSTEPS)

            def slots_out(q, k, hf):
                act.wait_ge((xa_gathered, xb_gathered)[hf].sem, xa_gathered.at(q, k))
                act_f(xs[0:S, 512 * hf:512 * hf + 512], bY[hf][0:S, :], ACT.Copy).then_inc((xs0_out, xs1_out)[hf].sem, 1)

            def tokens_hi(q, k):
                act.wait_ge(xt_ready.sem, xt_ready.at(q, k))
                act_f(x_hl[:, :, 0, :], bX[:, :].rearrange("p (k s) -> p k s", k=KC), ACT.Copy).then_inc(xhi_ready.sem, 1)

            def results_hi(q):
                act.wait_ge(hl_free.sem, hl_free.at(q, 0))
                act.wait_ge(ws_done.sem, ws_done.at(q, 0))
                act.wait_ge(cmb_ready.sem, cmb_ready.at(q, 0))
                for hf in range(2):
                    act_f(y_hi[:, 512 * hf:512 * hf + 512], bY[hf][:, :], ACT.Copy, scale=ws[:, 0:1]).then_inc(yhi_ready.sem, 1)

            slots_out(0, 0, 0)
            slots_out(0, 0, 1)
            tokens_hi(0, 0)
            act.wait_ge(dve_mid.sem, dve_mid.at("pick0"))
            ch(act_f(sgq[:, 0:1], wAB[:, 0, 0:1], ACT.Silu))
            with act.Fori(0, n_steps) as q:
                def large(s):
                    act.wait_ge(landed[s], q * 16 + 16 * (base_land[s] + 1))
                    act.wait_ge(hl_free.sem, hl_free.at(q, s + 1 - R))
                    act_f(whi[s % R][:], wflat(s), ACT.Copy).then_inc(hi_ready.sem, 1)

                large(0)
                large(1)
                results_hi(q)
                for s in range(2, 8):
                    large(s)
                act.wait_ge(hl_free.sem, hl_free.at(q, 7))
                act_f(Gs[:, 0:512], bG1[:, :], ACT.Copy).then_inc(g1_out.sem, 1)
                act.wait_ge(hl_free.sem, hl_free.at(q, 8))
                act_f(Gs[:, 512:1024], bG3[:, :], ACT.Copy).then_inc(g3_out.sem, 1)
                large(8)
                slots_out(q, 1, 0)
                large(9)
                act.wait_ge(gt_ready.sem, gt_ready.at(q, 1))
                act_f(sgq, bGT[:, 0:256], ACT.Silu).then_inc(silu_e.sem, 1)
                slots_out(q, 1, 1)
                large(10)
                tokens_hi(q, 1)
                large(11)
            results_hi(n_steps)

            def gate_large(s):
                act.wait_ge(landed[s], n_steps * 16 + 16 * (base_land[s] + 1))
                act.wait_ge(hl_free.sem, hl_free.at(n_steps, s + 1 - R))
                act_f(whi[s % R][:], wflat(s), ACT.Copy).then_inc(hi_ready.sem, 1)

            for s in range(R):
                gate_large(s)
            ch = Chain(act, act_ch2)
            for j in range(8):
                act.wait_ge(dve_end.sem, dve_end.at(f"x3_{j}"))
                ch.step(act_f(sq[:, j, :], xT[:, j, :], ACT.Square), act_end, f"sg{j}")
            act.wait_ge(pe_end.sem, pe_end.at("grms"))
            ch(act_f(rs, bP[0][:, 0:T], ACT.Ln, bias=EPS, scale=1.0 / D))
            ch.step(act_f(rs, rs, ACT.Exp, scale=-0.5), act_end, "grs")

            def square_x4(j):
                act.wait_ge(dve_end.sem, dve_end.at(f"x4_{j}"))
                ch.step(act_f(sq[:, j, :], xT[:, j, :], ACT.Square), act_end, f"sy{j}")

            for k in range(KC):
                act.wait_ge(dve_end.sem, dve_end.at(f"hg{k}"))
                act_f(hg_hi[:, k, :], hT[:, k, :], ACT.Copy).then_inc(act_end.sem, 1)
            for j in range(8):
                act.wait_ge(hl_free.sem, hl_free.at(n_steps, j + 1))
                if j >= 2:
                    act.wait_ge(dve_end.sem, dve_end.at(f"x4_{j - 2}"))
                ch.step(act_f(sg[j % 2], R4[j % 4][:, 0:T], ACT.Sigmoid), act_end, f"sig{j}")
                if j + R < 8:
                    gate_large(j + R)
                if j >= 1:
                    square_x4(j - 1)
            square_x4(7)
            act.wait_ge(pe_end.sem, pe_end.at("yrms"))
            ch(act_f(rs, bP[1][:, 0:T], ACT.Ln, bias=EPS, scale=1.0 / D))
            ch.step(act_f(rs, rs, ACT.Exp, scale=-0.5), act_end, "yrs")

        @block.vector
        def _(dve):
            v = nc.vector
            ch = Chain(dve, dve_ch)
            for k in range(KC):
                dve.wait_ge(pe_pro.sem, pe_pro.at(f"x{k}"))
                v.tensor_copy(xT[:, k, :], bank[XB[k]][:, 0:T]).then_inc(dve_pro.sem, 1)
            dve.wait_ge(pe_pro.sem, pe_pro.at("par"))
            ch.step(v.tensor_copy(par[:], bank[4][:, 0:C_END]), dve_pro, "par")
            for i in range(5):
                ch(v.memset(pads[i][:, 0:3], 0.0))
            ch(v.memset(sp[0], 0.0))
            dve.wait_ge(pe_pro.sem, pe_pro.at("hist"))
            cs = cstS[:].rearrange("p a b -> p (a b)")
            ch(v.tensor_copy(cs[:, 0:512], bank[1][:, :]))
            ch(v.tensor_copy(cs[:, 512:768], bank[2][:, 0:256]))
            ch(v.tensor_copy(cstL[:].rearrange("p a b -> p (a b)"), bank[2][:, 256:448]))
            ch.step(v.tensor_copy(h0T[:].rearrange("p a b -> p (a b)"), bank[2][:, 448:512]), dve_pro, "hist")

            def norm(dst, src, col, r, steps, name):
                for k in range(KC):
                    v.scalar_tensor_tensor(out=dst[:, k, :], in0=src[:, k, :], scalar=par[:, col + k:col + k + 1],
                                           in1=r, op0=ALU.mult, op1=ALU.mult).then_inc(steps.sem, 1)
                assert steps.at(f"{name}{KC - 1}") == steps.at(f"{name}0") + KC - 1

            dve.wait_ge(act_pro.sem, act_pro.at("rs"))
            norm(ya, xT, C_GMIX, rsP[:], dve_pro, "hT")
            for k in range(KC):
                dve.wait_ge(act_pro.sem, act_pro.at(f"hh{k}"))
                ins = v.tensor_tensor(h_lo[:, k, :], ya[:, k, :], h_hi[:, k, :].bitcast(F32), ALU.subtract)
            ch.step(ins, dve_pro, "hl")

            def small(g, b):
                s = b % 10 % 5
                dve.wait_ge(w_large.sem, w_large.at(g, b + 1))
                v.tensor_tensor(wlo[b % 2][:, 0:WLOD], wflat(s)[:, 0:WLOD], whi[b % 2][:, 0:WLOD].bitcast(F32),
                                ALU.subtract).then_inc(w_small_dve.sem, 1)

            small(0, 0)
            small(0, 1)
            dve.wait_ge(pe_pro.sem, pe_pro.at("dt"))
            dve.wait_ge(d_small, 48)
            ch(v.tensor_scalar(sp[0][0:H, 0:T], bank[4][0:H, 0:T], hc[:, 0:1], None, ALU.add))
            ch(v.tensor_scalar(sp[0][:, T:T + 8], par[:, C_LAM:C_LAM + 8], -1.0, None, ALU.mult))
            ch.step(v.scalar_tensor_tensor(out=sp[1], in0=sp[0], scalar=-1.0, in1=sp[0], op0=ALU.mult, op1=ALU.max), dve_pro, "ax")
            dve.wait_ge(act_pro.sem, act_pro.at("z"))
            ch.step(v.tensor_scalar(sp[3], sp[2], 1.0, None, ALU.add), dve_pro, "u")
            dve.wait_ge(act_pro.sem, act_pro.at("ln"))
            ch(v.tensor_scalar(sp[3], sp[3], -1.0, 1e-30, ALU.add, ALU.add))
            ch(v.reciprocal(sp[3], sp[3]))
            ch(v.scalar_tensor_tensor(out=sp[4], in0=sp[4], scalar=1e-30, in1=sp[3], op0=ALU.add, op1=ALU.mult))
            ch(v.tensor_tensor(sp[4], sp[4], sp[2], ALU.mult))
            ch.step(v.scalar_tensor_tensor(out=sp[0], in0=sp[0], scalar=0.0, in1=sp[4], op0=ALU.max, op1=ALU.add), dve_pro, "soft")
            ch(v.tensor_scalar(kc2[:, 0, :], sp[0][:, T:T + 8], -8.0, None, ALU.mult))
            ch(v.tensor_scalar(kc2[:, 1, :], sp[0][:, T:T + 8], 8.0, None, ALU.mult))
            dve.wait_ge(act_pro.sem, act_pro.at("A"))
            ch.step(v.tensor_scalar(aT, sp[0][0:H, 0:T], Acol, -1.0, ALU.mult, ALU.mult), dve_pro, "aT")
            dve.wait_ge(pe_pro.sem, pe_pro.at("atok"))
            ch(v.tensor_copy(Dt[:], bank[5][:, P:P + 16]))
            ch(v.tensor_copy(atok[:, 0:2, :].rearrange("p c h -> p (c h)"), bank[5][:, 0:2 * H]))
            ch.step(v.tensor_copy(atok[0:NS, 2, :], bank[5][0:NS, 2 * H:3 * H]), dve_pro, "atok")
            dve.wait_ge(pe_pro.sem, pe_pro.at("cum"))
            ch.step(v.tensor_copy(cumT[:], bank[6][0:H, 0:T]), dve_pro, "cum")
            for c in range(QC):
                ch(v.tensor_scalar(dteT[:, c * P:(c + 1) * P], cumT[:, c * P:(c + 1) * P], -1.0,
                                   cumT[:, (c + 1) * P - 1:(c + 1) * P], ALU.mult, ALU.add))
            ct = cumT[:, NP:T].rearrange("p (b t) -> p b t", t=NT)
            ch.step(v.tensor_tensor(dteT[:, NP:T].rearrange("p (b t) -> p b t", t=NT), ct[:, :, NT - 1:NT].to_broadcast([H, NB, NT]),
                                    ct, ALU.subtract), dve_pro, "dteT")
            dve.wait_ge(pe_pro.sem, pe_pro.at("tm"))
            tmb = bank[7][:, 0:9 * H].rearrange("p (k c h) -> p k c h", k=3, c=3)
            ch(v.tensor_copy(TM[:, :, 0:2, :].rearrange("p k c h -> p k (c h)"), tmb[:, :, 0:2, :].rearrange("p k c h -> p k (c h)")))
            ch.step(v.tensor_copy(TM[0:NS, :, 2, :], tmb[0:NS, :, 2, :]), dve_pro, "tm")
            dve.sem_inc(conv_done.sem, 5)
            dve.sem_inc(y_done.sem, 1)
            dve.sem_inc(CU_free.sem, 1)
            dve.sem_inc(Y_free.sem, 1)
            dve.sem_inc(YO_free.sem, 1)
            dve.sem_inc(lru_tail.sem, 1)

            def new_tokens(w):
                return w[:, SMP:PAD].rearrange("p (b r) -> p b r", r=7)[:, :, 0:NT]

            def samples(w):
                return w.rearrange("p (b t) -> p b t", t=NT)

            with dve.Fori(0, G) as g:
                ch.enter(g, 38)

                def conv(i, wcol, stride, bcol, at):
                    dve.wait_ge(proj_free.sem, proj_free.at(g, i + 1))
                    dve.wait_ge(pad_hist.sem, pad_hist.at(g, i + 1))
                    dve.wait_ge(silu_done.sem, silu_done.at(g, i - 1))
                    x, y = pads[i], cv[i % 2]
                    w = lambda k: par[:, ds(at + (wcol + k * stride), 1)]
                    ch(v.tensor_scalar(y[:, 0:CVW], x[:, 0:CVW], w(0), par[:, ds(at + bcol, 1)], ALU.mult, ALU.add))
                    for k in (1, 2):
                        ch(v.scalar_tensor_tensor(out=y[:, 0:CVW], in0=x[:, k:k + CVW], scalar=w(k), in1=y[:, 0:CVW],
                                                  op0=ALU.mult, op1=ALU.add))
                    if i < 4:
                        ch.tell(v.scalar_tensor_tensor(out=y[:, 0:CVW], in0=x[:, 3:3 + CVW], scalar=w(3), in1=y[:, 0:CVW],
                                                       op0=ALU.mult, op1=ALU.add), conv_done, i + 1)
                    else:
                        ch(v.scalar_tensor_tensor(out=u[:, 0:NP], in0=x[:, 3:3 + NP], scalar=w(3), in1=y[:, 0:NP],
                                                  op0=ALU.mult, op1=ALU.add))
                        xs_ = x[:, SMP:PAD].rearrange("p (b r) -> p b r", r=7)[:, :, 3:7]
                        ch.tell(v.scalar_tensor_tensor(out=samples(u[:, NP:T]), in0=xs_, scalar=w(3), in1=new_tokens(y),
                                                       op0=ALU.mult, op1=ALU.add), conv_done, i + 1)

                def tokens(c):
                    n = TOK[c][1]
                    dve.wait_ge(T_ready.sem, T_ready.at(g, c + 1))
                    ch(v.tensor_tensor(xdt[0:n, c, :].rearrange("p (h e) -> p h e", h=4), bT[0:n, 0:256].rearrange("p (h e) -> p h e", h=4),
                                       TM[0:n, 0, c, ds(g * 4, 4)].unsqueeze(2).to_broadcast([n, 4, 64]), ALU.mult))
                    ch.tell(v.tensor_copy(btok[0:n, c, :], bT[0:n, 256:384]), T_free, c + 1)

                def diff(c):
                    n = TOK[c][1]
                    t = tw[:, c, :] if c < 2 else tws[:]
                    dve.wait_ge(CU_ready.sem, CU_ready.at(g, c + 1))
                    ins = v.tensor_tensor(t.rearrange("p (h q) -> p h q", h=4), bCU[0:n, 0:4 * n].rearrange("p (h q) -> p h q", h=4),
                                          TM[0:n, 1, c, ds(g * 4, 4)].unsqueeze(2).to_broadcast([n, 4, n]), ALU.subtract)
                    ch.tell(ins, CU_free, 1) if c == 0 else ch.tell(ins, diff_ready, c)

                def weights(c):
                    t0, n = TOK[c]
                    t = tw[:, c, :] if c < 2 else tws[:]
                    dve.wait_ge(decay_ready.sem, decay_ready.at(g, c + 1))
                    dve.wait_ge(CB_ready.sem, CB_ready.at(g, 1))
                    t4 = t.rearrange("p (h q) -> p h q", h=4)
                    ch.tell(v.tensor_tensor(t4, t4, bCB[0:n, t0:t0 + n].unsqueeze(1).to_broadcast([n, 4, n]), ALU.mult), W_ready, c + 1)

                small(g, 2)
                conv(0, C_SW, 32, C_SB, 2 * g)
                small(g, 3)
                conv(1, C_SW, 32, C_SB, 2 * g + 1)
                small(g, 4)
                conv(2, C_SW, 32, C_SB, g + 16)
                small(g, 5)
                conv(3, C_SW, 32, C_SB, g + 24)
                small(g, 6)
                conv(4, C_LW, 8, C_LB, g)
                small(g, 7)
                tokens(0)
                diff(0)
                small(g, 8)
                tokens(1)
                diff(1)
                dve.wait_ge(lru_act.sem, lru_act.at(g, 1))
                ch(v.tensor_tensor(rr[:], aS[:], aS[:], ALU.mult))
                ch.tell(v.scalar_tensor_tensor(out=TT[:], in0=rr[:], scalar=1.0, in1=TT[:], op0=ALU.add, op1=ALU.mult), m2_ready, 1)
                weights(0)
                weights(1)
                tokens(2)
                diff(2)
                weights(2)
                small(g, 9)
                dve.wait_ge(m_ready.sem, m_ready.at(g, 1))
                ch(v.memset(TT[:, 0:1], 1.0))
                ch(v.tensor_tensor(ii[:], ii[:], u[:], ALU.mult))
                ch(v.tensor_tensor(ii[:], ii[:], TT[:], ALU.mult))
                h0 = h0T[:, :, ds(g, 1)].rearrange("p b o -> p (b o)")
                ch(v.tensor_tensor(rr[:, 0:NB], aS[:, NP:T:NT], h0, ALU.mult))
                ch(v.tensor_tensor(ii[:, NP:T:NT], ii[:, NP:T:NT], rr[:, 0:NB], ALU.add))
                ch(v.memset(aS[:, 0:1], 0.0))
                ch(v.memset(aS[:, NP:T:NT], 0.0))
                ch(v.tensor_tensor_scan(rr[:], aS[:], ii[:], 0.0, ALU.mult, ALU.add))
                dve.wait_ge(Y_ready.sem, Y_ready.at(g, 2))
                for j in range(2):
                    ins = v.scalar_tensor_tensor(out=yb[:, ds(2 * g + j, 1), :].rearrange("p o t -> p (o t)"), in0=xbc[j][:],
                                                 scalar=Dt[:, ds(2 * g + j, 1)],
                                                 in1=bY[j][:, 0:T], op0=ALU.mult, op1=ALU.add)
                    ch(ins) if j == 0 else ch.tell(ins, Y_free, 2)
                small(g, 10)
                dve.wait_ge(CU_ready.sem, CU_ready.at(g, 4))
                dve.wait_ge(state_out, g * 48 + 1)
                for j in range(2):
                    ch(v.tensor_scalar(fin[:, j, :], bCU[:, 256 * j:256 * j + P],
                                       ex[:, j, P - 1:P], None, ALU.mult))
                    ins = v.tensor_tensor(fin[:, j, :], fin[:, j, :], bCU[:, 256 * j + P:256 * j + 2 * P], ALU.add)
                    ch(ins) if j == 0 else ch.tell(ins, CU_free, 4)

                def new_states(k):
                    j, hf = k // 2, k % 2
                    b, ready, free, n = SN[k]
                    dve.wait_ge(ready.sem, ready.at(g, n))
                    dve.wait_ge(sdec_ready.sem, sdec_ready.at(g, j + 1))
                    t = Snew[:, j, 4 * hf:4 * hf + 4, :].rearrange("p b n -> p (b n)")
                    ch.tell(v.tensor_tensor(t, t, b[:, :], ALU.add), free, n)

                new_states(0)
                dve.wait_ge(YO_ready.sem, YO_ready.at(g, 1))
                ch.tell(v.tensor_tensor(yot, bYO[:, 0:320].rearrange("p (j t) -> p j t", j=2), ex[:], ALU.mult), YO_free, 1)
                ch(v.tensor_tensor(yb[:, ds(2 * g, 2), P:T], yb[:, ds(2 * g, 2), P:T], yot, ALU.add))
                dve.wait_ge(proj_free.sem, proj_free.at(g, 7))
                ch.tell(v.tensor_tensor(yb[:, ds(2 * g, 2), :], yb[:, ds(2 * g, 2), :], zs[:], ALU.mult), y_done, 1)
                small(g, 11)
                new_states(1)
                new_states(2)
                new_states(3)
                ch(v.tensor_copy(hfin[:, 0:1, ds(g, 1)].rearrange("p b o -> p (b o)"), rr[:, NP - 1:NP]))
                ch(v.tensor_copy(hfin[:, 1:9, ds(g, 1)].rearrange("p b o -> p (b o)"), rr[:, NP + NT - 1:T:NT]))
                dve.wait_ge(CB_free.sem, CB_free.at(g, 1))
                ch(v.reciprocal(zs[:, 0, :], zs[:, 0, :]))
                for j in range(2):
                    t = yb[:, ds(2 * g + j, 1), :].rearrange("p o t -> p (o t)")
                    ch(v.scalar_tensor_tensor(out=t, in0=t, scalar=par[:, ds(2 * g + (C_NG + j), 1)], in1=zs[:, 0, :],
                                              op0=ALU.mult, op1=ALU.mult))
                dve.wait_ge(gelu_ready.sem, gelu_ready.at(g, 1))
                ch.tell(v.tensor_tensor(ya[:, ds(g, 1), :].rearrange("p o t -> p (o t)"), rr[:], gl[:], ALU.mult), lru_tail, 1)
            ch.leave(G)
            dve.sem_inc(b_small_dve.sem, 6 + 2)
            dve.sem_inc(br_done.sem, 2)
            for t in range(6):
                y = (ya[:, 4 * t:4 * t + 4, :] if t < 2 else yb[:, 4 * t - 8:4 * t - 4, :])
                dve.wait_ge(br_large.sem, br_large.at(0, t + 1))
                if t == 3:
                    dve.wait_ge(state_out, 16 * 3 * G + 1)
                v.tensor_tensor(br_lo[:, 4 * BR_LO[t]:4 * BR_LO[t] + 4, :], y, br_hi[:, 4 * t:4 * t + 4, :].bitcast(F32), ALU.subtract).then_inc(br_small.sem, 1)

            def branch_step(i, n):
                def branch_small(s):
                    dve.wait_ge(b_large.sem, b_large.at(i, s + 3))
                    slot = (s + 2) % 6
                    v.tensor_tensor(wlo[s % 2][:, 0:LOD], wflat(slot)[:, 0:LOD], whi[s % 2][:, 0:LOD].bitcast(F32),
                                    ALU.subtract).then_inc(b_small_dve.sem, 1)

                for s in range(3):
                    branch_small(s)
                if n == 6:
                    merge(i, 0)
                for s in range(3, n):
                    branch_small(s)
                if n < 6:
                    merge(i, 0)
                merge(i, 1)

            def merge(i, jj):
                dve.wait_ge(gates_ready, 2)
                dve.wait_ge(b_done.sem, b_done.at(i, 3 * jj + 3))
                ch(v.tensor_tensor(u[:], BR[jj][0][:, 0:T], ga[:, ds(2 * i + jj, 1), :].rearrange("p o t -> p (o t)"), ALU.mult))
                ch(v.tensor_tensor(ii[:], BR[jj][1][:, 0:T], gb[:, ds(2 * i + jj, 1), :].rearrange("p o t -> p (o t)"), ALU.mult))
                ch.tell(v.tensor_tensor(mg[:, ds(2 * i + jj, 1), :].rearrange("p o t -> p (o t)"), u[:], ii[:], ALU.add), br_done, jj + 1)

            with dve.Fori(0, 3) as i:
                ch.enter(i, 4)
                branch_step(i, 6)
            ch.peel(3)
            branch_step(3, 4)
            ch.leave(4)
            for j in range(8):
                dve.wait_ge(used[6 + j % 4], 1 + j // 4)
                ch.step(v.tensor_tensor(xT[:, j, :], xT[:, j, :], R4[j % 4][:, 0:T], ALU.add), dve_mid, f"x2_{j}")
            dve.wait_ge(act_mid.sem, act_mid.at("frs"))
            norm(hT, xT, C_GFFN, rs, dve_mid, "hf")
            def lo(i):
                c, hf = i // 2, i % 2
                n = TOK[c][1]
                dve.wait_ge(act_mid.sem, act_mid.at(f"hi{i}"))
                ch.step(v.tensor_tensor(htok_lo[0:n, c, 512 * hf:512 * hf + 512], R4[i % 4][0:n, :],
                                        htok_hi[0:n, c, 512 * hf:512 * hf + 512].bitcast(F32), ALU.subtract), dve_mid, f"lo{i}")

            ch(v.memset(r_lg, 0.0))
            dve.wait_ge(pe_mid.sem, pe_mid.at("route"))
            ch(v.tensor_copy(r_lg[:, 0:2, :].rearrange("p c n -> p (c n)"), bY[0][:, 0:40]))
            ch(v.tensor_copy(r_lg[0:NS, 2, :], bY[0][0:NS, 40:60]))
            bc = lambda t, n: t.unsqueeze(2).to_broadcast([P, 3, n])
            tie = cst[:, K_TIE:K_TIE + 4].unsqueeze(1).to_broadcast([P, 3, 4])

            def first_max(oh, x, m):
                ch(v.tensor_reduce(m, x, AX.X, ALU.max))
                ch(v.tensor_tensor(oh, x, bc(m, 4), ALU.is_equal))
                ch(v.tensor_tensor(oh, oh, tie, ALU.mult))
                ch(v.tensor_reduce(r_m2, oh, AX.X, ALU.max))
                ch(v.tensor_tensor(oh, oh, bc(r_m2, 4), ALU.is_equal))

            first_max(r_goh, r_lg[:, :, 0:4], r_m)
            ch.step(v.tensor_tensor(r_gs, r_lg[:, :, 0:4], bc(r_m, 4), ALU.subtract), dve_mid, "gsub")
            e4 = r_lg[:, :, 4:20].rearrange("p c (g j) -> p c g j", g=4)
            ch(v.tensor_tensor(r_pr, e4, r_goh.unsqueeze(3).to_broadcast([P, 3, 4, 4]), ALU.mult))
            ch(v.tensor_reduce(r_es, r_pr.rearrange("p c g j -> p c j g"), AX.X, ALU.add))
            ch(v.tensor_reduce(r_m, r_es, AX.X, ALU.max))
            ch.step(v.tensor_tensor(r_es, r_es, bc(r_m, 4), ALU.subtract), dve_mid, "esub")
            lo(0)
            lo(1)
            dve.wait_ge(act_mid.sem, act_mid.at("gexp"))
            ch(v.tensor_reduce(r_gw, r_gs, AX.X, ALU.add))
            dve.wait_ge(act_mid.sem, act_mid.at("eexp"))
            first_max(r_o1, r_es, r_m)
            ch(v.scalar_tensor_tensor(out=r_e2, in0=r_o1, scalar=-2.0, in1=r_es, op0=ALU.mult, op1=ALU.add))
            first_max(r_o2, r_e2, r_m)
            ch(v.tensor_tensor(r_e2, r_o1, r_es, ALU.mult))
            ch(v.tensor_reduce(r_v1, r_e2, AX.X, ALU.add))
            ch(v.tensor_tensor(r_e2, r_o2, r_es, ALU.mult))
            ch(v.tensor_reduce(r_v2, r_e2, AX.X, ALU.add))
            ch(v.tensor_tensor(r_m, r_v1, r_v2, ALU.add))
            ch(v.tensor_tensor(r_m, r_m, r_gw, ALU.mult))
            ch(v.reciprocal(r_m, r_m))
            ch(v.tensor_tensor(wAB[:, 0, :], r_v1, r_m, ALU.mult))
            ch(v.tensor_tensor(wAB[:, 1, :], r_v2, r_m, ALU.mult))
            oh = lambda i: rM[:, :, 16 * i:16 * i + 16]
            oh4 = lambda i: oh(i).rearrange("p c (g j) -> p c g j", g=4)
            for i, o in enumerate((r_o1, r_o2)):
                ch(v.tensor_tensor(oh4(i), r_goh.unsqueeze(3).to_broadcast([P, 3, 4, 4]), o.unsqueeze(2).to_broadcast([P, 3, 4, 4]), ALU.mult))
            ch.step(v.tensor_tensor(oh(2), oh(0), oh(1), ALU.add), dve_mid, "M")
            for i in range(2, 6):
                lo(i)
            dve.wait_ge(pe_mid.sem, pe_mid.at("MT"))
            ch(v.tensor_copy(rT, bY[1][0:NE, 0:T]))
            ch(v.tensor_tensor_scan(rC, rT, rT, 0.0, ALU.add, ALU.max))
            cnt, xs_, xe, xb = rC[:, T - 1:T], rX[:, 8:9], rX[:, 9:10], rX[:, 10:11]
            ch(v.tensor_scalar(rX[:, 0:CPE - 1], cst[0:NE, K_THR:K_II], cnt, None, ALU.is_lt))
            ch.step(v.tensor_reduce(xs_, rX[:, 0:CPE - 1], AX.X, ALU.add), dve_mid, "count")
            dve.wait_ge(pe_mid.sem, pe_mid.at("extra"))
            ch(v.tensor_copy(xe, bY[1][0:NE, T:T + 1]))
            ch(v.tensor_scalar(rX[:, 0:XSTEPS], cst[0:NE, K_IOTA:K_IOTA + XSTEPS], xe, None, ALU.is_ge))
            ch.step(v.tensor_tensor(xb, xe, xs_, ALU.subtract), dve_mid, "end")
            dve.wait_ge(pe_mid.sem, pe_mid.at("table"))
            ch(v.tensor_copy(steps[:, 0:NE], cst[0:1, K_IOTA:K_IOTA + NE]))
            ch(v.tensor_scalar(steps[:, NE:NE + XSTEPS], bY[1][0:1, 320:320 + XSTEPS], float(NE - 1), None, ALU.min))
            ch.step(v.tensor_scalar(steps[:, NE + XSTEPS:NE + XSTEPS + 1], bY[1][0:1, 330:331], float(NE), None, ALU.add), dve_mid, "steps")
            ch(v.tensor_scalar(xb, xb, float(S), cst[0:NE, K_D64:K_D64 + 1], ALU.mult, ALU.add))
            ch(v.tensor_scalar(rO, rC, float(S), xb, ALU.is_gt, ALU.mult))
            ch.step(v.scalar_tensor_tensor(out=rC, in0=rC, scalar=cst[0:NE, K_E64:K_E64 + 1], in1=rO, op0=ALU.add, op1=ALU.add),
                    dve_mid, "slots")
            ch(v.memset(rG[:], 0.0))
            dve.wait_ge(pe_mid.sem, pe_mid.at("slots"))
            ch(v.tensor_copy(rG[:, 0:2, :].rearrange("p c n -> p (c n)"), bY[0][:, 0:32]))
            ch(v.tensor_copy(rG[0:NS, 2, :], bY[0][0:NS, 32:48]))
            for i in range(2):
                ch(v.tensor_tensor(oh(i), oh(i), rG[:], ALU.mult))
                ins = v.tensor_reduce(AB[:, i, :], oh(i), AX.X, ALU.add)
                ch(ins) if i == 0 else ch.step(ins, dve_mid, "AB")
            dve.wait_ge(pe_mid.sem, pe_mid.at("rows"))
            ch(v.tensor_copy(ABrow[:, 0, :], bP[0][:, 0:T]))
            ch.step(v.tensor_copy(ABrow[:, 1, :], bP[1][:, 0:T]), dve_mid, "rows")
            def match_slots(last):
                ch(v.tensor_tensor(eA, iota, slot(AB, 0), ALU.is_equal))
                ch(v.tensor_tensor(eB, iota, slot(AB, 1), ALU.is_equal))
                last(v.tensor_scalar(AB[:], AB[:], -float(S), None, ALU.add))

            match_slots(ch)
            weigh_slots(v, ch)
            ch.step(v.tensor_tensor(eW, eA, eB, ALU.add), dve_mid, "pick0")
            ch(v.memset(ws[:], 0.0))
            ch.tell(v.memset(acc[:], 0.0), ws_done, 0)
            ch(v.tensor_copy(rowid[:], cst[:, K_ROW:K_ROW + 1]))
            ch(v.memset(xs[S:P, :], 0.0))
            ch.tell(v.memset(back[:].bitcast(F32), 0.0), back_ready, 0)
            n_steps = dve.value_load(steps[0:1, NE + XSTEPS:NE + XSTEPS + 1], min_val=NE, max_val=NE + XSTEPS)
            dve.sem_inc(cmb_done.sem, 2)
            dve.sem_inc(pick_ready.sem, 1)

            def slot_weights(q, k):
                dve.wait_ge(xb_gathered.sem, xb_gathered.at(q, k))
                v.tensor_copy(wsn[:], bank[2][:, 500:501]).then_inc(wsn_done.sem, 1)

            def tokens_lo(q, k):
                dve.wait_ge(xhi_ready.sem, xhi_ready.at(q, k))
                v.tensor_tensor(x_hl[:, :, 1, :], bX[:, :].rearrange("p (k s) -> p k s", k=KC),
                                x_hl[:, :, 0, :].bitcast(F32), ALU.subtract).then_inc(x_ready.sem, 1)

            def results_lo(q):
                for hf in range(2):
                    dve.wait_ge(yhi_ready.sem, yhi_ready.at(q, hf + 1))
                    v.scalar_tensor_tensor(out=y_lo[:, 512 * hf:512 * hf + 512], in0=bY[hf][:, :], scalar=ws[:, 0:1],
                                           in1=y_hi[:, 512 * hf:512 * hf + 512].bitcast(F32), op0=ALU.mult,
                                           op1=ALU.subtract).then_inc(ylo_ready.sem, 1)

            slot_weights(0, 0)
            match_slots(ch)
            weigh_slots(v, ch)
            ch.tell(v.tensor_tensor(eW, eA, eB, ALU.add), pick_ready, 1)
            tokens_lo(0, 0)
            dve.sem_inc(lo_dve.sem, NBLK)
            with dve.Fori(0, n_steps) as q:
                ch.enter(q, 6)

                def small(s):
                    dve.wait_ge(hi_ready.sem, hi_ready.at(q, s + 1))
                    v.tensor_tensor(wlo[s % R][:, 0:LOD], wflat(s)[:, 0:LOD], whi[s % R][:, 0:LOD].bitcast(F32),
                                    ALU.subtract).then_inc(lo_dve.sem, 1)

                def add_combined(j):
                    dve.wait_ge(cmb_ready.sem, cmb_ready.at(q, j + 1))
                    v.tensor_tensor(acc[:, j, :], acc[:, j, :], bank[2 + j % 2][:, 0:T], ALU.add).then_inc(cmb_done.sem, 1)

                small(0)
                small(1)
                results_lo(q)
                small(2)
                add_combined(0)
                small(3)
                dve.wait_ge(ylo_ready.sem, ylo_ready.at(q, 2))
                dve.wait_ge(wsn_done.sem, wsn_done.at(q, 0))
                v.tensor_copy(ws[:], wsn[:]).then_inc(ws_done.sem, 1)
                for j in range(1, 5):
                    add_combined(j)
                    small(j + 3)
                for j in range(5, 8):
                    add_combined(j)
                ch(v.tensor_scalar(backt, ABrow[:, 0, :], rowid[:, 0:1], None, ALU.is_equal))
                ch.tell(v.scalar_tensor_tensor(out=back[:], in0=ABrow[:, 1, :], scalar=rowid[:, 0:1], in1=backt,
                                               op0=ALU.is_equal, op1=ALU.add), back_ready, 1)
                ch(v.tensor_scalar(rowid[:], rowid[:], float(S), None, ALU.add))
                dve.wait_ge(pick_ready.sem, pick_ready.at(q, 1))
                match_slots(lambda ins: ch.tell(ins, eq_ready, 1))
                small(8)
                small(9)
                dve.wait_ge(silu_e.sem, silu_e.at(q, 1))
                ch(v.tensor_tensor(aq, sgq, bGT[:, 256:512], ALU.mult))
                a4 = aq.rearrange("p (f s) -> p f s", f=FC)
                ch(v.tensor_copy(a_hl[:, :, 0, :], a4))
                v.tensor_tensor(a_hl[:, :, 1, :], a4, a_hl[:, :, 0, :].bitcast(F32), ALU.subtract).then_inc(act_ready.sem, 1)
                slot_weights(q, 1)
                small(10)
                tokens_lo(q, 1)
                small(11)
            ch.leave(0)
            results_lo(n_steps)
            ch = Chain(dve, dve_ch2)
            for j in range(8):
                dve.wait_ge(cmb_ready.sem, cmb_ready.at(n_steps, j + 1))
                ch(v.tensor_tensor(acc[:, j, :], acc[:, j, :], bank[[2, 3, 4, 7, 0, 1, 5, 6][j]][:, 0:T], ALU.add))
            for j in range(8):
                ch.step(v.tensor_tensor(xT[:, j, :], xT[:, j, :], acc[:, j, :], ALU.add), dve_end, f"x3_{j}")

            def gate_small(s):
                dve.wait_ge(hi_ready.sem, hi_ready.at(n_steps, s + 1))
                v.tensor_tensor(wlo[s % R][:, 0:LOD], wflat(s)[:, 0:LOD], whi[s % R][:, 0:LOD].bitcast(F32),
                                ALU.subtract).then_inc(lo_dve.sem, 1)

            for s in range(R):
                gate_small(s)
            dve.wait_ge(act_end.sem, act_end.at("grs"))
            norm(hT, xT, C_GPG, rs, dve_end, "hg")
            for k in range(KC):
                dve.wait_ge(act_end.sem, act_end.at(f"hh{k}"))
                v.tensor_tensor(hg_lo[:, k, :], hT[:, k, :], hg_hi[:, k, :].bitcast(F32), ALU.subtract).then_inc(dve_end.sem, 1)
            norm(eT, eT, C_GPLE, rs2, dve_end, "eN")
            dve.wait_ge(dve_end.sem, dve_end.at("eN7"))
            for j in range(8):
                dve.wait_ge(act_end.sem, act_end.at(f"sig{j}"))
                ch(v.tensor_tensor(sgu, sg[j % 2], eT[:, j, :], ALU.mult))
                ch.step(v.tensor_tensor(xT[:, j, :], xT[:, j, :], sgu, ALU.add), dve_end, f"x4_{j}")
                if j + R < 8:
                    gate_small(j + R)
            dve.wait_ge(act_end.sem, act_end.at("yrs"))
            norm(hT, xT, C_GFIN, rs, dve_end, "hy")
            for i in range(6):
                c, hf = i // 2, i % 2
                n = TOK[c][1]
                dve.wait_ge(pe_end.sem, pe_end.at(f"out{i}"))
                ch.step(v.tensor_copy(yrow[0:n, c, 512 * hf:512 * hf + 512], bank[EB[i]][0:n, :]), dve_end, f"out{i}")

        @block.tensor
        def _(pe):
            mm, tr = nc.tensor.matmul, nc.tensor.transpose
            pe.wait_ge(d_cst, 16)
            pe.wait_ge(d_x, 32)
            for k in range(KC):
                if k == 7:
                    pe.wait_ge(dve_pro.sem, dve_pro.at("x0"))
                for c, (t0, n) in enumerate(TOK):
                    ins = tr(bank[XB[k]][:, t0:t0 + n], xrow[0:n, c, k * P:(k + 1) * P], ident[0:n, 0:n])
                ins.then_inc(pe_pro.sem, 1)
            pe.wait_ge(d_par, 16 * 13)
            pe.wait_ge(dve_pro.sem, dve_pro.at("x3"))
            for t, n in enumerate((P, P, 24)):
                ins = tr(bank[4][:, t * P:t * P + n], prow[0:n, t, :], ident[0:n, 0:n])
            ins.then_inc(pe_pro.sem, 1)
            pe.wait_ge(d_row, 48)
            for t in range(4):
                tr(bank[1][:, t * P:(t + 1) * P], srow[:, t, :], ident)
            for t in range(2):
                tr(bank[2][:, t * P:(t + 1) * P], srow[:, 4 + t, :], ident)
            for t in range(2):
                tr(bank[2][:, 256 + 96 * t:352 + 96 * t], lrow[0:96, t, :], ident[0:96, 0:96])
            tr(bank[2][:, 448:512], hrow[0:64], ident[0:64, 0:64]).then_inc(pe_pro.sem, 1)

            def rms(b, src, steps, names):
                for k in range(KC):
                    if names:
                        pe.wait_ge(names[0].sem, names[0].at(f"{names[1]}{k}"))
                    ins = mm(b[:, 0:T], ones, src[:, k, :], start=(k == 0), stop=(k == KC - 1))
                ins.then_inc(steps.sem, 1)

            rms(bCB, sq, pe_pro, (act_pro, "sq"))
            pe.wait_ge(d_wdt, 16)
            for k in range(KC):
                pe.wait_ge(dve_pro.sem, dve_pro.at(f"hT{k}"))
                ins = mm(bank[4][0:H, 0:T], wdt[:, k, :], ya[:, k, :], start=(k == 0), stop=(k == KC - 1))
            ins.then_inc(pe_pro.sem, 1)
            pe.wait_ge(dve_pro.sem, dve_pro.at("aT"))
            for c, (t0, n) in enumerate(TOK):
                tr(bank[5][0:n, c * H:(c + 1) * H], aT[:, t0:t0 + n], ident[0:H, 0:H])
            for h in range(2):
                ins = mm(bank[5][64 * h:64 * h + 64, P:P + 16], hc[:, 2:3].to_broadcast([H, 64]), ident[0:H, h:H:2], start=True, stop=True)
            ins.then_inc(pe_pro.sem, 1)
            pe.wait_ge(dve_pro.sem, dve_pro.at("atok"))
            for c, (t0, n) in enumerate(TOK):
                m = tri if c < 2 else cst[0:NS, K_TRIS:K_TRIS + NS]
                ins = mm(bank[6][0:H, t0:t0 + n], atok[0:n, c, :], m, start=True, stop=True)
            ins.then_inc(pe_pro.sem, 1)
            pe.wait_ge(act_pro.sem, act_pro.at("dte"))
            for i, src in enumerate((sp[0][0:H, 0:T], cumT[:], dteT)):
                for c, (t0, n) in enumerate(TOK):
                    ins = tr(bank[7][0:n, (3 * i + c) * H:(3 * i + c + 1) * H], src[:, t0:t0 + n], ident[0:H, 0:H])
            ins.then_inc(pe_pro.sem, 1)
            pe.wait_ge(dve_pro.sem, dve_pro.at("tm"))
            pe.sem_inc(YO_ready.sem, 1)

            pe.wait_ge(dve_pro.sem, dve_pro.at("hl"))
            pe.sem_inc(projected.sem, 2)
            with pe.Fori(0, G) as g:
                def proj(i):
                    pe.wait_ge(w_small_dve.sem, w_small_dve.at(g, i + 1))
                    pe.wait_ge(w_small_pool.sem, w_small_pool.at(g, i + 1))
                    pe.wait_ge(proj_free.sem, proj_free.at(g, i - 1))
                    for k in range(KC):
                        hi, lo = (t[i % 2][:, k * P:(k + 1) * P] for t in (whi, wlo))
                        mm(bP[i % 2][:, 0:T], hi, h_hi[:, k, :], start=(k == 0), stop=False)
                        mm(bP[i % 2][:, 0:T], hi, h_lo[:, k, :], start=False, stop=False)
                        ins = mm(bP[i % 2][:, 0:T], lo, h_hi[:, k, :], start=False, stop=(k == KC - 1))
                    ins.then_inc(projected.sem, 1)

                def token_major(c):
                    t0, n = TOK[c]
                    pe.wait_ge(T_free.sem, T_free.at(g, c))
                    for i in range(3):
                        ins = tr(bT[0:n, i * P:(i + 1) * P], xbc[i][:, t0:t0 + n], ident)
                    ins.then_inc(T_ready.sem, 1)

                def cum_rows(c):
                    t0, n = TOK[c]
                    pe.wait_ge(CU_free.sem, CU_free.at(g, c))
                    mm(bCU[:, 0:4 * n].rearrange("p (h q) -> p h q", h=4), cst[0:H, K_ONE:K_ONE + P], Dg[:, :, t0:t0 + n],
                       start=True, stop=True).then_inc(CU_ready.sem, 1)

                def y_diag(c):
                    t0, n = TOK[c]
                    pe.wait_ge(W_ready.sem, W_ready.at(g, c + 1))
                    w = (tw[:, c, :] if c < 2 else tws[:]).rearrange("p (h q) -> p h q", h=4)
                    for j in range(2):
                        for h in range(2):
                            ins = mm(bY[j][64 * h:64 * h + 64, t0:t0 + n], xdt[0:n, c, (2 * j + h) * 64:(2 * j + h + 1) * 64],
                                     w[:, 2 * j + h, :], start=True, stop=True)
                    return ins

                def state_T(j, hf):
                    k = 5 + 2 * j + hf
                    if j == 0 and hf == 0:
                        pe.wait_ge(sin_landed, g * 32 + 32)
                    pe.wait_ge(T_free.sem, T_free.at(g, k - 1))
                    for b in range(4):
                        ins = tr(bT[:, b * P:(b + 1) * P], Sin[:, j, 4 * hf + b, :], ident)
                    ins.then_inc(T_ready.sem, 1)

                def y_state(j):
                    pe.wait_ge(T_free.sem, T_free.at(g, 6 + 2 * j))
                    for b in range(NB):
                        ins = mm(bYO[:, j * 160 + P + NT * b:j * 160 + P + NT * b + NT], sT[:, b, :],
                                 xbc[3][:, NP + NT * b:NP + NT * b + NT], start=True, stop=True)
                    return ins

                def new_states(k):
                    j, hf = k // 2, k % 2
                    b, ready, free, n = SN[k]
                    pe.wait_ge(free.sem, free.at(g, n - 1))
                    mm(b[:, :], xdte[0:NS, 2, j * P:(j + 1) * P], Bm[:, 4 * hf:4 * hf + 4, :].rearrange("p b n -> p (b n)"),
                       start=True, stop=True).then_inc(ready.sem, 1)

                for i in range(6):
                    proj(i)
                pe.wait_ge(silu_done.sem, silu_done.at(g, 4))
                pe.wait_ge(CB_free.sem, CB_free.at(g, 0))
                for c, (t0, n) in enumerate(TOK):
                    ins = mm(bCB[0:n, t0:t0 + n], xbc[2][:, t0:t0 + n], xbc[3][:, t0:t0 + n], start=True, stop=True)
                ins.then_inc(CB_ready.sem, 1)
                token_major(0)
                pe.wait_ge(dg_ready.sem, dg_ready.at(g, 1))
                cum_rows(0)
                proj(6)
                pe.wait_ge(gate_landed, g * 32 + 32)
                pe.wait_ge(conv_done.sem, conv_done.at(g, 5))
                pe.wait_ge(Y_free.sem, Y_free.at(g, 0))
                mm(bY[0][:, 0:T], wg[:, 0, :], u[:], start=True, stop=True)
                mm(bY[1][:, 0:T], wg[:, 1, :], u[:], start=True, stop=True).then_inc(Y_ready.sem, 1)
                token_major(1)
                cum_rows(1)
                proj(7)
                token_major(2)
                cum_rows(2)
                proj(8)
                pe.wait_ge(xdte_ready.sem, xdte_ready.at(g, 1))
                pe.wait_ge(T_free.sem, T_free.at(g, 3))
                mm(bT[:, 0:256], btok[:, 0, :], xdte[:, 0, :], start=True, stop=True).then_inc(T_ready.sem, 1)
                pe.wait_ge(Y_free.sem, Y_free.at(g, 1))
                y_diag(0)
                state_T(0, 0)
                y_diag(1)
                pe.wait_ge(YO_free.sem, YO_free.at(g, 0))
                for j in range(2):
                    mm(bYO[:, 160 * j:160 * j + P], sprev[:, j * P:(j + 1) * P], xbc[3][:, P:2 * P], start=True, stop=True)
                state_T(0, 1)
                y_diag(2).then_inc(Y_ready.sem, 1)
                pe.wait_ge(xdte_ready.sem, xdte_ready.at(g, 3))
                pe.wait_ge(CU_free.sem, CU_free.at(g, 3))
                for j in range(2):
                    for c in range(QC):
                        ins = mm(bCU[:, 256 * j + P * c:256 * j + P * (c + 1)], xdte[:, c, j * P:(j + 1) * P], btok[:, c, :],
                                 start=True, stop=True)
                ins.then_inc(CU_ready.sem, 1)
                y_state(0)
                state_T(1, 0)
                pe.wait_ge(bm_ready.sem, bm_ready.at(g, 1))
                new_states(0)
                state_T(1, 1)
                proj(9)
                y_state(1).then_inc(YO_ready.sem, 1)
                for k in range(1, 4):
                    new_states(k)
                pe.wait_ge(sq_ready.sem, sq_ready.at(g, 1))
                for j in range(2):
                    ins = mm(bCB[:, 0:T], ones, tw[:, j, 0:T], start=(j == 0), stop=(j == 1))
                ins.then_inc(CB_ready.sem, 1)

            pe.wait_ge(lru_tail.sem, lru_tail.at(G - 1, 1))

            def branch_matmuls(i, first):
                for s in range(6):
                    jj, t = s // 3, s % 3
                    if t == 0:
                        pe.wait_ge(br_done.sem, br_done.at(i, jj - 1))
                    pe.wait_ge(b_small_dve.sem, b_small_dve.at(i, s + 1))
                    pe.wait_ge(b_small_pool.sem, b_small_pool.at(i, s + 1))
                    out = BR[jj][t > 0][:, 0:T]
                    for k in range(KC):
                        if first and s < 3 and k % 4 == 0:
                            pe.wait_ge(br_large.sem, br_large.at(0, 2 * t + k // 4 + 1))
                        for w in (whi, wlo):
                            mm(out, w[s % 2][:, k * P:(k + 1) * P], br_hi[:, 8 * t + k, :], start=(k == 0 and w is whi and t < 2), stop=False)
                    for k in range(KC):
                        if first and s < 3 and k % 4 == 0:
                            pe.wait_ge(br_small.sem, br_small.at(0, 2 * t + k // 4 + 1))
                        ins = mm(out, whi[s % 2][:, k * P:(k + 1) * P], br_lo[:, 4 * BR_LO[2 * t + k // 4] + k % 4, :], start=False,
                                 stop=(k == KC - 1 and t != 1))
                    ins.then_inc(b_done.sem, 1)

            pe.wait_ge(w_small_dve.sem, w_small_dve.at(G, 2))
            pe.wait_ge(w_small_pool.sem, w_small_pool.at(G, 2))
            branch_matmuls(0, True)
            with pe.Fori(1, 4) as i:
                branch_matmuls(i, False)
            pe.wait_ge(br_done.sem, br_done.at(3, 2))
            for j in range(8):
                s = 6 + j % 4
                pe.wait_ge(landed[s], 16 * (1 + j // 4))
                if j >= 4:
                    pe.wait_ge(dve_mid.sem, dve_mid.at(f"x2_{j - 4}"))
                for k in range(KC):
                    ins = mm(R4[j % 4][:, 0:T], wblk(s)[:, k, :], mg[:, k, :], start=(k == 0), stop=(k == KC - 1))
                ins.then_inc(used[s], 1)
            pe.wait_ge(stashed.sem, stashed.at(G - 1, 5))
            pe.wait_ge(dve_mid.sem, dve_mid.at("x2_6"))
            fS = stS[:].rearrange("p r c -> p (r c)")
            fL = stL[:].rearrange("p r c -> p (r c)")
            fH = hfin[:].rearrange("p r c -> p (r c)")
            tr(bT[0:96, 0:P], fS[:, 0:96], ident)
            for t in range(6):
                b, o = (bT, P * (1 + t)) if t < 3 else (bCB, P * (t - 3))
                tr(b[:, o:o + P], fS[:, 96 + P * t:96 + P * (t + 1)], ident)
            tr(bCB[0:24, 384:512], fL[:, 0:24], ident)
            tr(bCU[0:96, 0:P], fL[:, 24:120], ident)
            tr(bCU[0:96, P:2 * P], fL[:, 120:216], ident)
            tr(bCU[0:72, 256:384], fH, ident).then_inc(pe_mid.sem, 1)
            pe.wait_ge(d_plr, 48)
            for k in range(2):
                for c, (t0, n) in enumerate(TOK):
                    ins = tr(bY[k][:, t0:t0 + n], plr[0:n, c, k * P:(k + 1) * P], ident[0:n, 0:n])
            ins.then_inc(pe_mid.sem, 1)
            rms(bP[0], sq, pe_mid, (act_mid, "sqf"))
            pe.wait_ge(act_mid.sem, act_mid.at("pT"))
            pe.wait_ge(act_mid.sem, act_mid.at("st"))
            pe.wait_ge(dve_mid.sem, dve_mid.at("x2_7"))
            for j in range(8):
                s = 10 + j // 4
                if j % 4 == 0:
                    pe.wait_ge(landed[s], 16)
                if j >= 4:
                    pe.wait_ge(act_mid.sem, act_mid.at(f"e{j - 4}"))
                w = wblk(s).rearrange("p a b -> p (a b)").rearrange("p (k c) -> p k c", k=2)
                for k in range(2):
                    ins = mm(R4[j % 4][:, 0:T], w[:, k, (j % 4) * P:(j % 4 + 1) * P], pT[:, k, :], start=(k == 0), stop=(k == 1))
                ins.then_inc(pe_mid.sem, 1)
            rms(bP[1], sq, pe_mid, (act_mid, "e"))
            pe.wait_ge(d_wr, 64)
            pe.wait_ge(dve_mid.sem, dve_mid.at("hf7"))
            for c, (t0, n) in enumerate(TOK):
                for k in range(KC):
                    mm(bY[0][0:n, 20 * c:20 * c + 20], hT[:, k, t0:t0 + n], wr[:, k, :], start=(k == 0), stop=False)
                ins = mm(bY[0][0:n, 20 * c:20 * c + 20], cst[0:1, K_ONE:K_ONE + n], rb[:], start=False, stop=True)
            ins.then_inc(pe_mid.sem, 1)
            def tokens_T(i):
                c, hf = i // 2, i % 2
                t0, n = TOK[c]
                for k in range(4):
                    ins = tr(R4[i % 4][0:n, k * P:(k + 1) * P], hT[:, 4 * hf + k, t0:t0 + n], ident)
                ins.then_inc(pe_mid.sem, 1)

            pe.wait_ge(act_mid.sem, act_mid.at("ers"))
            for i in range(4):
                tokens_T(i)
            pe.wait_ge(dve_mid.sem, dve_mid.at("M"))
            for c, (t0, n) in enumerate(TOK):
                ins = tr(bY[1][0:NE, t0:t0 + n], rM[0:n, c, 32:48], ident[0:n, 0:n])
            ins.then_inc(pe_mid.sem, 1)
            for i in range(4, 6):
                pe.wait_ge(dve_mid.sem, dve_mid.at(f"lo{i - 4}"))
                tokens_T(i)
            pe.wait_ge(dve_mid.sem, dve_mid.at("count"))
            mm(bY[1][0:NE, T:T + 1], tri[0:NE, 0:NE], rX[:, 8:9], start=True, stop=True).then_inc(pe_mid.sem, 1)
            pe.wait_ge(dve_mid.sem, dve_mid.at("end"))
            mm(bY[1][0:1, 320:320 + XSTEPS], ones[0:NE, 0:1], rX[:, 0:XSTEPS], start=True, stop=True)
            mm(bY[1][0:1, 330:331], ones[0:NE, 0:1], rX[:, 8:9], start=True, stop=True).then_inc(pe_mid.sem, 1)
            pe.wait_ge(dve_mid.sem, dve_mid.at("slots"))
            for c, (t0, n) in enumerate(TOK):
                ins = tr(bY[0][0:n, NE * c:NE * c + NE], rC[:, t0:t0 + n], ident[0:NE, 0:NE])
            ins.then_inc(pe_mid.sem, 1)
            pe.wait_ge(dve_mid.sem, dve_mid.at("AB"))
            for i in range(2):
                for c, (t0, n) in enumerate(TOK):
                    ins = mm(bP[i][:, t0:t0 + n], AB[0:n, i, c:c + 1].to_broadcast([n, P]), ident[0:n, 0:n], start=True, stop=True)
            ins.then_inc(pe_mid.sem, 1)

            II = cst[:, K_II:K_II + S]

            def gather(hf):
                for i, h in enumerate((htok_hi, htok_lo)):
                    for c, (t0, n) in enumerate(TOK):
                        ins = mm(bY[hf][0:S, :], pick[0:n, c, :], h[0:n, c, 512 * hf:512 * hf + 512],
                                 start=(i == 0 and c == 0), stop=(i == 1 and c == 2))
                return ins

            def gather_weights():
                for i in range(2):
                    for c, (t0, n) in enumerate(TOK):
                        ins = mm(bank[2][S * i:S * i + S, 500:501], eW[0:n, c, :], ones[0:n, 0:1], start=(c == 0), stop=(c == 2))
                return ins

            def tokens_by_feature(q, kk):
                for k in range(KC):
                    if k % 4 == 0:
                        out = (xs0_out, xs1_out)[k // 4]
                        pe.wait_ge(out.sem, out.at(q, kk))
                    ins = mm(bX[:, k * S:(k + 1) * S], xs[:, k * P:(k + 1) * P], ident[:, 0:S], start=True, stop=True)
                ins.then_inc(xt_ready.sem, 1)

            pe.wait_ge(dve_mid.sem, dve_mid.at("pick0"))
            pe.wait_ge(dve_mid.sem, dve_mid.at("rows"))
            for hf in range(2):
                mm(bY[hf][:, :], ones, xT[:].rearrange("p a b -> p (a b)")[:, 0:512], start=True, stop=True)
            gather(0).then_inc(xa_gathered.sem, 1)
            gather(1)
            gather_weights().then_inc(xb_gathered.sem, 1)
            pe.wait_ge(back_ready.sem, back_ready.at(0, 0))
            tokens_by_feature(0, 0)
            pe.sem_inc(hl_free.sem, R)
            pe.sem_inc(cmb_ready.sem, 1)
            n_steps = pe.value_load(steps[0:1, NE + XSTEPS:NE + XSTEPS + 1], min_val=NE, max_val=NE + XSTEPS)

            def combine(j, b):
                mm(b[:, 0:T], y_hi[:, j * P:(j + 1) * P], back[:], start=True, stop=False)
                mm(b[:, 0:T], y_lo[:, j * P:(j + 1) * P], back[:], start=False, stop=True).then_inc(cmb_ready.sem, 1)

            with pe.Fori(0, n_steps) as q:
                def split(s):
                    pe.wait_ge(lo_dve.sem, lo_dve.at(q, s + 1))
                    pe.wait_ge(lo_pool.sem, lo_pool.at(q, s + 1))

                def up(s):
                    split(s)
                    for k in range(2):
                        for i, w in enumerate((whi, wlo)):
                            kk = 2 * (s // 2) + k
                            ins = mm((bG1, bG3)[s % 2][:, :], x_hl[:, kk, :, :], w[s % R][:, 512 * k:512 * k + 512],
                                     start=(kk == 0 and i == 0), stop=(kk == KC - 1 and i == 1))
                    ins.then_inc(hl_free.sem, 1)

                def put_back(j):
                    if j % 4 == 0:
                        pe.wait_ge(ylo_ready.sem, ylo_ready.at(q, 1 + j // 4))
                    pe.wait_ge(cmb_done.sem, cmb_done.at(q, j - 1))
                    combine(j, bank[2 + j % 2])

                pe.wait_ge(x_ready.sem, x_ready.at(q, 0))
                up(0)
                up(1)
                pe.wait_ge(wsn_done.sem, wsn_done.at(q, 0))
                pe.wait_ge(back_ready.sem, back_ready.at(q, 0))
                for j in range(6):
                    put_back(j)
                    up(2 + j)
                put_back(6)
                put_back(7)
                pe.wait_ge(pick_ready.sem, pick_ready.at(q, 1))
                gather(0).then_inc(xa_gathered.sem, 1)
                for i, (out, o) in enumerate(((g1_out, 0), (g3_out, 512))):
                    pe.wait_ge(out.sem, out.at(q, 1))
                    for f in range(FC):
                        ins = mm(bGT[:, 256 * i + f * S:256 * i + (f + 1) * S], Gs[:, o + f * P:o + (f + 1) * P], II,
                                 start=True, stop=True)
                ins.then_inc(gt_ready.sem, 1)
                gather(1)
                pe.wait_ge(cmb_done.sem, cmb_done.at(q, 7))
                gather_weights().then_inc(xb_gathered.sem, 1)
                tokens_by_feature(q, 1)
                pe.wait_ge(act_ready.sem, act_ready.at(q, 1))
                for f in range(FC):
                    split(8 + f)
                    for i, w in enumerate((whi, wlo)):
                        for hf in range(2):
                            ins = mm(bY[hf][:, :], a_hl[:, f, :, :], w[(8 + f) % R][:, 512 * hf:512 * hf + 512],
                                     start=(f == 0 and i == 0), stop=(f == FC - 1 and i == 1))
                    ins.then_inc(hl_free.sem, 1)
            pe.wait_ge(ylo_ready.sem, ylo_ready.at(n_steps, 2))
            pe.wait_ge(back_ready.sem, back_ready.at(n_steps, 0))
            pe.wait_ge(cmb_done.sem, cmb_done.at(n_steps, 0))
            pe.wait_ge(wsn_done.sem, wsn_done.at(n_steps, 0))
            for j in range(8):
                combine(j, bank[[2, 3, 4, 7, 0, 1, 5, 6][j]])
            pe.wait_ge(dve_end.sem, dve_end.at("x3_0"))
            rms(bP[0], sq, pe_end, (act_end, "sg"))
            for j in range(8):
                pe.wait_ge(lo_dve.sem, lo_dve.at(n_steps, j + 1))
                pe.wait_ge(lo_pool.sem, lo_pool.at(n_steps, j + 1))
                if j >= 4:
                    pe.wait_ge(act_end.sem, act_end.at(f"sig{j - 4}"))
                for k in range(KC):
                    if j == 0:
                        pe.wait_ge(act_end.sem, act_end.at(f"hh{k}"))
                    for i, w in enumerate((whi, wlo)):
                        mm(R4[j % 4][:, 0:T], w[j % R][:, k * P:(k + 1) * P], hg_hi[:, k, :], start=(k == 0 and i == 0), stop=False)
                for k in range(KC):
                    if j == 0:
                        pe.wait_ge(dve_end.sem, dve_end.at(f"hl{k}"))
                    ins = mm(R4[j % 4][:, 0:T], whi[j % R][:, k * P:(k + 1) * P], hg_lo[:, k, :], start=False, stop=(k == KC - 1))
                ins.then_inc(hl_free.sem, 1)
            rms(bP[1], sq, pe_end, (act_end, "sy"))
            for i in range(6):
                c, hf = i // 2, i % 2
                pe.wait_ge(dve_end.sem, dve_end.at(f"hy{4 * hf + 3}"))
                t0, n = TOK[c]
                for k in range(4):
                    ins = tr(bank[EB[i]][0:n, k * P:(k + 1) * P], hT[:, 4 * hf + k, t0:t0 + n], ident)
                ins.then_inc(pe_end.sem, 1)


_INS = ["x_prompt", "x_sample", "state_lru_h", "state_lru_conv", "state_ssd", "state_ssd_conv", "p_prompt", "p_sample",
        "g_mix", "w_in", "lru_conv_w", "lru_conv_b", "lru_wa", "lru_ba", "lru_wx", "lru_bx", "lru_lambda",
        "ssd_conv_w", "ssd_conv_b", "ssd_dt_bias", "ssd_A_log", "ssd_D", "ssd_norm_g",
        "w_br_lru", "w_br_ssd", "w_out", "g_ffn", "w_router_g", "b_router_g", "w_router_e", "b_router_e",
        "w1", "w3", "w2", "w_ple_proj", "g_ple", "g_ple_gate", "w_ple_gate", "g_final"]
_OUTS = [("y_prompt", (1, NP, D)), ("y_sample", (NB, NT, D)), ("new_lru_h_p", (1, 1, D)), ("new_lru_conv_p", (1, 1, 3, D)),
         ("new_ssd_p", (1, 1, H, 64, P)), ("new_ssd_conv_p", (1, 1, 3, 4096)), ("new_lru_h_s", (1, NB, D)),
         ("new_lru_conv_s", (1, NB, 3, D)), ("new_ssd_s", (1, NB, H, 64, P)), ("new_ssd_conv_s", (1, NB, 3, 4096))]


def kernel(**inputs):
    import numpy as _np
    import concourse.bacc as _bacc
    from concourse import mybir as _mybir
    from concourse.bass_utils import run_bass_kernel_spmd as _run

    nc = _bacc.Bacc("TRN2", target_bir_lowering=False, num_devices=1)
    arrays, aps = {}, {}
    for name in _INS + ["constants"]:
        x = constants() if name == "constants" else _np.ascontiguousarray(inputs[name])
        arrays[f"in_{name}"] = x
        aps[name] = nc.dram_tensor(f"in_{name}", x.shape, _mybir.dt.from_np(x.dtype), kind="ExternalInput").ap()
    for name, shape in _OUTS:
        aps[name] = nc.dram_tensor(f"out_{name}", shape, _mybir.dt.float32, kind="ExternalOutput").ap()
    build(nc, aps)
    r = _run(nc, [arrays], core_ids=[0])
    return tuple(r.results[0][f"out_{name}"] for name, _ in _OUTS)
```
